# Optimizing a Trainium2 kernel written in Bass

```python
import jax, jax.numpy as jnp
from jax import lax
import numpy as np

D_MODEL = 1024
BATCH = 1
SEQ = 2048
DEPTH = 1

CHUNK = 64
Q_BLOCK = 128
ROPE_THETA = 10000.0
EPS = 1e-6

A_HEADS = 8
A_KV_HEADS = 2
A_HEAD_DIM = 64
IDX_HEADS = 8
IDX_DIM = 64
TOPK_MAX = 256

B_HEADS = 4
B_HEAD_DIM = 128
CONV_WIDTH = 4

D_FF = 4 * D_MODEL
MIX_WIDTH = A_HEADS * A_HEAD_DIM + B_HEADS * B_HEAD_DIM
B_CONV_CH = 3 * B_HEADS * B_HEAD_DIM

SPLIT_SIZES = (A_HEADS * A_HEAD_DIM, A_KV_HEADS * A_HEAD_DIM, A_KV_HEADS * A_HEAD_DIM,
               IDX_HEADS * IDX_DIM, IDX_DIM, IDX_HEADS,
               B_HEADS * B_HEAD_DIM, B_HEADS * B_HEAD_DIM, B_HEADS * B_HEAD_DIM,
               B_HEADS * B_HEAD_DIM, B_HEADS, B_HEADS)
IN_DIM = sum(SPLIT_SIZES)
SPLIT_POINTS = tuple(int(v) for v in np.cumsum(SPLIT_SIZES)[:-1])

kernel_name = 'hybrid_dsa_gdn_block'

def rms_norm(x, g):
    xf = x.astype(jnp.float32)
    y = xf * lax.rsqrt(jnp.mean(jnp.square(xf), axis=-1, keepdims=True) + EPS)
    return (y * g.astype(jnp.float32)).astype(x.dtype)

def l2_norm(x):
    return x * lax.rsqrt(jnp.sum(jnp.square(x), axis=-1, keepdims=True) + EPS)

def rope(x, pos):
    d = x.shape[-1]
    half = d // 2
    inv_freq = 1.0 / (ROPE_THETA ** (jnp.arange(half, dtype=jnp.float32) / half))
    ang = pos.astype(jnp.float32)[:, None] * inv_freq[None, :]
    cos = jnp.cos(ang)[:, None, :]
    sin = jnp.sin(ang)[:, None, :]
    xf = x.astype(jnp.float32)
    x1, x2 = xf[..., :half], xf[..., half:]
    return jnp.concatenate([x1 * cos - x2 * sin, x2 * cos + x1 * sin], axis=-1).astype(x.dtype)

def causal_depthwise_conv(x, w):
    ch = x.shape[-1]
    return lax.conv_general_dilated(
        x, w[:, None, :].astype(x.dtype), window_strides=(1,),
        padding=[(CONV_WIDTH - 1, 0)], dimension_numbers=('NWC', 'WIO', 'NWC'),
        feature_group_count=ch)

def sparse_indexer_attention(q, k, v, q_idx, k_idx, w_idx):
    bsz, seq = q.shape[0], q.shape[1]
    n_keys = seq
    topk = min(TOPK_MAX, n_keys // 4)
    n_blocks = seq // Q_BLOCK
    group = A_HEADS // A_KV_HEADS
    key_pos = jnp.arange(n_keys)
    gather = jax.vmap(lambda table, idx: table[idx])

    def blocks(a):
        return jnp.moveaxis(a.reshape((bsz, n_blocks, Q_BLOCK) + a.shape[2:]), 1, 0)

    def one_block(args):
        qb, qib, wb, blk = args
        q_pos = blk * Q_BLOCK + jnp.arange(Q_BLOCK)
        limit = (q_pos // CHUNK + 1) * CHUNK
        rel = jax.nn.relu(jnp.einsum('bqhd,bsd->bqhs', qib, k_idx).astype(jnp.float32))
        iscore = jnp.einsum('bqhs,bqh->bqs', rel, wb.astype(jnp.float32))
        iscore = jnp.where(key_pos[None, None, :] < limit[None, :, None], iscore, -jnp.inf)
        _, sel = lax.top_k(iscore, topk)
        valid = sel < limit[None, :, None]
        k_sel = gather(k, sel)
        v_sel = gather(v, sel)
        qg = qb.reshape(bsz, Q_BLOCK, A_KV_HEADS, group, A_HEAD_DIM)
        s = jnp.einsum('bqngd,bqknd->bqngk', qg, k_sel).astype(jnp.float32) * (A_HEAD_DIM ** -0.5)
        s = jnp.where(valid[:, :, None, None, :], s, -jnp.inf)
        p = jax.nn.softmax(s, axis=-1).astype(v.dtype)
        o = jnp.einsum('bqngk,bqknd->bqngd', p, v_sel)
        return o.reshape(bsz, Q_BLOCK, A_HEADS * A_HEAD_DIM)

    out = lax.map(one_block, (blocks(q), blocks(q_idx), blocks(w_idx), jnp.arange(n_blocks)))
    return jnp.moveaxis(out, 0, 1).reshape(bsz, seq, A_HEADS * A_HEAD_DIM)

def gated_delta_rule_chunked(q, k, v, g, beta):
    bsz, seq, nh, dk = q.shape
    dv = v.shape[-1]
    n = seq // CHUNK

    def to_chunks(a):
        return a.reshape(bsz, n, CHUNK, nh, -1).transpose(0, 3, 1, 2, 4)

    q = to_chunks(q) * (dk ** -0.5)
    k = to_chunks(k)
    v = to_chunks(v)
    g = g.reshape(bsz, n, CHUNK, nh).transpose(0, 3, 1, 2)
    beta = beta.reshape(bsz, n, CHUNK, nh).transpose(0, 3, 1, 2)
    gc = jnp.cumsum(g, axis=-1)
    incl = jnp.tril(jnp.ones((CHUNK, CHUNK), dtype=bool))
    strict = jnp.tril(jnp.ones((CHUNK, CHUNK), dtype=bool), k=-1)
    decay = jnp.exp(jnp.where(incl, gc[..., :, None] - gc[..., None, :], -jnp.inf))
    kb = k * beta[..., None]
    m = jnp.where(strict, jnp.einsum('bhncd,bhnsd->bhncs', kb, k) * decay, 0.0)
    a = m + jnp.eye(CHUNK, dtype=m.dtype)
    rhs = jnp.concatenate([v * beta[..., None], kb * jnp.exp(gc)[..., None]], axis=-1)
    sol = lax.linalg.triangular_solve(a, rhs, left_side=True, lower=True, unit_diagonal=True)
    u, w = sol[..., :dv], sol[..., dv:]
    att = jnp.einsum('bhncd,bhnsd->bhncs', q, k) * decay
    q_dec = q * jnp.exp(gc)[..., None]
    k_tail = k * jnp.exp(gc[..., -1:] - gc)[..., None]
    g_last = jnp.exp(gc[..., -1])

    def step(state, inp):
        u_n, w_n, qd_n, att_n, kt_n, gl_n = inp
        v_new = u_n - jnp.einsum('bhcd,bhde->bhce', w_n, state)
        o_n = jnp.einsum('bhcd,bhde->bhce', qd_n, state) + jnp.einsum('bhcs,bhse->bhce', att_n, v_new)
        state = state * gl_n[..., None, None] + jnp.einsum('bhcd,bhce->bhde', kt_n, v_new)
        return state, o_n

    xs = (jnp.moveaxis(u, 2, 0), jnp.moveaxis(w, 2, 0), jnp.moveaxis(q_dec, 2, 0),
          jnp.moveaxis(att, 2, 0), jnp.moveaxis(k_tail, 2, 0), jnp.moveaxis(g_last, 2, 0))
    s0 = jnp.zeros((bsz, nh, dk, dv), jnp.float32)
    _, o = lax.scan(step, s0, xs)
    return o.transpose(1, 0, 3, 2, 4).reshape(bsz, seq, nh, dv)

def gated_deltanet(q, k, v, z, b, a, conv_w, a_log, dt_bias, norm_g):
    bsz, seq = q.shape[0], q.shape[1]
    qkv = jax.nn.silu(causal_depthwise_conv(jnp.concatenate([q, k, v], axis=-1), conv_w))
    qkv = qkv.astype(jnp.float32)
    q, k, v = jnp.split(qkv, 3, axis=-1)
    q = l2_norm(q.reshape(bsz, seq, B_HEADS, B_HEAD_DIM))
    k = l2_norm(k.reshape(bsz, seq, B_HEADS, B_HEAD_DIM))
    v = v.reshape(bsz, seq, B_HEADS, B_HEAD_DIM)
    beta = jax.nn.sigmoid(b.astype(jnp.float32))
    g = -jnp.exp(a_log.astype(jnp.float32)) * jax.nn.softplus(a.astype(jnp.float32) + dt_bias.astype(jnp.float32))
    o = gated_delta_rule_chunked(q, k, v, g, beta)
    zf = z.reshape(bsz, seq, B_HEADS, B_HEAD_DIM).astype(jnp.float32)
    o = rms_norm(o, norm_g) * jax.nn.silu(zf)
    return o.reshape(bsz, seq, B_HEADS * B_HEAD_DIM).astype(z.dtype)

def setup_inputs(seed: int = 0) -> dict:
    key = jax.random.key(seed)
    ks = jax.random.split(key, 13)
    f32 = jnp.float32
    x = jax.random.normal(ks[0], (BATCH, SEQ, D_MODEL), f32)
    norm_mix_g = 1.0 + 0.02 * jax.random.normal(ks[1], (DEPTH, D_MODEL), f32)
    w_in = jax.random.normal(ks[2], (DEPTH, D_MODEL, IN_DIM), f32) * (D_MODEL ** -0.5)
    conv_w = jax.random.normal(ks[3], (DEPTH, CONV_WIDTH, B_CONV_CH), f32) * (CONV_WIDTH ** -0.5)
    a_log = jnp.log(jax.random.uniform(ks[4], (DEPTH, B_HEADS), f32, minval=1.0, maxval=16.0))
    dt = jnp.exp(jax.random.uniform(ks[5], (DEPTH, B_HEADS), f32, minval=np.log(1e-3), maxval=np.log(1e-1)))
    dt_bias = dt + jnp.log(-jnp.expm1(-dt))
    gdn_norm_g = 1.0 + 0.02 * jax.random.normal(ks[6], (DEPTH, B_HEAD_DIM), f32)
    w_out = jax.random.normal(ks[7], (DEPTH, MIX_WIDTH, D_MODEL), f32) * (MIX_WIDTH ** -0.5)
    norm_ffn_g = 1.0 + 0.02 * jax.random.normal(ks[8], (DEPTH, D_MODEL), f32)
    w_ff1 = jax.random.normal(ks[9], (DEPTH, D_MODEL, D_FF), f32) * (D_MODEL ** -0.5)
    w_ff2 = jax.random.normal(ks[10], (DEPTH, D_FF, D_MODEL), f32) * (D_FF ** -0.5)
    norm_final_g = 1.0 + 0.02 * jax.random.normal(ks[11], (D_MODEL,), f32)
    return {'x': x, 'norm_mix_g': norm_mix_g, 'w_in': w_in, 'conv_w': conv_w,
            'a_log': a_log, 'dt_bias': dt_bias, 'gdn_norm_g': gdn_norm_g, 'w_out': w_out,
            'norm_ffn_g': norm_ffn_g, 'w_ff1': w_ff1, 'w_ff2': w_ff2, 'norm_final_g': norm_final_g}

def reference(x, norm_mix_g, w_in, conv_w, a_log, dt_bias, gdn_norm_g, w_out,
              norm_ffn_g, w_ff1, w_ff2, norm_final_g):
    bsz, seq = x.shape[0], x.shape[1]
    pos = jnp.arange(seq)
    for l in range(DEPTH):
        h = rms_norm(x, norm_mix_g[l])
        proj = h @ w_in[l]
        (qa, ka, va, qi, ki, wi, qb, kb, vb, zb, bb, ab) = jnp.split(proj, SPLIT_POINTS, axis=-1)
        qa = rope(qa.reshape(bsz, seq, A_HEADS, A_HEAD_DIM), pos)
        ka = rope(ka.reshape(bsz, seq, A_KV_HEADS, A_HEAD_DIM), pos)
        va = va.reshape(bsz, seq, A_KV_HEADS, A_HEAD_DIM)
        qi = rope(qi.reshape(bsz, seq, IDX_HEADS, IDX_DIM), pos)
        ki = rope(ki.reshape(bsz, seq, 1, IDX_DIM), pos)[:, :, 0]
        wi = wi * ((IDX_HEADS ** -0.5) * (IDX_DIM ** -0.5))
        o_a = sparse_indexer_attention(qa, ka, va, qi, ki, wi)
        o_b = gated_deltanet(qb, kb, vb, zb, bb, ab, conv_w[l], a_log[l], dt_bias[l], gdn_norm_g[l])
        x = x + jnp.concatenate([o_a, o_b], axis=-1) @ w_out[l]
        h = rms_norm(x, norm_ffn_g[l])
        x = x + jnp.square(jax.nn.relu(h @ w_ff1[l])) @ w_ff2[l]
    return rms_norm(x, norm_final_g)


_drawn_inputs = setup_inputs


def setup_inputs(seed=0):
    import zlib

    import numpy as np

    out = dict(_drawn_inputs(seed))
    spreads = {}
    factors = {'norm_mix_g': 2.928, 'gdn_norm_g': 6.557, 'norm_ffn_g': 10.627, 'norm_final_g': 7.937}
    for name, (base, spread) in spreads.items():
        noise = np.random.default_rng([zlib.crc32(name.encode()), seed]).standard_normal(out[name].shape)
        drawn = base * np.exp(spread * noise) if base else spread * noise
        out[name] = __import__('jax').numpy.asarray(drawn.astype(out[name].dtype))
    for name, factor in factors.items():
        out[name] = (out[name] * factor).astype(out[name].dtype)
    return out
```

```python
import numpy as np
import concourse.bass as bass
from concourse import mybir
from contextlib import ExitStack

fp32 = mybir.dt.float32
f32r = mybir.dt.float32r
i32 = mybir.dt.int32
ALU = mybir.AluOpType
ACT = mybir.ActivationFunctionType

P = 128
D_MODEL, D_FF = 1024, 4096
KC = D_MODEL // P
A_HEADS, KV_HEADS, HD = 8, 2, 64
IDX_HEADS = 8
B_HEADS, BD = 4, 128
CONV = 4
TOPK_MAX, CHUNK = 256, 64
EPS = 1e-6
C_SMALL, C_QI, C_QA, C_KA, C_VA, C_CONV, C_Z, N_CHUNK = 0, 1, 5, 9, 10, 11, 23, 27
N_CONV = C_Z - C_CONV
HALO = 4
BARRED = -2.0e38
MASK_BIAS = -1.0e38


class Steps:

    def __init__(self, eng, sem):
        self.eng, self.sem, self.base, self.n = eng, sem, 0, 0

    def do(self, ins):
        ins.then_inc(self.sem, 1)
        self.n += 1
        self.eng.wait_ge(self.sem, self.base + self.n)

    def loop(self, done, i, per):
        self.base, self.n, self.at = i * per + done, 0, (done, per)

    def leave(self, turns):
        done, per = self.at
        assert self.n == per, self.n
        self.base, self.n = 0, done + per * turns


def norm_and_projection(nc, S, xT, g_mix, conv_w, w_proj, projT):
    XB = 256
    NX, NB = S // XB, S // 512
    with ExitStack() as ctx:
        sb = lambda n, s, d=fp32: ctx.enter_context(nc.sbuf_tensor(n, s, d))
        sem = lambda n: ctx.enter_context(nc.semaphore(n))
        xh = sb("xh", [P, KC, S], f32r)
        xl = sb("xl", [P, KC, S], f32r)
        work = sb("work", [P, 8192])
        xb = work[:, 0:4096].rearrange("p (u k s) -> p u k s", u=2, k=KC)
        xsq = work[:, 4096:6144].rearrange("p (k s) -> p k s", k=KC)
        xn = work[:, 6144:8192].rearrange("p (k s) -> p k s", k=KC)
        conv_acc = work[:, 0:2 * S].rearrange("p (u s) -> p u s", u=2)
        conv_out = work[:, 2 * S:4 * S].rearrange("p (u s) -> p u s", u=2)
        rstd = sb("rstd", [P, XB])
        ones = sb("ones", [P, P])
        gm = sb("gm", [P, KC])
        eps_col = sb("eps_col", [P, 1])
        cw = sb("cw", [P, N_CONV, CONV])
        wraw = sb("wraw", [P, 2, KC, P])
        wh = sb("wh", [P, 2, KC, P], f32r)
        wl = sb("wl", [P, 2, KC, P], f32r)
        stage = sb("stage", [P, 2, HALO + S])
        ps = ctx.enter_context(nc.psum_tensor("ps", [P, 8, 512], fp32))
        const_in, const_set = sem("const_in"), sem("const_set")
        pair = lambda n: [sem(f"{n}{u}") for u in range(2)]
        x_in, w_in, plain_out, conv_stored, z_out = map(pair, ["x_in", "w_in", "plain_out", "conv_stored", "z_out"])
        sq_done, ss_done, std_done, xn_done, xh_done, xl_done = map(
            sem, ["sq_done", "ss_done", "std_done", "xn_done", "xh_done", "xl_done"])
        w_hi, w_lo = map(sem, ["w_hi", "w_lo"])
        acc_done, evac_done = map(sem, ["acc_done", "evac_done"])
        conv_done, silu_done = map(sem, ["conv_done", "silu_done"])
        dve_s = sem("dve_s")
        N_PLAIN, N_Z = C_CONV, N_CHUNK - C_Z
        block = ctx.enter_context(nc.Block())

        @block.sync
        def _(sp):
            for stored in plain_out + conv_stored + z_out:
                sp.sem_inc(stored, 16)
            sp.dma_start(gm[:, :], g_mix).then_inc(const_in, 16)
            sp.dma_start(cw[:, :, :], conv_w).then_inc(const_in, 16)
            with sp.Fori(0, NX // 2) as i:
                for u in range(2):
                    sp.wait_ge(xl_done, 2 * i + u + 1)
                    sp.dma_start(xb[:, u, :, :], xT[:, :, bass.ds(i * 2 * XB + u * XB, XB)]).then_inc(x_in[u], 16)
            with sp.Fori(0, (N_CHUNK + 1) // 2) as i:
                for u in range(2):
                    sp.wait_ge(w_lo, 2 * i + u + 1)
                    sp.dma_start(wraw[:, u, :, :], w_proj[bass.ds(2 * i + u, 1)].rearrange(
                        "a p k n -> p (a k) n")).then_inc(w_in[u], 16)

        @block.gpsimd
        def _(pool):
            pool.sem_inc(w_lo, 2)
            nc.gpsimd.memset(ones[:, :], 1.0).then_inc(const_set, 1)
            nc.gpsimd.memset(stage[:, :, 0:HALO], 0.0).then_inc(const_set, 1)
            nc.gpsimd.memset(eps_col[:, :], EPS).then_inc(const_set, 1)
            with pool.Fori(0, (N_CHUNK + 1) // 2) as i:
                for u in range(2):
                    c = 2 * i + u
                    pool.wait_ge(w_hi, c + 1)
                    pool.wait_ge(acc_done, NB * c + NB)
                    nc.gpsimd.tensor_tensor(wl[:, u, :, :], wraw[:, u, :, :], wh[:, u, :, :].bitcast(fp32),
                                            ALU.subtract).then_inc(w_lo, 1)

        @block.vector
        def _(dve):
            st = Steps(dve, dve_s)
            dve.sem_inc(xl_done, 2)
            dve.wait_ge(const_in, 32)
            with dve.Fori(0, NX // 2) as i:
                st.loop(0, i, 2)
                for u in range(2):
                    b = 2 * i + u
                    tok = bass.ds(i * 2 * XB + u * XB, XB)
                    dve.wait_ge(std_done, b + 1)
                    st.do(nc.vector.reciprocal(rstd[:, :], rstd[:, :]))
                    for k in range(KC):
                        last = nc.vector.scalar_tensor_tensor(
                            out=xn[:, k, :], in0=xb[:, u, k, :], scalar=gm[:, k:k + 1], in1=rstd[:, :],
                            op0=ALU.mult, op1=ALU.mult)
                    last.then_inc(xn_done, 1)
                    dve.wait_ge(xh_done, b + 1)
                    nc.vector.tensor_tensor(xl[:, :, tok], xn[:, :, :], xh[:, :, tok].bitcast(fp32),
                                            ALU.subtract).then_inc(xl_done, 1)
                    dve.wait_ge(xl_done, b + 3)
            st.leave(NX // 2)
            done = st.n
            with dve.Fori(0, N_CONV // 2) as i:
                st.loop(done, i, 2 * (CONV - 1))
                for v in range(2):
                    k, u = 2 * i + v, (C_CONV + v) % 2
                    dve.wait_ge(evac_done, NB * k + NB * (C_CONV + 3))
                    dve.wait_ge(silu_done, k + 1)
                    st.do(nc.vector.tensor_scalar(conv_acc[:, u, :], stage[:, u, 1:1 + S],
                                                  cw[:, bass.ds(k, 1), 0:1].rearrange("p a b -> p (a b)"),
                                                  None, ALU.mult))
                    for j in range(1, CONV):
                        ins = nc.vector.scalar_tensor_tensor(
                            out=conv_acc[:, u, :], in0=stage[:, u, 1 + j:1 + j + S],
                            scalar=cw[:, bass.ds(k, 1), j:j + 1].rearrange("p a b -> p (a b)"),
                            in1=conv_acc[:, u, :], op0=ALU.mult, op1=ALU.add)
                        if j < CONV - 1:
                            st.do(ins)
                        else:
                            ins.then_inc(conv_done, 1)
            st.leave(N_CONV // 2)

        @block.scalar
        def _(act):
            act.sem_inc(evac_done, 2 * NB)
            act.sem_inc(conv_done, 2)
            act.sem_inc(silu_done, 2)
            with act.Fori(0, NX // 2) as i:
                for u in range(2):
                    b = 2 * i + u
                    act.wait_ge(x_in[u], 16 * i + 16)
                    nc.scalar.activation(xsq[:, :, :], xb[:, u, :, :], ACT.Square).then_inc(sq_done, 1)
                    act.wait_ge(ss_done, b + 1)
                    nc.scalar.activation(rstd[:, :], ps[:, 7, 0:XB], ACT.Sqrt, scale=1.0 / D_MODEL,
                                         bias=eps_col[:, :]).then_inc(std_done, 1)
                    act.wait_ge(xn_done, b + 1)
                    nc.scalar.activation(xh[:, :, bass.ds(i * 2 * XB + u * XB, XB)], xn[:, :, :],
                                         ACT.Copy).then_inc(xh_done, 1)

            def split_hi(c, turn, u):
                act.wait_ge(w_in[u], 16 * turn + 16)
                act.wait_ge(acc_done, NB * c + NB)
                nc.scalar.activation(wh[:, u, :, :], wraw[:, u, :, :], ACT.Copy).then_inc(w_hi, 1)

            def chunk(kind, c, turn, k, kturn, u):
                split_hi(c + 1, turn + u, 1 - u)
                if kind == "plain":
                    act.wait_ge(plain_out[u], 16 * kturn + 16)
                elif kind == "conv":
                    act.wait_ge(plain_out[u], 16 * ((N_PLAIN + 1 - u) // 2) + 16)
                    act.wait_ge(conv_done, k + 1)
                else:
                    act.wait_ge(z_out[u], 16 * kturn + 16)
                for tb in range(NB):
                    act.wait_ge(acc_done, NB * c + tb + 1 + 2 * NB)
                    nc.scalar.activation(stage[:, u, HALO + 512 * tb:HALO + 512 * (tb + 1)], ps[:, NB * u + tb, :],
                                         ACT.Silu if kind == "z" else ACT.Copy).then_inc(evac_done, 1)
                if kind == "conv":
                    act.wait_ge(conv_done, k + 3)
                    act.wait_ge(conv_stored[u], 16 * kturn + 16)
                    nc.scalar.activation(conv_out[:, u, :], conv_acc[:, u, :], ACT.Silu).then_inc(silu_done, 1)
                    act.wait_ge(silu_done, k + 3)
                    src, stored = conv_out[:, u, :], conv_stored
                else:
                    act.wait_ge(evac_done, NB * c + 3 * NB)
                    src, stored = stage[:, u, HALO:HALO + S], plain_out if kind == "plain" else z_out
                act.dma_start(projT[bass.ds(c, 1)].rearrange("a p s -> p (a s)"), src).then_inc(stored[u], 16)

            split_hi(0, 0, 0)
            chunk("plain", 0, 0, 0, 0, 0)
            for kind, first, n in (("plain", 1, N_PLAIN - 1), ("conv", C_CONV, N_CONV), ("z", C_Z, N_Z)):
                with act.Fori(0, n // 2) as i:
                    for v, u in ((0, 1), (1, 0)):
                        k = 2 * i + v + (1 if kind == "plain" else 0)
                        chunk(kind, 2 * i + (first + v), i + (first + v) // 2, k, i + (v if kind == "plain" else 0), u)
            for u in range(2):
                act.wait_ge(plain_out[u], 16 * ((N_PLAIN + 1 - u) // 2) + 16)
                act.wait_ge(conv_stored[u], 16 * (N_CONV // 2) + 16)
                act.wait_ge(z_out[u], 16 * (N_Z // 2) + 16)

        @block.tensor
        def _(pe):
            pe.sem_inc(acc_done, 2 * NB)
            pe.wait_ge(const_set, 3)
            with pe.Fori(0, NX) as i:
                pe.wait_ge(sq_done, i + 1)
                for k in range(KC):
                    last = nc.tensor.matmul(ps[:, 7, 0:XB], ones[:, :], xsq[:, k, :], start=(k == 0), stop=(k == KC - 1))
                last.then_inc(ss_done, 1)
            pe.wait_ge(xl_done, NX + 2)

            def project(c, u):
                pe.wait_ge(w_lo, c + 3)
                for tb in range(NB):
                    pe.wait_ge(evac_done, NB * c + tb + 1)
                    tok = slice(512 * tb, 512 * (tb + 1))
                    for kc in range(KC):
                        acc = ps[:, NB * u + tb, :]
                        nc.tensor.matmul(acc, wh[:, u, kc, :], xh[:, kc, tok], start=(kc == 0), stop=False)
                        nc.tensor.matmul(acc, wh[:, u, kc, :], xl[:, kc, tok], start=False, stop=False)
                        last = nc.tensor.matmul(acc, wl[:, u, kc, :], xh[:, kc, tok], start=False, stop=(kc == KC - 1))
                    last.then_inc(acc_done, 1)

            with pe.Fori(0, N_CHUNK // 2) as i:
                for u in range(2):
                    project(2 * i + u, u)
            project(N_CHUNK - 1, 0)


R_W, R_B, R_A = 0, IDX_HEADS, IDX_HEADS + B_HEADS
N_SMALL = IDX_HEADS + 2 * B_HEADS


def gated_deltanet(nc, S, projT, a_log, dt_bias, g_gdn, consts, mixT):
    NT = S // P
    H, W = B_HEADS, B_HEADS * P
    QK = float(BD) ** -0.5
    with ExitStack() as ctx:
        sb = lambda n, s, d=fp32: ctx.enter_context(nc.sbuf_tensor(n, s, d))
        sem = lambda n: ctx.enter_context(nc.semaphore(n))
        ident = sb("g_ident", [P, P])
        triu = sb("g_triu", [P, P])
        ones = sb("g_ones", [P, P])
        incl = sb("g_incl", [P, P])
        strict = sb("g_strict", [P, P])
        diag16 = sb("g_diag16", [P, P])
        off16 = sb("g_off16", [P, P])
        small = sb("g_small", [N_SMALL, S])
        eps_col = sb("g_eps", [P, 1])
        eps_ms = sb("g_eps_ms", [P, 1])
        one_col = sb("g_one", [P, 1])
        alog = sb("g_alog", [P, H])
        dtb = sb("g_dtb", [P, H])
        gg = sb("g_gg", [P, 1])
        sm = sb("g_sm", [P, NT, N_SMALL])
        beta = sb("g_beta", [P, NT, H])
        gate = sb("g_gate", [P, NT, H])
        sp_a = sb("g_spa", [P, NT, H])
        sp_b = sb("g_spb", [P, NT, H])
        gcum = sb("g_gcum", [P, NT, H])
        egc = sb("g_egc", [P, NT, H])
        nbeg = sb("g_nbeg", [P, NT, H])
        qkvz = sb("g_qkvz", [P, 2, 4, H, P])
        sq = sb("g_sq", [P, 2, H, P])
        rn = sb("g_rn", [P, 2, H, P])
        qk = sb("g_qk", [P, 2, H, P])
        big = {n: sb("g_" + n, [P, H, P]) for n in
               "G X D Dq Ds EG N at m n LT L Y n2 m2 n4 m4 n8 Dinv E F E2 F2 E4 Z attT kt kbe vb qd wT vnew osq orn otmp".split()}
        B = lambda n: big[n][:, :, :]
        out_b = sb("g_out", [P, 2, H, P])
        st_S = sb("g_state", [P, H, P])
        tail = sb("g_tail", [P, H])
        etail = sb("g_etail", [P, H])
        ps = ctx.enter_context(nc.psum_tensor("g_ps", [P, 8, H, P], fp32))
        const_in, const_set = sem("g_const_in"), sem("g_const_set")
        load = [sem(f"g_load{u}") for u in range(2)]
        stored = [sem(f"g_stored{u}") for u in range(2)]
        dve_s, act_s, pool_s, pe_s = sem("g_dve"), sem("g_act"), sem("g_pool"), sem("g_pe")
        block = ctx.enter_context(nc.Block())
        ph = lambda a: a.rearrange("p a b -> p (a b)")
        bc = lambda m: m[:, :].unsqueeze(1).to_broadcast([P, H, P])

        PE = {n: i + 1 for i, n in enumerate("ss gb kk att tr kT vT n2 m2 n4 m4 Y1 n8 Y2 Y3 Dinv E F E2 F2 Z1 E4 Z2 Z3 wT vnew out state oss".split())}
        DV = {n: i + 1 for i, n in enumerate("G rn qk X tail N at m LT qd kt kbe vb m2 Y1 m4 Y2 Y3 F F2 Z1 Z2 Z3 vnew S orn otmp".split())}
        AC = {n: i + 1 for i, n in enumerate("sq rn EG D etail attT n2 n4 n8 Dinv E E2 E4 wT osq orn".split())}
        PO = {n: i + 1 for i, n in enumerate("X Dq Ds n L Y out".split())}
        PE0, DV0, AC0, PO0 = 2, 7, 6, 0

        @block.sync
        def _(sp):
            for dst, src in ((ident[:, :], consts["ident"]), (triu[:, :], consts["triu"]), (incl[:, :], consts["incl"]),
                             (strict[:, :], consts["strict"]), (diag16[:, :], consts["diag16"]), (off16[:, :], consts["off16"]),
                             (small[:, :], projT[0, 0:N_SMALL, :]), (alog[:, :], a_log.to_broadcast([P, H])),
                             (dtb[:, :], dt_bias.to_broadcast([P, H])), (gg[:, :], g_gdn)):
                sp.dma_start(dst, src).then_inc(const_in, 16)
            for u in range(2):
                sp.sem_inc(stored[u], 16)
            with sp.Fori(0, NT // 2) as i:
                for u in range(2):
                    t = 2 * i + u
                    sp.wait_ge(stored[u], 16 * i + 16)
                    sp.dma_start(qkvz[:, u, :, :, :].rearrange("p a h s -> p (a h) s"),
                                 projT[C_CONV:N_CHUNK, :, bass.ds(i * 2 * P + u * P, P)].rearrange("c p s -> p c s")
                                 ).then_inc(load[u], 16)
                for u in range(2):
                    t = 2 * i + u
                    sp.wait_ge(pool_s, PO0 + len(PO) * t + PO["out"])
                    sp.dma_start(mixT[4:8, :, bass.ds(i * 2 * P + u * P, P)].rearrange("c p s -> p c s"),
                                 out_b[:, u, :, :]).then_inc(stored[u], 16)
            for u in range(2):
                sp.wait_ge(stored[u], 16 * (NT // 2) + 16)

        @block.gpsimd
        def _(pool):
            nc.gpsimd.memset(ones[:, :], 1.0).then_inc(const_set, 1)
            nc.gpsimd.memset(eps_col[:, :], EPS).then_inc(const_set, 1)
            nc.gpsimd.memset(one_col[:, :], 1.0).then_inc(const_set, 1)
            nc.gpsimd.memset(st_S[:, :, :], 0.0).then_inc(const_set, 1)
            pool.wait_ge(const_in, 160)
            with pool.Fori(0, NT // 2) as i:
                for u in range(2):
                    t = 2 * i + u
                    step = lambda ins: ins.then_inc(pool_s, 1)
                    dv = lambda n: pool.wait_ge(dve_s, DV0 + len(DV) * t + DV[n])
                    ac = lambda n: pool.wait_ge(act_s, AC0 + len(AC) * t + AC[n])
                    po = lambda n: pool.wait_ge(pool_s, PO0 + len(PO) * t + PO[n])
                    dv("X")
                    step(nc.gpsimd.tensor_tensor(B("X"), B("X"), bc(incl), ALU.mult))
                    ac("D")
                    step(nc.gpsimd.tensor_tensor(B("Dq"), B("D"), bc(incl), ALU.mult))
                    step(nc.gpsimd.tensor_tensor(B("Ds"), B("D"), bc(strict), ALU.mult))
                    dv("N")
                    step(nc.gpsimd.tensor_tensor(B("n"), B("N"), bc(diag16), ALU.mult))
                    step(nc.gpsimd.tensor_tensor(B("L"), B("N"), bc(off16), ALU.mult))
                    dv("m")
                    step(nc.gpsimd.tensor_tensor(B("Y"), bc(ident), B("m"), ALU.subtract))
                    dv("otmp")
                    pool.wait_ge(stored[u], 16 * i + 16)
                    step(nc.gpsimd.tensor_tensor(out_b[:, u, :, :], B("otmp"), qkvz[:, u, 3, :, :], ALU.mult))

        @block.tensor
        def _(pe):
            pe.wait_ge(const_in, 160)
            pe.wait_ge(const_set, 4)
            for t in range(NT):
                last = nc.tensor.transpose(ps[:, 0, :, :].rearrange("p a b -> p (a b)")[:, t * N_SMALL:(t + 1) * N_SMALL],
                                           small[:, t * P:(t + 1) * P], ident[0:N_SMALL, 0:N_SMALL])
            last.then_inc(pe_s, 1)
            pe.wait_ge(dve_s, 6)
            nc.tensor.matmul(ph(ps[:, 1, :, :])[:, 0:NT * H], triu[:, :], gate[:, :, :].rearrange("p a b -> p (a b)"),
                             start=True, stop=True).then_inc(pe_s, 1)
            pe.wait_ge(dve_s, 7)
            pe.wait_ge(act_s, 6)
            with pe.Fori(0, NT // 2) as i:
                for u in range(2):
                    t = 2 * i + u
                    dv = lambda n: pe.wait_ge(dve_s, DV0 + len(DV) * t + DV[n])
                    ac = lambda n: pe.wait_ge(act_s, AC0 + len(AC) * t + AC[n])
                    po = lambda n: pe.wait_ge(pool_s, PO0 + len(PO) * t + PO[n])

                    def heads(bank, lhsT, rhs, more=None):
                        for h in range(H):
                            last = nc.tensor.matmul(ps[:, bank, h, :], lhsT[:, h, :], rhs[:, h, :], start=True, stop=more is None)
                            if more:
                                last = nc.tensor.matmul(ps[:, bank, h, :], more[0][:, h, :], more[1][:, h, :], start=False, stop=True)
                        last.then_inc(pe_s, 1)

                    def transposes(bank, src):
                        for h in range(H):
                            last = nc.tensor.transpose(ps[:, bank, h, :], src[:, h, :], ident[:, :])
                        last.then_inc(pe_s, 1)

                    ac("sq")
                    for a in range(2):
                        last = nc.tensor.matmul(ph(ps[:, a, :, :]), ones[:, :], ph(sq[:, a, :, :]), start=True, stop=True)
                    last.then_inc(pe_s, 1)
                    dv("G")
                    nc.tensor.matmul(ph(ps[:, 2, :, :]), ones[:, :], ph(B("G")), start=True, stop=True).then_inc(pe_s, 1)
                    dv("qk")
                    heads(3, qk[:, 1, :, :], qk[:, 1, :, :])
                    heads(4, qk[:, 0, :, :], qk[:, 1, :, :])
                    dv("N")
                    dv("at")
                    for h in range(H):
                        nc.tensor.transpose(ps[:, 5, h, :], big["N"][:, h, :], ident[:, :])
                    for h in range(H):
                        last = nc.tensor.transpose(ps[:, 6, h, :], big["at"][:, h, :], ident[:, :])
                    last.then_inc(pe_s, 1)
                    transposes(7, qk[:, 1, :, :])
                    transposes(0, qkvz[:, u, 2, :, :])
                    dv("m")
                    po("n")
                    ac("EG")
                    heads(1, B("m"), B("n"))
                    heads(2, B("n"), B("m"))
                    ac("n2")
                    dv("m2")
                    heads(3, B("m2"), B("n2"))
                    heads(4, B("n2"), B("m2"))
                    po("Y")
                    dv("LT")
                    heads(5, B("n2"), B("Y"))
                    ac("n4")
                    dv("m4")
                    ac("attT")
                    heads(6, B("m4"), B("n4"))
                    dv("Y1")
                    dv("kbe")
                    heads(7, B("n4"), B("Y"))
                    dv("Y2")
                    ac("n8")
                    heads(1, B("n8"), B("Y"))
                    dv("Y3")
                    transposes(2, B("Y"))
                    ac("Dinv")
                    heads(3, B("LT"), B("Dinv"))
                    heads(4, B("Dinv"), B("LT"))
                    ac("E")
                    dv("F")
                    heads(5, B("F"), B("E"))
                    heads(6, B("E"), B("F"))
                    heads(7, B("E"), B("Y"))
                    ac("E2")
                    dv("F2")
                    heads(1, B("F2"), B("E2"))
                    dv("Z1")
                    heads(2, B("E2"), B("Z"))
                    ac("E4")
                    dv("Z2")
                    heads(3, B("E4"), B("Z"))
                    dv("Z3")
                    heads(4, B("kbe"), B("Z"))
                    ac("wT")
                    heads(5, B("Z"), B("vb"), (B("wT"), st_S[:, :, :]))
                    dv("vnew")
                    heads(6, st_S[:, :, :], B("qd"), (B("vnew"), B("attT")))
                    heads(7, B("kt"), B("vnew"))
                    ac("osq")
                    dv("vb")
                    nc.tensor.matmul(ph(ps[:, 0, :, :]), ones[:, :], ph(B("osq")), start=True, stop=True).then_inc(pe_s, 1)

        @block.scalar
        def _(act):
            n = [0]

            def step(ins):
                ins.then_inc(act_s, 1)
                n[0] += 1

            act.wait_ge(const_set, 4)
            act.wait_ge(const_in, 160)
            act.wait_ge(dve_s, 1)
            step(nc.scalar.activation(beta[:, :, :], sm[:, :, R_B:R_B + H], ACT.Sigmoid))
            act.wait_ge(dve_s, 3)
            step(nc.scalar.activation(sp_b[:, :, :], sp_b[:, :, :], ACT.Exp))
            act.wait_ge(act_s, 2)
            step(nc.scalar.activation(sp_b[:, :, :], sp_b[:, :, :], ACT.Ln, bias=one_col[:, :]))
            step(nc.scalar.activation(alog[:, :], alog[:, :], ACT.Exp))
            act.wait_ge(pe_s, 2)
            step(nc.scalar.activation(gcum[:, :, :].rearrange("p a b -> p (a b)"), ph(ps[:, 1, :, :])[:, 0:NT * H], ACT.Copy))
            act.wait_ge(act_s, 5)
            step(nc.scalar.activation(egc[:, :, :], gcum[:, :, :], ACT.Exp))
            assert n[0] == AC0
            with act.Fori(0, NT // 2) as i:
                for u in range(2):
                    t = 2 * i + u
                    n[0] = 0
                    dv = lambda m: act.wait_ge(dve_s, DV0 + len(DV) * t + DV[m])
                    pe = lambda m: act.wait_ge(pe_s, PE0 + len(PE) * t + PE[m])
                    po = lambda m: act.wait_ge(pool_s, PO0 + len(PO) * t + PO[m])
                    act.wait_ge(load[u], 16 * i + 16)
                    step(nc.scalar.activation(sq[:, :, :, :], qkvz[:, u, 0:2, :, :], ACT.Square))
                    pe("ss")
                    step(nc.scalar.activation(rn[:, :, :, :], ps[:, 0:2, :, :], ACT.Sqrt, bias=eps_col[:, :]))
                    pe("gb")
                    step(nc.scalar.activation(B("EG"), ps[:, 2, :, :], ACT.Exp))
                    po("X")
                    step(nc.scalar.activation(B("D"), B("X"), ACT.Exp, scale=-1.0))
                    dv("tail")
                    step(nc.scalar.activation(etail[:, :], tail[:, :], ACT.Exp))
                    pe("tr")
                    step(nc.scalar.activation(B("attT"), ps[:, 6, :, :], ACT.Copy))
                    for name, bank in (("n2", 1), ("n4", 3), ("n8", 6), ("Dinv", 2), ("E", 3), ("E2", 5), ("E4", 1), ("wT", 4)):
                        pe(name)
                        step(nc.scalar.activation(B(name), ps[:, bank, :, :], ACT.Copy))
                    pe("out")
                    step(nc.scalar.activation(B("osq"), ps[:, 6, :, :], ACT.Square))
                    pe("oss")
                    step(nc.scalar.activation(B("orn"), ps[:, 0, :, :], ACT.Sqrt, scale=1.0 / BD, bias=eps_col[:, :]))
                    assert n[0] == len(AC)

        @block.vector
        def _(dve):
            n = [0]

            def step(ins):
                ins.then_inc(dve_s, 1)
                n[0] += 1

            dve.wait_ge(const_in, 160)
            dve.wait_ge(pe_s, 1)
            step(nc.vector.tensor_copy(sm[:, :, :].rearrange("p a b -> p (a b)"), ph(ps[:, 0, :, :])[:, 0:NT * N_SMALL]))
            dve.wait_ge(dve_s, 1)
            step(nc.vector.tensor_tensor(sp_a[:, :, :], sm[:, :, R_A:R_A + H],
                                         dtb[:, :].unsqueeze(1).to_broadcast([P, NT, H]), ALU.add))
            dve.wait_ge(dve_s, 2)
            step(nc.vector.scalar_tensor_tensor(out=sp_b[:, :, :], in0=sp_a[:, :, :], scalar=-1.0, in1=sp_a[:, :, :],
                                                op0=ALU.mult, op1=ALU.min))
            dve.wait_ge(act_s, 4)
            step(nc.vector.scalar_tensor_tensor(out=sp_a[:, :, :], in0=sp_a[:, :, :], scalar=0.0, in1=sp_b[:, :, :],
                                                op0=ALU.max, op1=ALU.add))
            dve.wait_ge(dve_s, 4)
            step(nc.vector.scalar_tensor_tensor(out=gate[:, :, :], in0=sp_a[:, :, :], scalar=-1.0,
                                                in1=alog[:, :].unsqueeze(1).to_broadcast([P, NT, H]),
                                                op0=ALU.mult, op1=ALU.mult))
            dve.wait_ge(dve_s, 5)
            step(nc.vector.tensor_copy(sp_a[:, :, :], gate[:, :, :]))
            dve.wait_ge(act_s, 6)
            step(nc.vector.scalar_tensor_tensor(out=nbeg[:, :, :], in0=beta[:, :, :], scalar=-1.0, in1=egc[:, :, :],
                                                op0=ALU.mult, op1=ALU.mult))
            assert n[0] == DV0
            with dve.Fori(0, NT // 2) as i:
                for u in range(2):
                    t = 2 * i + u
                    n[0] = 0
                    own = lambda m: dve.wait_ge(dve_s, DV0 + len(DV) * t + DV[m])
                    ac = lambda m: dve.wait_ge(act_s, AC0 + len(AC) * t + AC[m])
                    pe = lambda m: dve.wait_ge(pe_s, PE0 + len(PE) * t + PE[m])
                    po = lambda m: dve.wait_ge(pool_s, PO0 + len(PO) * t + PO[m])
                    tile = lambda a: a[:, bass.ds(t, 1), :].rearrange("p a h -> p (a h)")
                    col = lambda a: tile(a).unsqueeze(2).to_broadcast([P, H, P])
                    step(nc.vector.tensor_tensor(B("G"), bc(triu), col(gate), ALU.mult))
                    ac("rn")
                    step(nc.vector.reciprocal(rn[:, :, :, :], rn[:, :, :, :]))
                    own("rn")
                    step(nc.vector.tensor_tensor(qk[:, :, :, :], qkvz[:, u, 0:2, :, :], rn[:, :, :, :], ALU.mult))
                    ac("EG")
                    step(nc.vector.tensor_tensor(B("X"), ps[:, 2, :, :], col(gcum), ALU.subtract))
                    step(nc.vector.tensor_tensor(tail[:, :], ps[:, 2, :, P - 1:P].rearrange("p a b -> p (a b)"), tile(gcum), ALU.subtract))
                    pe("att")
                    po("Ds")
                    for h in range(H):
                        last = nc.vector.scalar_tensor_tensor(out=big["N"][:, h, :], in0=ps[:, 3, h, :],
                                                              scalar=beta[:, bass.ds(t, 1), h:h + 1].rearrange("p a b -> p (a b)"),
                                                              in1=big["Ds"][:, h, :], op0=ALU.mult, op1=ALU.mult)
                    step(last)
                    step(nc.vector.scalar_tensor_tensor(out=ph(B("at")), in0=ph(ps[:, 4, :, :]), scalar=QK, in1=ph(B("Dq")),
                                                        op0=ALU.mult, op1=ALU.mult))
                    pe("tr")
                    step(nc.vector.tensor_tensor(B("m"), ps[:, 5, :, :], bc(diag16), ALU.mult))
                    step(nc.vector.tensor_tensor(B("LT"), ps[:, 5, :, :], bc(off16), ALU.mult))
                    ac("EG")
                    step(nc.vector.scalar_tensor_tensor(out=ph(B("qd")), in0=ph(qk[:, 0, :, :]), scalar=QK, in1=ph(B("EG")),
                                                        op0=ALU.mult, op1=ALU.mult))
                    ac("etail")
                    pe("kT")
                    step(nc.vector.tensor_tensor(B("kt"), ps[:, 7, :, :], etail[:, :].unsqueeze(2).to_broadcast([P, H, P]), ALU.mult))
                    step(nc.vector.tensor_tensor(B("kbe"), ps[:, 7, :, :], col(nbeg), ALU.mult))
                    pe("vT")
                    step(nc.vector.tensor_tensor(B("vb"), ps[:, 0, :, :], col(beta), ALU.mult))
                    pe("m2")
                    step(nc.vector.tensor_copy(B("m2"), ps[:, 2, :, :]))
                    po("Y")

                    def add(name, bank, out, acc, op=ALU.add):
                        pe(name)
                        step(nc.vector.tensor_tensor(B(out), B(acc), ps[:, bank, :, :], op))

                    add("Y1", 5, "Y", "Y")
                    pe("m4")
                    step(nc.vector.tensor_copy(B("m4"), ps[:, 4, :, :]))
                    own("Y1")
                    add("Y2", 7, "Y", "Y")
                    own("Y2")
                    add("Y3", 1, "Y", "Y")
                    pe("F")
                    step(nc.vector.tensor_copy(B("F"), ps[:, 4, :, :]))
                    pe("F2")
                    step(nc.vector.tensor_copy(B("F2"), ps[:, 6, :, :]))
                    own("Y3")
                    add("Z1", 7, "Z", "Y", ALU.subtract)
                    own("Z1")
                    add("Z2", 2, "Z", "Z")
                    own("Z2")
                    add("Z3", 3, "Z", "Z")
                    pe("vnew")
                    step(nc.vector.tensor_copy(B("vnew"), ps[:, 5, :, :]))
                    pe("state")
                    for h in range(H):
                        last = nc.vector.scalar_tensor_tensor(out=st_S[:, h, :], in0=st_S[:, h, :], scalar=big["EG"][:, h, P - 1:P],
                                                              in1=ps[:, 7, h, :], op0=ALU.mult, op1=ALU.add)
                    step(last)
                    ac("orn")
                    step(nc.vector.reciprocal(B("orn"), B("orn")))
                    own("orn")
                    step(nc.vector.scalar_tensor_tensor(out=ph(B("otmp")), in0=ph(ps[:, 6, :, :]), scalar=gg[:, 0:1], in1=ph(B("orn")),
                                                        op0=ALU.mult, op1=ALU.mult))
                    assert n[0] == len(DV)


def indexed_attention(nc, S, topk, projT, consts, mixT):
    NT, PIECE = S // P, 1024
    G = A_HEADS // KV_HEADS
    with ExitStack() as ctx:
        sb = lambda n, s, d=fp32: ctx.enter_context(nc.sbuf_tensor(n, s, d))
        sem = lambda n: ctx.enter_context(nc.semaphore(n))
        ident, ones = sb("a_ident", [P, P]), sb("a_ones", [P, P])
        cosT, sinT = sb("a_cos", [P, S]), sb("a_sin", [P, S])
        small = sb("a_small", [IDX_HEADS, S])
        w_idx = sb("a_w", [P, NT, IDX_HEADS])
        keys = sb("a_keys", [P, 1 + KV_HEADS, S], f32r)
        vals = sb("a_vals", [P, NT, KV_HEADS * HD])
        rot = sb("a_rot", [P, 2, 8, P])
        rot2 = sb("a_rot2", [P, 2, 8, P])
        q_hi = [sb(f"a_qhi{k}", [P, 8, P], f32r) for k in range(2)]
        q_lo = [sb(f"a_qlo{k}", [P, 8, P], f32r) for k in range(2)]
        score = sb("a_score", [P, S])
        left = sb("a_left", [P, S])
        bias = sb("a_bias", [P, S])
        relu = sb("a_relu", [P, 2, PIECE])
        prob = sb("a_prob", [P, A_HEADS, S])
        BITS = 31
        count, bound, sign, value, room = [sb("a_" + n, [P, 1]) for n in "count bound sign value room".split()]
        trial, drop = sb("a_trial", [P, 1], i32), sb("a_drop", [P, 1], i32)
        mx = sb("a_mx", [P, 2, A_HEADS])
        nmx = sb("a_nmx", [P, A_HEADS])
        rsum = sb("a_rsum", [P, A_HEADS])
        rinv = sb("a_rinv", [P, A_HEADS])
        diag = sb("a_diag", [P, G, P])
        pT = sb("a_pT", [P, 2, G * P])
        rb = sb("a_rb", [HD, KV_HEADS, G * P])
        out = sb("a_out", [HD, 2, G, P])
        ps = ctx.enter_context(nc.psum_tensor("a_ps", [P, 8, 512], fp32))
        slot_ps = lambda n, w: ps[:, 2 * (n % 2):2 * (n % 2) + 2, :].rearrange("p a b -> p (a b)")[:, 0:w]

        const_in, const_set, key_in, key_rot, key_tmp, key_done, v_in, v_T, v_done, w_T = map(sem, (
            "a_const_in a_const_set a_key_in a_key_rot a_key_tmp a_key_done a_v_in a_v_T a_v_done a_w_T").split())
        q_in, q_mul, q_rot, q_hid, q_lod = [[sem(f"a_{n}{k}") for k in range(2)] for n in
                                                    "q_in q_mul q_rot q_hi_done q_lo_done".split()]
        idx_done, relu_done, acc_done, att_done, masked = map(sem, "a_idx a_relu a_acc a_att a_masked".split())
        max_done, exp_done, pT_done, pT_evac, rinv_done, diag_done, o_done, rb_done, norm_done = map(
            sem, "a_max a_exp a_pTd a_pTe a_rinvd a_diagd a_o a_rbd a_norm".split())
        stored = [sem(f"a_stored{u}") for u in range(2)]
        dve_s, w_done = sem("a_dve"), sem("a_w_done")

        def pieces(t):
            n = (t + 1) * P
            return [(a, min(PIECE, n - a)) for a in range(0, n, PIECE)]

        selects = [t for t in range(NT) if (t + 1) * P > topk]
        assert all(t * P + CHUNK >= topk for t in selects)
        items = []
        of_tile = lambda kind, t: [(kind, t, h, p) for h in range(8) for p in range(len(pieces(t)))] \
            if kind == "att" or t in selects else []
        items += of_tile("idx", 0)
        for t in range(NT):
            items += of_tile("att", t) + (of_tile("idx", t + 1) if t + 1 < NT else [])
        place = {it: n for n, it in enumerate(items)}
        number, seen = {}, {"idx": 0, "att": 0}
        for it in items:
            seen[it[0]] += 1
            number[it] = seen[it[0]]
        kinds = ("idx", "att")

        def wait_q_used(eng, k, t):
            n = sum(1 for it in items if it[0] == kinds[k] and it[1] < t)
            if n:
                eng.wait_ge((idx_done, att_done)[k], n)

        chunks_before = lambda t: sum(i + 1 for i in range(t)) * KV_HEADS
        block = ctx.enter_context(nc.Block())

        rows = projT.rearrange("c p s -> (c p) s")
        out_rows = mixT.rearrange("c p s -> (c p) s")
        heads_of = lambda c, n, tok: rows[c * P:c * P + n * HD, tok].rearrange("(h r) s -> r h s", r=HD)

        def load_rotated(eng, a, b, src, sem_in):
            half = HD // 2
            for base in (0, HD):
                eng.dma_start(a[base:base + HD], src).then_inc(sem_in, 16)
                eng.dma_start(b[base:base + half], src[half:HD]).then_inc(sem_in, 16)
                eng.dma_start(b[base + half:base + HD], src[0:half]).then_inc(sem_in, 16)

        KP = min(S, 1024)
        key_steps = [(k, a) for k in range(1 + KV_HEADS) for a in range(0, S, KP)]
        flat = lambda r, k: r[:, k, :, :].rearrange("p a b -> p (a b)")[:, 0:KP]

        @block.sync
        def _(sp):
            for dst, src in ((ident[:, :], consts["ident"]), (cosT[:, :], consts["cosT"]), (sinT[:, :], consts["sinT"]),
                             (small[:, :], projT[C_SMALL, R_W:R_W + IDX_HEADS, :])):
                sp.dma_start(dst, src).then_inc(const_in, 16)
            sp.dma_start(prob[:, 0, :], projT[C_VA]).then_inc(v_in, 16)
            for n, (k, a) in enumerate(key_steps):
                if n:
                    sp.wait_ge(key_done, n)
                row = C_SMALL * P + HD if k == 0 else C_KA * P + (k - 1) * HD
                load_rotated(sp, flat(rot, 0), flat(rot, 1), rows[row:row + HD, a:a + KP], key_in)
            sp.wait_ge(key_done, len(key_steps))

            def store(t):
                for g in range(KV_HEADS):
                    sp.wait_ge(norm_done, KV_HEADS * t + g + 1)
                    sp.dma_start(out_rows[g * G * HD:(g + 1) * G * HD, t * P:(t + 1) * P].rearrange("(h d) s -> d h s", d=HD),
                                 out[:, g, :, :]).then_inc(stored[g], 16)

            for t in range(NT):
                tok = slice(t * P, (t + 1) * P)
                for k, c, buf in ((0, C_QI, rot), (1, C_QA, rot2)):
                    if t:
                        sp.wait_ge(q_lod[k], t)
                    load_rotated(sp, buf[:, 0], buf[:, 1], heads_of(c, 8, tok), q_in[k])
                if t:
                    store(t - 1)
            store(NT - 1)
            for g in range(KV_HEADS):
                sp.wait_ge(stored[g], 16 * NT)

        @block.gpsimd
        def _(pool):
            nc.gpsimd.memset(ones[:, :], 1.0).then_inc(const_set, 1)
            pool.wait_ge(const_in, 64)
            for n, (k, a) in enumerate(key_steps):
                pool.wait_ge(key_in, 96 * (n + 1))
                nc.gpsimd.tensor_tensor(flat(rot, 0), flat(rot, 0), cosT[:, a:a + KP], ALU.mult).then_inc(key_rot, 1)
                nc.gpsimd.tensor_tensor(flat(rot, 1), flat(rot, 1), sinT[:, a:a + KP], ALU.mult).then_inc(key_rot, 1)
                pool.wait_ge(key_rot, 3 * n + 2)
                nc.gpsimd.tensor_tensor(flat(rot, 0), flat(rot, 0), flat(rot, 1), ALU.add).then_inc(key_rot, 1)
                pool.wait_ge(key_tmp, n + 1)
                up = keys[HD:P, k, a:a + KP]
                nc.gpsimd.tensor_tensor(up, flat(rot, 0)[HD:P], up.bitcast(fp32), ALU.subtract).then_inc(key_done, 1)

            def rotate(k, t):
                buf = (rot, rot2)[k]
                table = lambda m: m[:, t * P:(t + 1) * P].unsqueeze(1).to_broadcast([P, 8, P])
                if t == 0:
                    pool.wait_ge(key_done, len(key_steps))
                pool.wait_ge(q_in[k], 96 * (t + 1))
                nc.gpsimd.tensor_tensor(buf[:, 0], buf[:, 0], table(cosT), ALU.mult).then_inc(q_mul[k], 1)
                nc.gpsimd.tensor_tensor(buf[:, 1], buf[:, 1], table(sinT), ALU.mult).then_inc(q_mul[k], 1)
                pool.wait_ge(q_mul[k], 2 * (t + 1))
                nc.gpsimd.tensor_tensor(buf[:, 0], buf[:, 0], buf[:, 1], ALU.add).then_inc(q_rot[k], 1)
                pool.wait_ge(q_hid[k], t + 1)
                wait_q_used(pool, k, t)
                nc.gpsimd.tensor_tensor(q_lo[k][:, :, :], buf[:, 0], q_hi[k][:, :, :].bitcast(fp32),
                                        ALU.subtract).then_inc(q_lod[k], 1)

            rotate(0, 0)
            rotate(1, 0)
            for t in range(NT):
                if t + 1 < NT:
                    rotate(0, t + 1)
                    rotate(1, t + 1)
                for g in range(KV_HEADS):
                    pool.wait_ge(rinv_done, KV_HEADS * t + g + 1)
                    if t or g:
                        pool.wait_ge(o_done, KV_HEADS * t + g)
                    nc.gpsimd.tensor_tensor(diag[:, :, :], ident[:, :].unsqueeze(1).to_broadcast([P, G, P]),
                                            rinv[:, g * G:(g + 1) * G].unsqueeze(2).to_broadcast([P, G, P]),
                                            ALU.mult).then_inc(diag_done, 1)

        @block.scalar
        def _(act):
            for n, (k, a) in enumerate(key_steps):
                act.wait_ge(key_rot, 3 * (n + 1))
                nc.scalar.activation(keys[:, k, a:a + KP], flat(rot, 0), ACT.Copy).then_inc(key_tmp, 1)
            act.wait_ge(w_T, 1)
            nc.scalar.activation(w_idx[:, :, :].rearrange("p a b -> p (a b)"), ps[:, 7, 0:NT * IDX_HEADS], ACT.Copy,
                                 scale=float((IDX_HEADS * HD) ** -0.5)).then_inc(w_done, 1)
            for n in range(NT // 4):
                act.wait_ge(v_T, n + 1)
                nc.scalar.activation(vals[:, 4 * n:4 * n + 4, :].rearrange("p a b -> p (a b)"), ps[:, 4 + n % 2, :],
                                     ACT.Copy).then_inc(v_done, 1)
            def round_q(k, t):
                act.wait_ge(q_rot[k], t + 1)
                wait_q_used(act, k, t)
                nc.scalar.activation(q_hi[k][:, :, :], (rot, rot2)[k][:, 0], ACT.Copy).then_inc(q_hid[k], 1)

            def index_relu(t):
                for it in of_tile("idx", t):
                    a, w = pieces(t)[it[3]]
                    act.wait_ge(idx_done, number[it])
                    if number[it] > 2:
                        act.wait_ge(acc_done, number[it] - 2)
                    nc.scalar.activation(relu[:, number[it] % 2, 0:w], slot_ps(place[it], w), ACT.Relu).then_inc(relu_done, 1)

            n_pT = 0
            round_q(0, 0)
            round_q(1, 0)
            index_relu(0)
            for t in range(NT):
                N = (t + 1) * P
                if t + 1 < NT:
                    round_q(0, t + 1)
                for g in range(KV_HEADS):
                    act.wait_ge(max_done, KV_HEADS * t + g + 1)
                    for h in range(g * G, (g + 1) * G):
                        nc.scalar.activation(prob[:, h, 0:N], prob[:, h, 0:N], ACT.Exp, bias=nmx[:, h:h + 1],
                                             scale=HD ** -0.5, accum_out=rsum[:, h:h + 1]).then_inc(exp_done, 1)
                if t + 1 < NT:
                    index_relu(t + 1)
                    round_q(1, t + 1)
                for g in range(KV_HEADS):
                    for c in range(t + 1):
                        n_pT += 1
                        act.wait_ge(pT_done, n_pT)
                        nc.scalar.activation(pT[:, n_pT % 2, :], ps[:, 4 + n_pT % 2, :], ACT.Copy).then_inc(pT_evac, 1)
                    act.wait_ge(o_done, KV_HEADS * t + g + 1)
                    if t:
                        act.wait_ge(norm_done, KV_HEADS * (t - 1) + g + 1)
                    nc.scalar.activation(rb[:, g, :], ps[HD:P, 6 + g, :], ACT.Copy).then_inc(rb_done, 1)

        @block.vector
        def _(dve):
            st = Steps(dve, dve_s)
            dve.wait_ge(w_done, 1)
            dve.wait_ge(const_in, 64)

            def index_scores(t):
                for it in of_tile("idx", t):
                    _, _, h, p = it
                    a, w = pieces(t)[p]
                    n = number[it]
                    dve.wait_ge(relu_done, n)
                    if h == 0:
                        nc.vector.tensor_scalar(score[:, a:a + w], relu[:, n % 2, 0:w], w_idx[:, t, h:h + 1], None,
                                                ALU.mult).then_inc(acc_done, 1)
                    else:
                        dve.wait_ge(acc_done, n - len(pieces(t)))
                        nc.vector.scalar_tensor_tensor(out=score[:, a:a + w], in0=relu[:, n % 2, 0:w],
                                                       scalar=w_idx[:, t, h:h + 1], in1=score[:, a:a + w],
                                                       op0=ALU.mult, op1=ALU.add).then_inc(acc_done, 1)

            def select(t):
                N = (t + 1) * P
                if t not in selects:
                    st.do(nc.vector.memset(bias[:, 0:N], 0.0))
                    st.do(nc.vector.memset(bias[0:CHUNK, N - CHUNK:N], MASK_BIAS))
                    return
                sc, m, junk = score[:, 0:N], left[:, 0:N], bias[:, 0:N]
                dve.wait_ge(acc_done, number[of_tile("idx", t)[-1]])
                st.do(nc.vector.memset(score[0:CHUNK, N - CHUNK:N], BARRED))
                st.do(nc.vector.tensor_scalar(junk, sc, 0.0, None, ALU.is_ge, ALU.add, accum_out=count[:, :]))
                st.do(nc.vector.tensor_scalar(bound[:, :], count[:, :], float(topk), None, ALU.is_ge))
                nc.vector.tensor_scalar(sign[:, :], bound[:, :], 2.0, -1.0, ALU.mult, ALU.add)
                st.do(nc.vector.tensor_scalar(bound[:, :], bound[:, :], float(2 * topk - N - 1), float(N - topk + 1),
                                              ALU.mult, ALU.add))
                st.do(nc.vector.memset(trial[:, :], 2 ** (BITS - 1)))
                st.do(nc.vector.tensor_scalar(m, sc, sign[:, 0:1], None, ALU.mult))
                for k in range(BITS - 1, -1, -1):
                    st.do(nc.vector.tensor_scalar(junk, m, trial[:, 0:1].bitcast(fp32), None, ALU.is_ge, ALU.add,
                                                  accum_out=count[:, :]))
                    st.do(nc.vector.tensor_scalar(drop[:, :], count[:, :], bound[:, 0:1], float(2 ** k), ALU.is_lt, ALU.mult))
                    st.do(nc.vector.scalar_tensor_tensor(out=trial[:, :], in0=drop[:, :], scalar=2 ** k // 2, in1=trial[:, :],
                                                         op0=ALU.bitwise_or, op1=ALU.bitwise_xor))
                st.do(nc.vector.tensor_scalar(value[:, :], trial[:, 0:1].bitcast(fp32), sign[:, 0:1], None, ALU.mult))
                st.do(nc.vector.tensor_scalar(junk, sc, value[:, 0:1], None, ALU.is_gt, ALU.add, accum_out=count[:, :]))
                nc.vector.tensor_scalar(room[:, :], count[:, :], -1.0, float(topk), ALU.mult, ALU.add)
                st.do(nc.vector.tensor_scalar(m, sc, value[:, 0:1], None, ALU.is_equal))
                st.do(nc.vector.tensor_tensor_scan(bias[:, 0:N], m, m, 0.0, ALU.add, ALU.bypass))
                st.do(nc.vector.scalar_tensor_tensor(out=m, in0=bias[:, 0:N], scalar=room[:, 0:1], in1=m,
                                                     op0=ALU.is_gt, op1=ALU.mult))
                st.do(nc.vector.scalar_tensor_tensor(out=m, in0=sc, scalar=value[:, 0:1], in1=m, op0=ALU.is_lt, op1=ALU.add))
                st.do(nc.vector.tensor_scalar(bias[:, 0:N], m, MASK_BIAS, None, ALU.mult))

            index_scores(0)
            select(0)
            for t in range(NT):
                for g in range(KV_HEADS):
                    hs = slice(g * G, (g + 1) * G)
                    if t:
                        dve.wait_ge(pT_done, chunks_before(t - 1) + (g + 1) * t)
                    for h in range(g * G, (g + 1) * G):
                        for p, (a, w) in enumerate(pieces(t)):
                            it = ("att", t, h, p)
                            dve.wait_ge(att_done, number[it])
                            nc.vector.tensor_tensor_reduce(out=prob[:, h, a:a + w], in0=slot_ps(place[it], w), in1=bias[:, a:a + w],
                                                           scale=1.0, scalar=-3.0e38, op0=ALU.add, op1=ALU.max,
                                                           accum_out=mx[:, p, h:h + 1]).then_inc(masked, 1)
                    dve.wait_ge(masked, number[it])
                    if len(pieces(t)) == 2:
                        st.do(nc.vector.tensor_tensor(mx[:, 0, hs], mx[:, 0, hs], mx[:, 1, hs], ALU.max))
                    nc.vector.tensor_scalar(nmx[:, hs], mx[:, 0, hs], -HD ** -0.5, None, ALU.mult).then_inc(max_done, 1)
                if t + 1 < NT:
                    index_scores(t + 1)
                for g in range(KV_HEADS):
                    hs = slice(g * G, (g + 1) * G)
                    dve.wait_ge(exp_done, A_HEADS * t + (g + 1) * G)
                    if t:
                        dve.wait_ge(diag_done, KV_HEADS * (t - 1) + g + 1)
                    nc.vector.reciprocal(rinv[:, hs], rsum[:, hs]).then_inc(rinv_done, 1)
                if t + 1 < NT:
                    select(t + 1)
                for g in range(KV_HEADS):
                    n = KV_HEADS * t + g
                    dve.wait_ge(rb_done, n + 1)
                    if t:
                        dve.wait_ge(stored[g], 16 * t)
                    nc.vector.tensor_tensor(out[:, g, :, :].rearrange("p a b -> p (a b)"), ps[0:HD, 6 + g, :], rb[:, g, :],
                                            ALU.mult).then_inc(norm_done, 1)

        @block.tensor
        def _(pe):
            pe.wait_ge(const_set, 1)
            pe.wait_ge(const_in, 64)
            for t in range(NT):
                last = nc.tensor.transpose(ps[:, 7, t * IDX_HEADS:(t + 1) * IDX_HEADS], small[:, t * P:(t + 1) * P],
                                           ident[0:IDX_HEADS, 0:IDX_HEADS])
            last.then_inc(w_T, 1)
            pe.wait_ge(v_in, 16)
            for n in range(NT // 4):
                if n >= 2:
                    pe.wait_ge(v_done, n - 1)
                for j in range(4):
                    c = 4 * n + j
                    last = nc.tensor.transpose(ps[:, 4 + n % 2, j * P:(j + 1) * P], prob[:, 0, c * P:(c + 1) * P], ident[:, :])
                last.then_inc(v_T, 1)
            pe.wait_ge(key_done, len(key_steps))
            pe.wait_ge(v_done, NT // 4)
            pe.wait_ge(w_done, 1)

            def scores(kind, t):
                k = 0 if kind == "idx" else 1
                pe.wait_ge(q_lod[k], t + 1)
                for h in range(8):
                    ks = keys[:, 0 if k == 0 else 1 + h // G, :]
                    for p, (a, w) in enumerate(pieces(t)):
                        n = place[kind, t, h, p]
                        if n >= 2:
                            before = items[n - 2]
                            pe.wait_ge(relu_done if before[0] == "idx" else masked, number[before])
                        for x in range(0, w, 512):
                            y = min(512, w - x)
                            dst = slot_ps(n, w)[:, x:x + y]
                            nc.tensor.matmul(dst, q_hi[k][:, h, :], ks[:, a + x:a + x + y], start=True, stop=False)
                            last = nc.tensor.matmul(dst, q_lo[k][:, h, :], ks[:, a + x:a + x + y], start=False, stop=True)
                        last.then_inc(idx_done if k == 0 else att_done, 1)

            n_pT = 0
            if 0 in selects:
                scores("idx", 0)
            for t in range(NT):
                scores("att", t)
                if t + 1 in selects:
                    scores("idx", t + 1)
                for g in range(KV_HEADS):
                    pe.wait_ge(exp_done, A_HEADS * t + (g + 1) * G)
                    if t:
                        pe.wait_ge(norm_done, KV_HEADS * (t - 1) + g + 1)

                    def transpose(c):
                        n = n_pT + c + 1
                        if n > 2:
                            pe.wait_ge(pT_evac, n - 2)
                        for j in range(G):
                            last = nc.tensor.transpose(ps[:, 4 + n % 2, j * P:(j + 1) * P], prob[:, g * G + j, c * P:(c + 1) * P],
                                                       ident[:, :])
                        last.then_inc(pT_done, 1)

                    transpose(0)
                    for c in range(t + 1):
                        if c < t:
                            transpose(c + 1)
                        n = n_pT + c + 1
                        pe.wait_ge(pT_evac, n)
                        nc.tensor.matmul(ps[0:HD, 6 + g, :], vals[:, c, g * HD:(g + 1) * HD], pT[:, n % 2, :],
                                         start=(c == 0), stop=(c == t))
                    n_pT += t + 1
                    pe.wait_ge(diag_done, KV_HEADS * t + g + 1)
                    nc.tensor.matmul(ps[HD:P, 6 + g, :], ones[:, 0:HD], diag[:, :, :].rearrange("p a b -> p (a b)"),
                                     start=True, stop=True).then_inc(o_done, 1)



def output_and_mlp(nc, S, xT, mixT, w_units, g_ffn, g_final, outT):
    TB, NB, NG, U = 512, S // 512, D_FF // 512, 4
    SEGS, UNITS = 2 + 2 * NG, 4 * (2 + 2 * NG)
    F_BLK, Y_BLK = 2 * U + NG * U, NG * KC
    with ExitStack() as ctx:
        sb = lambda n, s, d=fp32: ctx.enter_context(nc.sbuf_tensor(n, s, d))
        sem = lambda n: ctx.enter_context(nc.semaphore(n))
        ones, eps_col = sb("f_ones", [P, P]), sb("f_eps", [P, 1])
        gf, gl = sb("f_gf", [P, KC]), sb("f_gl", [P, KC])
        raw = sb("f_raw", [P, U, KC, P])
        wh = sb("f_wh", [P, 2 * U, KC, P], f32r)
        wl = sb("f_wl", [P, 2 * U, KC, P], f32r)
        tmp = sb("f_tmp", [P, KC, TB])
        acc = sb("f_acc", [P, KC, TB])
        ah = sb("f_ah", [P, KC, TB], f32r)
        al = sb("f_al", [P, KC, TB], f32r)
        th = sb("f_th", [P, 2, U, TB], f32r)
        tl = sb("f_tl", [P, 2, U, TB], f32r)
        rl = sb("f_rl", [P, 2, TB])
        r2 = sb("f_r2", [P, 2, TB])
        rstd = sb("f_rstd", [P, TB])
        ps = ctx.enter_context(nc.psum_tensor("f_ps", [P, 8, TB], fp32))
        (const_in, const_set, mix_in, x_in, mh_done, ml_done, x_done, sq_done, ss_done, std_done, h_done, hh_done, hl_done,
         f_done, y_done, y_add, r_done, th_done, r2_done, tl_done, out_done, stored, w_hi, w_lo, dve_s) = map(
            sem, ["f_" + n for n in ("const_in const_set mix_in x_in mh_done ml_done x_done sq_done ss_done std_done h_done "
                                     "hh_done hl_done f_done y_done y_add r_done th_done r2_done tl_done out_done stored "
                                     "w_hi w_lo dve").split()])
        raw_in = [sem(f"f_raw_in{n}") for n in range(U)]
        Y0, R0, SS0 = 2 * KC, 1, 1
        block = ctx.enter_context(nc.Block())

        def segments(eng, b, body):
            body("O", 0, 0, 0, 0, ("O", 1, 1))
            body("O", 1, 0, 1, 1, ("W1", 0, 2))
            body("W1", 0, 0, 2, 0, ("W1", 1, 3))
            with eng.Fori(0, (NG - 2) // 2) as j:
                for v in range(2):
                    g = 2 * j + (v + 1)
                    body("W1", g, (v + 1) % 2, 2 * g + 1, 1, ("W2", g - 1, 2 * g + 2))
                    body("W2", g - 1, v % 2, 2 * g + 2, 0, ("W1", g + 1, 2 * g + 3))
            g = NG - 1
            body("W1", g, g % 2, 2 * g + 1, 1, ("W2", g - 1, 2 * g + 2))
            body("W2", g - 1, (g - 1) % 2, 2 * g + 2, 0, ("W2", g, 2 * g + 3))
            body("W2", g, g % 2, 2 * g + 3, 1, None)

        def tokens(b):
            return bass.ds(b * TB, TB)

        @block.sync
        def _(sp):
            sp.dma_start(gf[:, :], g_ffn).then_inc(const_in, 16)
            sp.dma_start(gl[:, :], g_final).then_inc(const_in, 16)
            sp.sem_inc(w_lo, U)
            sp.sem_inc(stored, 16)
            with sp.Fori(0, NB) as b:
                def unit(k, n):
                    sp.wait_ge(w_lo, UNITS * b + n + 1)
                    sp.dma_start(raw[:, k, :, :].rearrange("p a b -> p (a b)"),
                                 w_units[bass.ds(n, 1)].rearrange("a p n -> p (a n)")).then_inc(raw_in[k], 16)

                sp.wait_ge(ss_done, 2 * b + SS0)
                sp.dma_start(tmp[:, :, :], mixT[:, :, tokens(b)].rearrange("c p s -> p c s")).then_inc(mix_in, 16)
                sp.wait_ge(stored, 16 * b + 16)
                sp.dma_start(acc[:, :, :], xT[:, :, tokens(b)]).then_inc(x_in, 16)
                with sp.Fori(0, UNITS // U) as j:
                    for k in range(U):
                        unit(k, U * j + k)
                sp.wait_ge(out_done, KC * b + KC)
                sp.dma_start(outT[:, :, tokens(b)].rearrange("c p s -> p c s"), acc[:, :, :]).then_inc(stored, 16)
            sp.wait_ge(stored, 16 * NB + 16)

        @block.gpsimd
        def _(pool):
            nc.gpsimd.memset(ones[:, :], 1.0).then_inc(const_set, 1)
            nc.gpsimd.memset(eps_col[:, :], EPS).then_inc(const_set, 1)
            with pool.Fori(0, NB * UNITS // (2 * U)) as i:
                for s in range(2 * U):
                    pool.wait_ge(w_hi, 2 * U * i + s + 1)
                    nc.gpsimd.tensor_tensor(wl[:, s, :, :], raw[:, s % U, :, :], wh[:, s, :, :].bitcast(fp32),
                                            ALU.subtract).then_inc(w_lo, 1)

        @block.scalar
        def _(act):
            act.sem_inc(r_done, R0)
            act.wait_ge(const_set, 2)
            with act.Fori(0, NB) as b:
                def done(kind, g):
                    if kind == "W2":
                        act.wait_ge(y_done, Y_BLK * b + KC * g + KC + Y0)
                    else:
                        act.wait_ge(f_done, F_BLK * b + U * g + U + (2 * U if kind == "W1" else 0))

                def split(seg, half, s):
                    act.wait_ge(raw_in[s], 16 * (SEGS * b + seg) + 16)
                    nc.scalar.activation(wh[:, U * half + s, :, :], raw[:, s, :, :], ACT.Copy).then_inc(w_hi, 1)

                def normalise(second, h_out):
                    for k in range(KC):
                        if second:
                            act.wait_ge(y_add, Y_BLK * b + Y_BLK - KC + k + 1 + 4)
                        else:
                            act.wait_ge(x_done, KC * b + k + 1)
                        if k == 0 and second:
                            act.wait_ge(hl_done, KC * b + KC)
                        if k == 0 and not second:
                            act.wait_ge(ml_done, KC * b + KC)
                        nc.scalar.activation(tmp[:, k, :], acc[:, k, :], ACT.Square).then_inc(sq_done, 1)
                    act.wait_ge(ss_done, 2 * b + (2 if second else 1) + SS0)
                    nc.scalar.activation(rstd[:, :], ps[:, 6, :], ACT.Sqrt, scale=1.0 / D_MODEL,
                                         bias=eps_col[:, :]).then_inc(std_done, 1)
                    if not second:
                        for k in range(KC):
                            act.wait_ge(h_done, KC * b + k + 1)
                            nc.scalar.activation(ah[:, k, :], tmp[:, k, :], ACT.Copy).then_inc(hh_done, 1)

                act.wait_ge(y_done, Y_BLK * b + Y0)
                for s in range(U):
                    split(0, 0, s)
                act.wait_ge(mix_in, 16 * b + 16)
                for k in range(KC):
                    nc.scalar.activation(ah[:, k, :], tmp[:, k, :], ACT.Copy).then_inc(mh_done, 1)

                def segment(kind, g, par, seg, half, nxt):
                    for s in range(U):
                        if nxt:
                            if s == 0 and not (kind == "O" and g == 0):
                                before = {"O": ("O", 0), "W2": ("W1", g + 1)}.get(kind)
                                if kind == "W1":
                                    before = ("O", 1) if isinstance(seg, int) and seg == 2 else ("W2", g - 2)
                                if kind == "W1" and not (isinstance(seg, int) and seg == 2):
                                    act.wait_ge(y_done, Y_BLK * b + KC * g - KC + Y0)
                                    act.wait_ge(f_done, F_BLK * b + 3 * U)
                                else:
                                    done(*before)
                            split(nxt[2], 1 - half, s)
                        if kind == "W1":
                            n = U * g + s
                            act.wait_ge(f_done, F_BLK * b + 2 * U + n + 1)
                            act.wait_ge(tl_done, UW * b + n + 1)
                            nc.scalar.activation(rl[:, s % 2, :], ps[:, s % 2, :], ACT.Relu).then_inc(r_done, 1)
                            act.wait_ge(r_done, UW * b + n + 1 + R0)
                            act.wait_ge(y_done, Y_BLK * b + KC * g - KC + Y0)
                            nc.scalar.activation(th[:, par, s, :], rl[:, s % 2, :], ACT.Square).then_inc(th_done, 1)
                    if isinstance(seg, int) and seg == 1:
                        normalise(False, None)

                UW = NG * U
                segments(act, b, segment)
                normalise(True, None)

        @block.vector
        def _(dve):
            st = Steps(dve, dve_s)
            UW = NG * U
            dve.sem_inc(tl_done, 2)
            dve.sem_inc(y_add, 4)
            dve.wait_ge(const_in, 32)
            with dve.Fori(0, NB) as b:
                st.loop(0, b, 2)
                for k in range(KC):
                    dve.wait_ge(mh_done, KC * b + k + 1)
                    nc.vector.tensor_tensor(al[:, k, :], tmp[:, k, :], ah[:, k, :].bitcast(fp32), ALU.subtract).then_inc(ml_done, 1)

                def segment(kind, g, par, seg, half, nxt):
                    if kind == "O":
                        for s in range(U):
                            k = U * g + s
                            if k == 0:
                                dve.wait_ge(x_in, 16 * b + 16)
                            dve.wait_ge(f_done, F_BLK * b + k + 1)
                            nc.vector.tensor_tensor(acc[:, k, :], acc[:, k, :], ps[:, s % 2, :], ALU.add).then_inc(x_done, 1)
                        if g == 1:
                            dve.wait_ge(std_done, 2 * b + 1)
                            st.do(nc.vector.reciprocal(rstd[:, :], rstd[:, :]))
                            for k in range(KC):
                                nc.vector.scalar_tensor_tensor(out=tmp[:, k, :], in0=acc[:, k, :], scalar=gf[:, k:k + 1],
                                                               in1=rstd[:, :], op0=ALU.mult, op1=ALU.mult).then_inc(h_done, 1)
                            for k in range(KC):
                                dve.wait_ge(hh_done, KC * b + k + 1)
                                nc.vector.tensor_tensor(al[:, k, :], tmp[:, k, :], ah[:, k, :].bitcast(fp32),
                                                        ALU.subtract).then_inc(hl_done, 1)
                    elif kind == "W1":
                        for s in range(U):
                            n = U * g + s
                            dve.wait_ge(r_done, UW * b + n + 1 + R0)
                            nc.vector.tensor_tensor(r2[:, s % 2, :], rl[:, s % 2, :], rl[:, s % 2, :], ALU.mult).then_inc(r2_done, 1)
                            dve.wait_ge(th_done, UW * b + n + 1)
                            dve.wait_ge(r2_done, UW * b + n + 1)
                            nc.vector.tensor_tensor(tl[:, par, s, :], r2[:, s % 2, :], th[:, par, s, :].bitcast(fp32),
                                                    ALU.subtract).then_inc(tl_done, 1)
                    else:
                        for k in range(KC):
                            dve.wait_ge(y_done, Y_BLK * b + KC * g + k + 1 + Y0)
                            nc.vector.tensor_tensor(acc[:, k, :], acc[:, k, :], ps[:, 2 + k % 4, :], ALU.add).then_inc(y_add, 1)

                segments(dve, b, segment)
                dve.wait_ge(std_done, 2 * b + 2)
                st.do(nc.vector.reciprocal(rstd[:, :], rstd[:, :]))
                for k in range(KC):
                    nc.vector.scalar_tensor_tensor(out=acc[:, k, :], in0=acc[:, k, :], scalar=gl[:, k:k + 1],
                                                   in1=rstd[:, :], op0=ALU.mult, op1=ALU.mult).then_inc(out_done, 1)
            st.leave(NB)

        @block.tensor
        def _(pe):
            UW = NG * U
            pe.sem_inc(y_done, Y0)
            pe.sem_inc(ss_done, SS0)
            pe.wait_ge(const_set, 2)
            with pe.Fori(0, NB) as b:
                def sum_squares(first):
                    for k in range(KC):
                        pe.wait_ge(sq_done, 2 * KC * b + k + 1 + (0 if first else KC))
                        last = nc.tensor.matmul(ps[:, 6, :], ones[:, :], tmp[:, k, :], start=(k == 0), stop=(k == KC - 1))
                    last.then_inc(ss_done, 1)

                def three(dst, hi, lo, rh, rl_, first, last):
                    nc.tensor.matmul(dst, hi, rh, start=first, stop=False)
                    nc.tensor.matmul(dst, hi, rl_, start=False, stop=False)
                    return nc.tensor.matmul(dst, lo, rh, start=False, stop=last)

                def segment(kind, g, par, seg, half, nxt):
                    if kind != "W2":
                        for s in range(U):
                            pe.wait_ge(w_lo, UNITS * b + U * seg + s + 1 + U)
                            if kind == "O":
                                if g == 0 and s == 0:
                                    pe.wait_ge(r_done, UW * b + R0)
                                    pe.wait_ge(ml_done, KC * b + KC)
                                if g or s >= 2:
                                    pe.wait_ge(x_done, KC * b + U * g + s - 1)
                            elif isinstance(seg, int) and seg == 2 and s < 2:
                                pe.wait_ge(x_done, KC * b + KC)
                                pe.wait_ge(hl_done, KC * b + KC)
                            else:
                                pe.wait_ge(r_done, UW * b + U * g + s - 1 + R0)
                            for k in range(KC):
                                last = three(ps[:, s % 2, :], wh[:, U * half + s, k, :], wl[:, U * half + s, k, :],
                                             ah[:, k, :], al[:, k, :], k == 0, k == KC - 1)
                            last.then_inc(f_done, 1)
                        if isinstance(seg, int) and seg == 1:
                            sum_squares(True)
                    else:
                        pe.wait_ge(w_lo, UNITS * b + U * seg + U + U)
                        pe.wait_ge(tl_done, UW * b + U * g + U + 2)
                        for k in range(KC):
                            pe.wait_ge(y_add, Y_BLK * b + KC * g + k + 1)
                            for s in range(U):
                                last = three(ps[:, 2 + k % 4, :], wh[:, U * half + s, k, :], wl[:, U * half + s, k, :],
                                             th[:, par, s, :], tl[:, par, s, :], s == 0, s == U - 1)
                            last.then_inc(y_done, 1)

                segments(pe, b, segment)
                sum_squares(False)


def program(nc, S, a, projT, mixT, outT):
    norm_and_projection(nc, S, a["xT"], a["g_mix"], a["conv_w"], a["w_proj"], projT)
    gated_deltanet(nc, S, projT, a["a_log"], a["dt_bias"], a["g_gdn"], a, mixT)
    indexed_attention(nc, S, min(TOPK_MAX, S // 4), projT, a, mixT)
    output_and_mlp(nc, S, a["xT"], mixT, a["w_units"], a["g_ffn"], a["g_final"], outT)


def shape_constants(S):
    i = np.arange(P)
    f = lambda m: np.ascontiguousarray(m.astype(np.float32))
    same = (i[:, None] // 16) == (i[None, :] // 16)
    half = HD // 2
    inv = (1.0 / (np.float32(10000.0) ** (np.arange(half, dtype=np.float32) / np.float32(half)))).astype(np.float32)
    ang = np.arange(S, dtype=np.float32)[None, :] * inv[i % half][:, None]
    sign = np.where(i % HD < half, -1.0, 1.0).astype(np.float32)[:, None]
    return {
        "ident": f(np.eye(P)), "triu": f(i[:, None] <= i[None, :]), "incl": f(i[:, None] >= i[None, :]),
        "strict": f(i[:, None] > i[None, :]), "diag16": f(same), "off16": f(~same),
        "cosT": f(np.cos(ang)), "sinT": f(np.sin(ang) * sign),
    }


def proj_columns():
    sizes = [A_HEADS * HD, KV_HEADS * HD, KV_HEADS * HD, IDX_HEADS * HD, HD, IDX_HEADS] + [B_HEADS * BD] * 4 + [B_HEADS] * 2
    off = np.concatenate([[0], np.cumsum(sizes)])
    qa, ka, va, qi, ki, wi, qb, kb, vb, zb, bb, ab = [list(range(off[n], off[n + 1])) for n in range(len(sizes))]
    small = wi + bb + ab
    return small + [-1] * (P - HD - len(small)) + ki + qi + qa + ka + va + qb + kb + vb + zb


def weight_units(w_out, w_ff1, w_ff2):
    by_output = lambda w: w.reshape(KC, P, -1, P).transpose(2, 1, 0, 3).reshape(-1, P, KC * P)
    o, w1 = by_output(w_out), by_output(w_ff1)
    w2 = w_ff2.reshape(-1, P, D_MODEL)
    n = D_FF // 512
    part = lambda w, g: w[4 * g:4 * g + 4]
    seq = [o, part(w1, 0)]
    for g in range(1, n):
        seq += [part(w1, g), part(w2, g - 1)]
    return np.ascontiguousarray(np.concatenate(seq + [part(w2, n - 1)]))


def host_layout(d):
    x = d["x"][0]
    S = x.shape[0]
    cols = np.array(proj_columns())
    w = np.zeros((D_MODEL, (N_CHUNK + 1) * P), np.float32)
    w[:, :len(cols)] = np.where(cols >= 0, d["w_in"][0][:, cols], np.float32(0))
    chunks = lambda a: np.ascontiguousarray(a.reshape(KC, P, -1, P).transpose(2, 1, 0, 3))
    col = lambda g: np.ascontiguousarray(g.reshape(-1, P).T)
    return {
        "xT": np.ascontiguousarray(x.T.reshape(KC, P, S).transpose(1, 0, 2)),
        "g_mix": col(d["norm_mix_g"][0]),
        "conv_w": np.ascontiguousarray(d["conv_w"][0].reshape(CONV, N_CONV, P).transpose(2, 1, 0)),
        "w_proj": chunks(w),
        "w_units": weight_units(d["w_out"][0], d["w_ff1"][0], d["w_ff2"][0]),
        "g_ffn": col(d["norm_ffn_g"][0]), "g_final": col(d["norm_final_g"]),
        "a_log": d["a_log"][0:1], "dt_bias": d["dt_bias"][0:1], "g_gdn": col(d["gdn_norm_g"][0]),
    }


_OUT = "out_dram"


def kernel(**inputs):
    import concourse.bacc as bacc
    from concourse.bass_utils import run_bass_kernel_spmd

    d = {k: np.asarray(v) for k, v in inputs.items()}
    S = d["x"].shape[1]
    arrays = {**host_layout(d), **shape_constants(S)}
    arrays = {k: np.ascontiguousarray(v) for k, v in arrays.items()}
    nc = bacc.Bacc("TRN2", target_bir_lowering=False, num_devices=1)
    a = {n: nc.dram_tensor(n, v.shape, fp32, kind="ExternalInput").ap() for n, v in arrays.items()}
    projT = nc.dram_tensor("projT", (N_CHUNK, P, S), fp32, kind="Internal").ap()
    mixT = nc.dram_tensor("mixT", (KC, P, S), fp32, kind="Internal").ap()
    outT = nc.dram_tensor(_OUT, (KC, P, S), fp32, kind="ExternalOutput").ap()
    program(nc, S, a, projT, mixT, outT)
    r = run_bass_kernel_spmd(nc, [arrays], core_ids=[0])
    out = r.results[0][_OUT].reshape(D_MODEL, S)
    return np.ascontiguousarray(out.T)[None]
```

```python
import numpy as np
import concourse.bass as bass
from concourse import mybir
from contextlib import ExitStack

fp32 = mybir.dt.float32
f32r = mybir.dt.float32r
i32 = mybir.dt.int32
ALU = mybir.AluOpType
ACT = mybir.ActivationFunctionType

P = 128
D_MODEL, D_FF = 1024, 4096
KC = D_MODEL // P
A_HEADS, KV_HEADS, HD = 8, 2, 64
IDX_HEADS = 8
B_HEADS, BD = 4, 128
CONV = 4
TOPK_MAX, CHUNK = 256, 64
EPS = 1e-6
C_SMALL, C_QI, C_QA, C_KA, C_VA, C_CONV, C_Z, N_CHUNK = 0, 1, 5, 9, 10, 11, 23, 27
N_CONV = C_Z - C_CONV
HALO = 4
BARRED = -2.0e38
MASK_BIAS = -1.0e38


class Steps:

    def __init__(self, eng, sem):
        self.eng, self.sem, self.base, self.n = eng, sem, 0, 0

    def do(self, ins):
        ins.then_inc(self.sem, 1)
        self.n += 1
        self.eng.wait_ge(self.sem, self.base + self.n)

    def loop(self, done, i, per):
        self.base, self.n, self.at = i * per + done, 0, (done, per)

    def leave(self, turns):
        done, per = self.at
        assert self.n == per, self.n
        self.base, self.n = 0, done + per * turns


def norm_and_projection(nc, S, xT, g_mix, conv_w, w_proj, projT):
    XB = 256
    NX, NB = S // XB, S // 512
    with ExitStack() as ctx:
        sb = lambda n, s, d=fp32: ctx.enter_context(nc.sbuf_tensor(n, s, d))
        sem = lambda n: ctx.enter_context(nc.semaphore(n))
        xh = sb("xh", [P, KC, S], f32r)
        xl = sb("xl", [P, KC, S], f32r)
        work = sb("work", [P, 8192])
        xb = work[:, 0:4096].rearrange("p (u k s) -> p u k s", u=2, k=KC)
        xsq = work[:, 4096:6144].rearrange("p (k s) -> p k s", k=KC)
        xn = work[:, 6144:8192].rearrange("p (k s) -> p k s", k=KC)
        conv_acc = work[:, 0:2 * S].rearrange("p (u s) -> p u s", u=2)
        conv_out = work[:, 2 * S:4 * S].rearrange("p (u s) -> p u s", u=2)
        rstd = sb("rstd", [P, XB])
        ones = sb("ones", [P, P])
        gm = sb("gm", [P, KC])
        eps_col = sb("eps_col", [P, 1])
        cw = sb("cw", [P, N_CONV, CONV])
        wraw = sb("wraw", [P, 2, KC, P])
        wh = sb("wh", [P, 2, KC, P], f32r)
        wl = sb("wl", [P, 2, KC, P], f32r)
        stage = sb("stage", [P, 2, HALO + S])
        ps = ctx.enter_context(nc.psum_tensor("ps", [P, 8, 512], fp32))
        const_in, const_set = sem("const_in"), sem("const_set")
        pair = lambda n: [sem(f"{n}{u}") for u in range(2)]
        x_in, w_in, plain_out, conv_stored, z_out = map(pair, ["x_in", "w_in", "plain_out", "conv_stored", "z_out"])
        sq_done, ss_done, std_done, xn_done, xh_done, xl_done = map(
            sem, ["sq_done", "ss_done", "std_done", "xn_done", "xh_done", "xl_done"])
        w_hi, w_lo = map(sem, ["w_hi", "w_lo"])
        acc_done, evac_done = map(sem, ["acc_done", "evac_done"])
        conv_done, silu_done = map(sem, ["conv_done", "silu_done"])
        dve_s = sem("dve_s")
        N_PLAIN, N_Z = C_CONV, N_CHUNK - C_Z
        block = ctx.enter_context(nc.Block())

        @block.sync
        def _(sp):
            for stored in plain_out + conv_stored + z_out:
                sp.sem_inc(stored, 16)
            sp.dma_start(gm[:, :], g_mix).then_inc(const_in, 16)
            sp.dma_start(cw[:, :, :], conv_w).then_inc(const_in, 16)
            with sp.Fori(0, NX // 2) as i:
                for u in range(2):
                    sp.wait_ge(xl_done, 2 * i + u + 1)
                    sp.dma_start(xb[:, u, :, :], xT[:, :, bass.ds(i * 2 * XB + u * XB, XB)]).then_inc(x_in[u], 16)
            with sp.Fori(0, (N_CHUNK + 1) // 2) as i:
                for u in range(2):
                    sp.wait_ge(w_lo, 2 * i + u + 1)
                    sp.dma_start(wraw[:, u, :, :], w_proj[bass.ds(2 * i + u, 1)].rearrange(
                        "a p k n -> p (a k) n")).then_inc(w_in[u], 16)

        @block.gpsimd
        def _(pool):
            pool.sem_inc(w_lo, 2)
            nc.gpsimd.memset(ones[:, :], 1.0).then_inc(const_set, 1)
            nc.gpsimd.memset(stage[:, :, 0:HALO], 0.0).then_inc(const_set, 1)
            nc.gpsimd.memset(eps_col[:, :], EPS).then_inc(const_set, 1)
            with pool.Fori(0, (N_CHUNK + 1) // 2) as i:
                for u in range(2):
                    c = 2 * i + u
                    pool.wait_ge(w_hi, c + 1)
                    pool.wait_ge(acc_done, NB * c + NB)
                    nc.gpsimd.tensor_tensor(wl[:, u, :, :], wraw[:, u, :, :], wh[:, u, :, :].bitcast(fp32),
                                            ALU.subtract).then_inc(w_lo, 1)

        @block.vector
        def _(dve):
            st = Steps(dve, dve_s)
            dve.sem_inc(xl_done, 2)
            dve.wait_ge(const_in, 32)
            with dve.Fori(0, NX // 2) as i:
                st.loop(0, i, 2)
                for u in range(2):
                    b = 2 * i + u
                    tok = bass.ds(i * 2 * XB + u * XB, XB)
                    dve.wait_ge(std_done, b + 1)
                    st.do(nc.vector.reciprocal(rstd[:, :], rstd[:, :]))
                    for k in range(KC):
                        last = nc.vector.scalar_tensor_tensor(
                            out=xn[:, k, :], in0=xb[:, u, k, :], scalar=gm[:, k:k + 1], in1=rstd[:, :],
                            op0=ALU.mult, op1=ALU.mult)
                    last.then_inc(xn_done, 1)
                    dve.wait_ge(xh_done, b + 1)
                    nc.vector.tensor_tensor(xl[:, :, tok], xn[:, :, :], xh[:, :, tok].bitcast(fp32),
                                            ALU.subtract).then_inc(xl_done, 1)
                    dve.wait_ge(xl_done, b + 3)
            st.leave(NX // 2)
            done = st.n
            with dve.Fori(0, N_CONV // 2) as i:
                st.loop(done, i, 2 * (CONV - 1))
                for v in range(2):
                    k, u = 2 * i + v, (C_CONV + v) % 2
                    dve.wait_ge(evac_done, NB * k + NB * (C_CONV + 3))
                    dve.wait_ge(silu_done, k + 1)
                    st.do(nc.vector.tensor_scalar(conv_acc[:, u, :], stage[:, u, 1:1 + S],
                                                  cw[:, bass.ds(k, 1), 0:1].rearrange("p a b -> p (a b)"),
                                                  None, ALU.mult))
                    for j in range(1, CONV):
                        ins = nc.vector.scalar_tensor_tensor(
                            out=conv_acc[:, u, :], in0=stage[:, u, 1 + j:1 + j + S],
                            scalar=cw[:, bass.ds(k, 1), j:j + 1].rearrange("p a b -> p (a b)"),
                            in1=conv_acc[:, u, :], op0=ALU.mult, op1=ALU.add)
                        if j < CONV - 1:
                            st.do(ins)
                        else:
                            ins.then_inc(conv_done, 1)
            st.leave(N_CONV // 2)

        @block.scalar
        def _(act):
            act.sem_inc(evac_done, 2 * NB)
            act.sem_inc(conv_done, 2)
            act.sem_inc(silu_done, 2)
            with act.Fori(0, NX // 2) as i:
                for u in range(2):
                    b = 2 * i + u
                    act.wait_ge(x_in[u], 16 * i + 16)
                    nc.scalar.activation(xsq[:, :, :], xb[:, u, :, :], ACT.Square).then_inc(sq_done, 1)
                    act.wait_ge(ss_done, b + 1)
                    nc.scalar.activation(rstd[:, :], ps[:, 7, 0:XB], ACT.Sqrt, scale=1.0 / D_MODEL,
                                         bias=eps_col[:, :]).then_inc(std_done, 1)
                    act.wait_ge(xn_done, b + 1)
                    nc.scalar.activation(xh[:, :, bass.ds(i * 2 * XB + u * XB, XB)], xn[:, :, :],
                                         ACT.Copy).then_inc(xh_done, 1)

            def split_hi(c, turn, u):
                act.wait_ge(w_in[u], 16 * turn + 16)
                act.wait_ge(acc_done, NB * c + NB)
                nc.scalar.activation(wh[:, u, :, :], wraw[:, u, :, :], ACT.Copy).then_inc(w_hi, 1)

            def chunk(kind, c, turn, k, kturn, u):
                split_hi(c + 1, turn + u, 1 - u)
                if kind == "plain":
                    act.wait_ge(plain_out[u], 16 * kturn + 16)
                elif kind == "conv":
                    act.wait_ge(plain_out[u], 16 * ((N_PLAIN + 1 - u) // 2) + 16)
                    act.wait_ge(conv_done, k + 1)
                else:
                    act.wait_ge(z_out[u], 16 * kturn + 16)
                for tb in range(NB):
                    act.wait_ge(acc_done, NB * c + tb + 1 + 2 * NB)
                    nc.scalar.activation(stage[:, u, HALO + 512 * tb:HALO + 512 * (tb + 1)], ps[:, NB * u + tb, :],
                                         ACT.Silu if kind == "z" else ACT.Copy).then_inc(evac_done, 1)
                if kind == "conv":
                    act.wait_ge(conv_done, k + 3)
                    act.wait_ge(conv_stored[u], 16 * kturn + 16)
                    nc.scalar.activation(conv_out[:, u, :], conv_acc[:, u, :], ACT.Silu).then_inc(silu_done, 1)
                    act.wait_ge(silu_done, k + 3)
                    src, stored = conv_out[:, u, :], conv_stored
                else:
                    act.wait_ge(evac_done, NB * c + 3 * NB)
                    src, stored = stage[:, u, HALO:HALO + S], plain_out if kind == "plain" else z_out
                act.dma_start(projT[bass.ds(c, 1)].rearrange("a p s -> p (a s)"), src).then_inc(stored[u], 16)

            split_hi(0, 0, 0)
            chunk("plain", 0, 0, 0, 0, 0)
            for kind, first, n in (("plain", 1, N_PLAIN - 1), ("conv", C_CONV, N_CONV), ("z", C_Z, N_Z)):
                with act.Fori(0, n // 2) as i:
                    for v, u in ((0, 1), (1, 0)):
                        k = 2 * i + v + (1 if kind == "plain" else 0)
                        chunk(kind, 2 * i + (first + v), i + (first + v) // 2, k, i + (v if kind == "plain" else 0), u)
            for u in range(2):
                act.wait_ge(plain_out[u], 16 * ((N_PLAIN + 1 - u) // 2) + 16)
                act.wait_ge(conv_stored[u], 16 * (N_CONV // 2) + 16)
                act.wait_ge(z_out[u], 16 * (N_Z // 2) + 16)

        @block.tensor
        def _(pe):
            pe.sem_inc(acc_done, 2 * NB)
            pe.wait_ge(const_set, 3)
            with pe.Fori(0, NX) as i:
                pe.wait_ge(sq_done, i + 1)
                for k in range(KC):
                    last = nc.tensor.matmul(ps[:, 7, 0:XB], ones[:, :], xsq[:, k, :], start=(k == 0), stop=(k == KC - 1))
                last.then_inc(ss_done, 1)
            pe.wait_ge(xl_done, NX + 2)

            def project(c, u):
                pe.wait_ge(w_lo, c + 3)
                for tb in range(NB):
                    pe.wait_ge(evac_done, NB * c + tb + 1)
                    tok = slice(512 * tb, 512 * (tb + 1))
                    for kc in range(KC):
                        acc = ps[:, NB * u + tb, :]
                        nc.tensor.matmul(acc, wh[:, u, kc, :], xh[:, kc, tok], start=(kc == 0), stop=False)
                        nc.tensor.matmul(acc, wh[:, u, kc, :], xl[:, kc, tok], start=False, stop=False)
                        last = nc.tensor.matmul(acc, wl[:, u, kc, :], xh[:, kc, tok], start=False, stop=(kc == KC - 1))
                    last.then_inc(acc_done, 1)

            with pe.Fori(0, N_CHUNK // 2) as i:
                for u in range(2):
                    project(2 * i + u, u)
            project(N_CHUNK - 1, 0)


R_W, R_B, R_A = 0, IDX_HEADS, IDX_HEADS + B_HEADS
N_SMALL = IDX_HEADS + 2 * B_HEADS


STAGES = 17
SPARE = (2, 1, 2) + (1,) * 11 + (1.5, 1.5, 1)
BITS = 31
RELUS = 4


class SelectionPlan:

    def __init__(self, S, topk):
        NT = S // P
        end = STAGES * NT
        self.tiles = [t for t in range(NT) if (t + 1) * P > topk]
        assert all(t * P + CHUNK >= topk for t in self.tiles)
        self.parts = {}
        self.number, acc_slot, relu_slot, score_slot = {}, [], [], []
        cost = lambda j, k: (500 + 1.05 * (j + 1) * P) * (1 if 1 <= k <= BITS else 2)
        pieces = lambda j: [(h, x) for h in range(IDX_HEADS) for x in range(0, (j + 1) * P, 512)]
        total = sum(sum(cost(j, k) for k in range(BITS + 4)) + 600 * len(pieces(j)) for j in self.tiles)
        slot = STAGES
        rate = total / sum(SPARE[s % STAGES] for s in range(slot, end - 2))
        ahead = [0.0]

        def dve(slot, part, cost):
            while ahead[0] + cost / 2 > 0 and slot < end - 1:
                slot += 1
                ahead[0] -= rate * SPARE[slot % STAGES]
            ahead[0] += cost
            self.put("dve", slot, part)
            return slot

        q_slot = self.rotation(self.tiles[0], 9)
        for i, j in enumerate(self.tiles):
            slot = max(slot, q_slot + 1)
            ready = q_slot
            if i + 1 < len(self.tiles):
                q_slot = self.rotation(self.tiles[i + 1], slot)
            for h, x in pieces(j):
                slot = dve(slot, ("acc", j, h, x), 600)
                n = len(acc_slot)
                acc_slot.append(slot)
                relu_slot.append(max(ready, slot - 3, acc_slot[n - RELUS] if n >= RELUS else 0))
                score_slot.append(max(ready, relu_slot[n] - 2, relu_slot[n - 2] if n >= 2 else 0))
                self.number[j, h, x] = n + 1
                self.put("act", relu_slot[n], ("relu", j, h, x))
                self.put("pe", score_slot[n], ("scores", j, h, x))
            for k in range(BITS + 4):
                slot = dve(slot, ("select", j, k), cost(j, k))
            self.put("sp", slot, ("store", j))

    def rotation(self, j, slot):
        self.put("sp", slot, ("load", j))
        slot += 1
        for k in range(4):
            while slot % STAGES in range(1, 5):
                slot += 1
            if k == 3:
                self.put("act", slot, ("round", j))
            self.put("pool", slot, ("rotate", j, k))
            slot += 1
        return slot - 1

    def put(self, eng, slot, part):
        self.parts.setdefault((eng, slot), []).append(part)

    def at(self, eng, t, m):
        return self.parts.get((eng, STAGES * t + m), [])


def rotated_rows(eng, a, b, src, sem_in):
    half = HD // 2
    for base in (0, HD):
        eng.dma_start(a[base:base + HD], src).then_inc(sem_in, 16)
        eng.dma_start(b[base:base + half], src[half:HD]).then_inc(sem_in, 16)
        eng.dma_start(b[base + half:base + HD], src[0:half]).then_inc(sem_in, 16)


def deltanet_and_selection(nc, S, topk, projT, a_log, dt_bias, g_gdn, consts, mixT, biasT):
    NT = S // P
    H, W = B_HEADS, B_HEADS * P
    QK = float(BD) ** -0.5
    plan = SelectionPlan(S, topk)
    with ExitStack() as ctx:
        sb = lambda n, s, d=fp32: ctx.enter_context(nc.sbuf_tensor(n, s, d))
        sem = lambda n: ctx.enter_context(nc.semaphore(n))
        ident = sb("g_ident", [P, P])
        triu = sb("g_triu", [P, P])
        ones = sb("g_ones", [P, P])
        incl = sb("g_incl", [P, P])
        strict = sb("g_strict", [P, P])
        diag16 = sb("g_diag16", [P, P])
        off16 = sb("g_off16", [P, P])
        small = sb("g_small", [N_SMALL, S])
        cosT, sinT = sb("i_cos", [P, S]), sb("i_sin", [P, S])
        ikeys = sb("i_keys", [P, S], f32r)
        rot = sb("i_rot", [P, 2, IDX_HEADS, P])
        q_hi, q_lo = sb("i_qhi", [P, 2, IDX_HEADS, P], f32r), sb("i_qlo", [P, 2, IDX_HEADS, P], f32r)
        w_idx = sb("i_w", [P, NT, IDX_HEADS])
        relu = sb("i_relu", [P, RELUS, 512])
        score, left, bias = sb("i_score", [P, S]), sb("i_left", [P, S]), sb("i_bias", [P, S])
        count, bound, sign, value, room = [sb("i_" + n, [P, 1]) for n in "count bound sign value room".split()]
        trial, drop = sb("i_trial", [P, 1], i32), sb("i_drop", [P, 1], i32)
        eps_col = sb("g_eps", [P, 1])
        ln_qk = sb("g_ln_qk", [P, 1])
        one_col = sb("g_one", [P, 1])
        alog = sb("g_alog", [P, H])
        dtb = sb("g_dtb", [P, H])
        gg = sb("g_gg", [P, 1])
        sm = sb("g_sm", [P, NT, N_SMALL])
        beta = sb("g_beta", [P, NT, H])
        gate = sb("g_gate", [P, NT, H])
        sp_a = sb("g_spa", [P, NT, H])
        sp_b = sb("g_spb", [P, NT, H])
        gcum = sb("g_gcum", [P, NT, H])
        egc = sb("g_egc", [P, NT, H])
        nbeg = sb("g_nbeg", [P, NT, H])
        qkvz = sb("g_qkvz", [P, 2, 4, H, P])
        sq = sb("g_sq", [P, 2, H, P])
        rn = sb("g_rn", [P, 2, H, P])
        qk = sb("g_qk", [P, 2, H, P])
        big = {n: sb("g_" + n, [P, H, P]) for n in
               "G X D Dq Ds EG N at m n LT L Y n2 m2 n4 m4 n8 Dinv E F E2 F2 E4 Z attT kt kbe vb qd wT vnew osq orn otmp".split()}
        B = lambda n: big[n][:, :, :]
        out_b = sb("g_out", [P, 2, H, P])
        st_S = sb("g_state", [P, H, P])
        tail = sb("g_tail", [P, H])
        etail = sb("g_etail", [P, H])
        ps = ctx.enter_context(nc.psum_tensor("g_ps", [P, 6, H, P], fp32))
        ips = ctx.enter_context(nc.psum_tensor("i_ps", [P, 2, 512], fp32))
        BANK = {n: i % 6 for i, n in enumerate("ssq ssk gb kk att NT atT kT vT n2 m2 n4 m4 Y1 n8 Y2 Y3 Dinv E F Z1 E2 F2 Z2 "
                                               "E4 Z3 wT vnew out state oss".split())}
        bank = lambda n: ps[:, BANK[n], :, :]
        const_in, const_set = sem("g_const_in"), sem("g_const_set")
        load = [sem(f"g_load{u}") for u in range(2)]
        stored = [sem(f"g_stored{u}") for u in range(2)]
        sel_s, key_in, key_mul, key_hi, key_done, w_done = map(sem, "i_sel i_key_in i_key_mul i_key_hi i_key_done i_w_done".split())
        q_in, q_mul, q_rot, q_hid, q_lod = map(sem, "i_q_in i_q_mul i_q_rot i_q_hid i_q_lod".split())
        scored, relu_done, acc_done, selected, bias_stored = map(sem, "i_scored i_relu i_acc i_selected i_stored".split())
        dve_s, act_s, pool_s, pe_s = sem("g_dve"), sem("g_act"), sem("g_pool"), sem("g_pe")
        block = ctx.enter_context(nc.Block())
        ph = lambda a: a.rearrange("p a b -> p (a b)")
        bc = lambda m: m[:, :].unsqueeze(1).to_broadcast([P, H, P])

        count_of = lambda names: {n: i + 1 for i, n in enumerate(names.split())}
        PE = count_of("ss gb kk att tr kT vT n2 m2 n4 m4 Y1 n8 Y2 Y3 Dinv E F Z1 E2 F2 Z2 E4 Z3 wT vnew out state oss")
        DV = count_of("qk X tail N at m LT kt kbe vb Y1 Y2 Y3 Z1 Z2 Z3 S otmp")
        AC = count_of("sq ln rnq rnk EG D etail attT n2 m2 n4 m4 n8 Dinv E F E2 F2 E4 wT vnew osq oln orn")
        PO = count_of("G X Dq Ds qd n L Y out")
        PE0, DV0, AC0 = 2, 7, 6

        def waits(eng, t):
            return (lambda n: eng.wait_ge(pe_s, PE0 + len(PE) * t + PE[n]),
                    lambda n: eng.wait_ge(dve_s, DV0 + len(DV) * t + DV[n]),
                    lambda n: eng.wait_ge(act_s, AC0 + len(AC) * t + AC[n]),
                    lambda n: eng.wait_ge(pool_s, len(PO) * t + PO[n]))

        order = {j: i for i, j in enumerate(plan.tiles)}
        last_piece = lambda j: plan.number[j, IDX_HEADS - 1, (j + 1) * P - ((j + 1) * P - 1) % 512 - 1]
        KEY_STAGE = {3 + 3 * k: k for k in range(-(-S // 1024))}
        KP = min(S, 1024)
        flat = lambda k: rot[:, k].rearrange("p a b -> p (a b)")[:, 0:KP]
        rows = projT.rearrange("c p s -> (c p) s")
        tokens = lambda t: slice(t * P, (t + 1) * P)
        width = lambda j, x: min(512, (j + 1) * P - x)

        @block.sync
        def _(sp):
            for dst, src in ((ident[:, :], consts["ident"]), (triu[:, :], consts["triu"]), (incl[:, :], consts["incl"]),
                             (strict[:, :], consts["strict"]), (diag16[:, :], consts["diag16"]), (off16[:, :], consts["off16"]),
                             (small[:, :], projT[0, 0:N_SMALL, :]), (alog[:, :], a_log.to_broadcast([P, H])),
                             (dtb[:, :], dt_bias.to_broadcast([P, H])), (gg[:, :], g_gdn)):
                sp.dma_start(dst, src).then_inc(const_in, 16)

            def load_tile(t):
                sp.dma_start(qkvz[:, t % 2, :, :, :].rearrange("p a h s -> p (a h) s"),
                             projT[C_CONV:N_CHUNK, :, tokens(t)].rearrange("c p s -> p c s")).then_inc(load[t % 2], 16)

            load_tile(0)
            load_tile(1)
            sp.dma_start(cosT[:, :], consts["cosT"]).then_inc(key_in, 16)
            sp.dma_start(sinT[:, :], consts["sinT"]).then_inc(key_in, 16)
            for n in range(S // KP):
                if n:
                    sp.wait_ge(key_done, n)
                row = C_SMALL * P + HD
                rotated_rows(sp, flat(0), flat(1), rows[row:row + HD, n * KP:(n + 1) * KP], key_in)

            def selection(t, m):
                for kind, j in plan.at("sp", t, m):
                    if kind == "load":
                        if order[j]:
                            sp.wait_ge(q_lod, order[j])
                        else:
                            sp.wait_ge(key_done, S // KP)
                        rotated_rows(sp, rot[:, 0], rot[:, 1], rows[C_QI * P:C_QI * P + IDX_HEADS * HD, tokens(j)]
                                     .rearrange("(h r) s -> r h s", r=HD), q_in)
                    else:
                        sp.wait_ge(selected, order[j] + 1)
                        sp.dma_start(biasT[j, :, 0:(j + 1) * P], bias[:, 0:(j + 1) * P]).then_inc(bias_stored, 16)

            for t in range(NT):
                for m in range(STAGES):
                    selection(t, m)
                sp.wait_ge(pool_s, len(PO) * t + PO["out"])
                sp.dma_start(mixT[4:8, :, tokens(t)].rearrange("c p s -> p c s"), out_b[:, t % 2, :, :]).then_inc(stored[t % 2], 16)
                if t + 2 < NT:
                    load_tile(t + 2)
            for u in range(2):
                sp.wait_ge(stored[u], 16 * (NT // 2))
            sp.wait_ge(bias_stored, 16 * len(plan.tiles))

        @block.gpsimd
        def _(pool):
            step = lambda ins: ins.then_inc(pool_s, 1)
            nc.gpsimd.memset(ones[:, :], 1.0).then_inc(const_set, 1)
            nc.gpsimd.memset(eps_col[:, :], EPS).then_inc(const_set, 1)
            nc.gpsimd.memset(one_col[:, :], 1.0).then_inc(const_set, 1)
            nc.gpsimd.memset(ln_qk[:, :], float(np.log(QK))).then_inc(const_set, 1)
            nc.gpsimd.memset(st_S[:, :, :], 0.0).then_inc(const_set, 1)
            pool.wait_ge(const_in, 160)
            pool.wait_ge(dve_s, DV0)

            def selection(t, m):
                for _, j, k in plan.at("pool", t, m):
                    i = order[j]
                    table = lambda tab: tab[:, tokens(j)].unsqueeze(1).to_broadcast([P, IDX_HEADS, P])
                    if k == 0:
                        pool.wait_ge(q_in, 96 * (i + 1))
                        nc.gpsimd.tensor_tensor(rot[:, 0], rot[:, 0], table(cosT), ALU.mult).then_inc(q_mul, 1)
                    elif k == 1:
                        nc.gpsimd.tensor_tensor(rot[:, 1], rot[:, 1], table(sinT), ALU.mult).then_inc(q_mul, 1)
                    elif k == 2:
                        pool.wait_ge(q_mul, 2 * (i + 1))
                        nc.gpsimd.tensor_tensor(rot[:, 0], rot[:, 0], rot[:, 1], ALU.add).then_inc(q_rot, 1)
                    else:
                        pool.wait_ge(q_hid, i + 1)
                        nc.gpsimd.tensor_tensor(q_lo[:, i % 2], rot[:, 0], q_hi[:, i % 2].bitcast(fp32),
                                                ALU.subtract).then_inc(q_lod, 1)

            for t in range(NT):
                pe, dv, ac, po = waits(pool, t)
                selection(t, 0)
                step(nc.gpsimd.tensor_tensor(B("G"), bc(triu), gate[:, t, :].unsqueeze(2).to_broadcast([P, H, P]), ALU.mult))
                selection(t, 1)
                dv("X")
                step(nc.gpsimd.tensor_tensor(B("X"), B("X"), bc(incl), ALU.mult))
                ac("D")
                step(nc.gpsimd.tensor_tensor(B("Dq"), B("D"), bc(incl), ALU.mult))
                step(nc.gpsimd.tensor_tensor(B("Ds"), B("D"), bc(strict), ALU.mult))
                selection(t, 2)
                step(nc.gpsimd.tensor_tensor(B("qd"), qk[:, 0, :, :], B("EG"), ALU.mult))
                selection(t, 3)
                dv("N")
                step(nc.gpsimd.tensor_tensor(B("n"), B("N"), bc(diag16), ALU.mult))
                step(nc.gpsimd.tensor_tensor(B("L"), B("N"), bc(off16), ALU.mult))
                selection(t, 4)
                dv("m")
                step(nc.gpsimd.tensor_tensor(B("Y"), bc(ident), B("m"), ALU.subtract))
                for m in range(5, STAGES):
                    selection(t, m)
                dv("otmp")
                if t >= 2:
                    pool.wait_ge(stored[t % 2], 16 * (t // 2))
                step(nc.gpsimd.tensor_tensor(out_b[:, t % 2, :, :], B("otmp"), qkvz[:, t % 2, 3, :, :], ALU.mult))

        @block.tensor
        def _(pe):
            pe.wait_ge(const_in, 160)
            pe.wait_ge(const_set, 5)
            for t in range(NT):
                last = nc.tensor.transpose(ph(ps[:, 0, :, :])[:, t * N_SMALL:(t + 1) * N_SMALL],
                                           small[:, t * P:(t + 1) * P], ident[0:N_SMALL, 0:N_SMALL])
            last.then_inc(pe_s, 1)
            pe.wait_ge(dve_s, 6)
            nc.tensor.matmul(ph(ps[:, 1, :, :])[:, 0:NT * H], triu[:, :], gate[:, :, :].rearrange("p a b -> p (a b)"),
                             start=True, stop=True).then_inc(pe_s, 1)
            pe.wait_ge(dve_s, 7)
            pe.wait_ge(act_s, 6)

            def selection(t, m):
                for _, j, h, x in plan.at("pe", t, m):
                    n, w, i = plan.number[j, h, x], width(j, x), order[j]
                    if n == 1:
                        pe.wait_ge(key_done, S // KP)
                    if h == x == 0:
                        pe.wait_ge(q_lod, i + 1)
                    if n > 2:
                        pe.wait_ge(relu_done, n - 2)
                    dst = ips[:, n % 2, 0:w]
                    nc.tensor.matmul(dst, q_hi[:, i % 2, h, :], ikeys[:, x:x + w], start=True, stop=False)
                    nc.tensor.matmul(dst, q_lo[:, i % 2, h, :], ikeys[:, x:x + w], start=False, stop=True).then_inc(scored, 1)

            for t in range(NT):
                _, dv, ac, po = waits(pe, t)

                def heads(name, lhsT, rhs, more=None):
                    for h in range(H):
                        last = nc.tensor.matmul(bank(name)[:, h, :], lhsT[:, h, :], rhs[:, h, :], start=True, stop=more is None)
                        if more:
                            last = nc.tensor.matmul(bank(name)[:, h, :], more[0][:, h, :], more[1][:, h, :], start=False, stop=True)
                    last.then_inc(pe_s, 1)

                def transposes(name, src):
                    for h in range(H):
                        last = nc.tensor.transpose(bank(name)[:, h, :], src[:, h, :], ident[:, :])
                    return last

                def sum_squares(name, src):
                    return nc.tensor.matmul(ph(bank(name)), ones[:, :], ph(src), start=True, stop=True)

                selection(t, 0)
                ac("sq")
                sum_squares("ssq", sq[:, 0, :, :])
                sum_squares("ssk", sq[:, 1, :, :]).then_inc(pe_s, 1)
                po("G")
                sum_squares("gb", B("G")).then_inc(pe_s, 1)
                selection(t, 1)
                dv("qk")
                heads("kk", qk[:, 1, :, :], qk[:, 1, :, :])
                heads("att", qk[:, 0, :, :], qk[:, 1, :, :])
                selection(t, 2)
                dv("at")
                transposes("NT", B("N"))
                transposes("atT", B("at")).then_inc(pe_s, 1)
                transposes("kT", qk[:, 1, :, :]).then_inc(pe_s, 1)
                transposes("vT", qkvz[:, t % 2, 2, :, :]).then_inc(pe_s, 1)
                selection(t, 3)
                dv("m")
                po("n")
                heads("n2", B("m"), B("n"))
                heads("m2", B("n"), B("m"))
                selection(t, 4)
                ac("m2")
                dv("LT")
                heads("n4", B("m2"), B("n2"))
                ac("attT")
                heads("m4", B("n2"), B("m2"))
                po("Y")
                dv("kbe")
                heads("Y1", B("n2"), B("Y"))
                selection(t, 5)
                ac("m4")
                dv("vb")
                heads("n8", B("m4"), B("n4"))
                dv("Y1")
                heads("Y2", B("n4"), B("Y"))
                selection(t, 6)
                dv("Y2")
                ac("n8")
                heads("Y3", B("n8"), B("Y"))
                selection(t, 7)
                dv("Y3")
                transposes("Dinv", B("Y")).then_inc(pe_s, 1)
                selection(t, 8)
                ac("Dinv")
                heads("E", B("LT"), B("Dinv"))
                heads("F", B("Dinv"), B("LT"))
                selection(t, 9)
                ac("E")
                heads("Z1", B("E"), B("Y"))
                ac("F")
                heads("E2", B("F"), B("E"))
                heads("F2", B("E"), B("F"))
                selection(t, 10)
                ac("E2")
                dv("Z1")
                heads("Z2", B("E2"), B("Z"))
                ac("F2")
                heads("E4", B("F2"), B("E2"))
                selection(t, 11)
                ac("E4")
                dv("Z2")
                heads("Z3", B("E4"), B("Z"))
                selection(t, 12)
                dv("Z3")
                heads("wT", B("kbe"), B("Z"))
                selection(t, 13)
                ac("wT")
                heads("vnew", B("Z"), B("vb"), (B("wT"), st_S[:, :, :]))
                selection(t, 14)
                ac("vnew")
                po("qd")
                heads("out", st_S[:, :, :], B("qd"), (B("vnew"), B("attT")))
                heads("state", B("kt"), B("vnew"))
                selection(t, 15)
                ac("osq")
                sum_squares("oss", B("osq")).then_inc(pe_s, 1)
                selection(t, 16)
                if t + 1 < NT:
                    ac("orn")
                    dv("S")

        @block.scalar
        def _(act):
            n = [0]

            def step(ins):
                ins.then_inc(act_s, 1)
                n[0] += 1

            act.wait_ge(const_set, 5)
            act.wait_ge(const_in, 160)
            act.wait_ge(dve_s, 1)
            step(nc.scalar.activation(beta[:, :, :], sm[:, :, R_B:R_B + H], ACT.Sigmoid))
            act.wait_ge(dve_s, 3)
            step(nc.scalar.activation(sp_b[:, :, :], sp_b[:, :, :], ACT.Exp))
            act.wait_ge(act_s, 2)
            step(nc.scalar.activation(sp_b[:, :, :], sp_b[:, :, :], ACT.Ln, bias=one_col[:, :]))
            step(nc.scalar.activation(alog[:, :], alog[:, :], ACT.Exp))
            act.wait_ge(pe_s, 2)
            step(nc.scalar.activation(gcum[:, :, :].rearrange("p a b -> p (a b)"), ph(ps[:, 1, :, :])[:, 0:NT * H], ACT.Copy))
            act.wait_ge(act_s, 5)
            step(nc.scalar.activation(egc[:, :, :], gcum[:, :, :], ACT.Exp))
            assert n[0] == AC0
            nc.scalar.activation(w_idx[:, :, :], sm[:, :, R_W:R_W + IDX_HEADS], ACT.Copy,
                                 scale=float((IDX_HEADS * HD) ** -0.5)).then_inc(w_done, 1)

            def selection(t, m):
                if t == 0 and m in KEY_STAGE:
                    k = KEY_STAGE[m]
                    act.wait_ge(key_mul, 3 * (k + 1))
                    nc.scalar.activation(ikeys[:, k * KP:(k + 1) * KP], flat(0), ACT.Copy).then_inc(key_hi, 1)
                for kind, j, *piece in plan.at("act", t, m):
                    if kind == "round":
                        i = order[j]
                        act.wait_ge(q_rot, i + 1)
                        if i >= 2:
                            act.wait_ge(scored, last_piece(plan.tiles[i - 2]))
                        nc.scalar.activation(q_hi[:, i % 2], rot[:, 0], ACT.Copy).then_inc(q_hid, 1)
                    else:
                        c = plan.number[j, *piece]
                        w = width(j, piece[1])
                        act.wait_ge(scored, c)
                        if c > RELUS:
                            act.wait_ge(acc_done, c - RELUS)
                        nc.scalar.activation(relu[:, c % RELUS, 0:w], ips[:, c % 2, 0:w], ACT.Relu).then_inc(relu_done, 1)

            for t in range(NT):
                n[0] = 0
                pe, dv, ac, po = waits(act, t)

                def copy(name):
                    pe(name)
                    step(nc.scalar.activation(B(name), bank(name), ACT.Copy))

                selection(t, 0)
                act.wait_ge(load[t % 2], 16 * (t // 2 + 1))
                step(nc.scalar.activation(sq[:, :, :, :], qkvz[:, t % 2, 0:2, :, :], ACT.Square))
                pe("ss")
                step(nc.scalar.activation(rn[:, :, :, :], ps[:, 0:2, :, :], ACT.Ln, bias=eps_col[:, :]))
                ac("ln")
                step(nc.scalar.activation(rn[:, 0, :, :], rn[:, 0, :, :], ACT.Exp, scale=-0.5, bias=ln_qk[:, :]))
                step(nc.scalar.activation(rn[:, 1, :, :], rn[:, 1, :, :], ACT.Exp, scale=-0.5))
                pe("gb")
                step(nc.scalar.activation(B("EG"), bank("gb"), ACT.Exp))
                selection(t, 1)
                po("X")
                step(nc.scalar.activation(B("D"), B("X"), ACT.Exp, scale=-1.0))
                dv("tail")
                step(nc.scalar.activation(etail[:, :], tail[:, :], ACT.Exp))
                selection(t, 2)
                pe("tr")
                step(nc.scalar.activation(B("attT"), bank("atT"), ACT.Copy))
                selection(t, 3)
                copy("n2")
                copy("m2")
                selection(t, 4)
                copy("n4")
                copy("m4")
                selection(t, 5)
                copy("n8")
                selection(t, 6)
                selection(t, 7)
                copy("Dinv")
                selection(t, 8)
                copy("E")
                copy("F")
                selection(t, 9)
                copy("E2")
                copy("F2")
                selection(t, 10)
                copy("E4")
                selection(t, 11)
                selection(t, 12)
                copy("wT")
                selection(t, 13)
                copy("vnew")
                selection(t, 14)
                pe("out")
                step(nc.scalar.activation(B("osq"), bank("out"), ACT.Square))
                selection(t, 15)
                pe("oss")
                step(nc.scalar.activation(B("orn"), bank("oss"), ACT.Ln, scale=1.0 / BD, bias=eps_col[:, :]))
                ac("oln")
                step(nc.scalar.activation(B("orn"), B("orn"), ACT.Exp, scale=-0.5))
                selection(t, 16)
                assert n[0] == len(AC)

        @block.vector
        def _(dve):
            n = [0]
            st = Steps(dve, sel_s)

            def step(ins):
                ins.then_inc(dve_s, 1)
                n[0] += 1

            dve.wait_ge(const_in, 160)
            dve.wait_ge(pe_s, 1)
            step(nc.vector.tensor_copy(sm[:, :, :].rearrange("p a b -> p (a b)"), ph(ps[:, 0, :, :])[:, 0:NT * N_SMALL]))
            dve.wait_ge(dve_s, 1)
            step(nc.vector.tensor_tensor(sp_a[:, :, :], sm[:, :, R_A:R_A + H],
                                         dtb[:, :].unsqueeze(1).to_broadcast([P, NT, H]), ALU.add))
            dve.wait_ge(dve_s, 2)
            step(nc.vector.scalar_tensor_tensor(out=sp_b[:, :, :], in0=sp_a[:, :, :], scalar=-1.0, in1=sp_a[:, :, :],
                                                op0=ALU.mult, op1=ALU.min))
            dve.wait_ge(act_s, 4)
            step(nc.vector.scalar_tensor_tensor(out=sp_a[:, :, :], in0=sp_a[:, :, :], scalar=0.0, in1=sp_b[:, :, :],
                                                op0=ALU.max, op1=ALU.add))
            dve.wait_ge(dve_s, 4)
            step(nc.vector.scalar_tensor_tensor(out=gate[:, :, :], in0=sp_a[:, :, :], scalar=-1.0,
                                                in1=alog[:, :].unsqueeze(1).to_broadcast([P, NT, H]),
                                                op0=ALU.mult, op1=ALU.mult))
            dve.wait_ge(dve_s, 5)
            step(nc.vector.tensor_copy(sp_a[:, :, :], gate[:, :, :]))
            dve.wait_ge(act_s, 6)
            step(nc.vector.scalar_tensor_tensor(out=nbeg[:, :, :], in0=beta[:, :, :], scalar=-1.0, in1=egc[:, :, :],
                                                op0=ALU.mult, op1=ALU.mult))
            assert n[0] == DV0
            dve.wait_ge(w_done, 1)

            def rotate_keys(k):
                toks = slice(k * KP, (k + 1) * KP)
                dve.wait_ge(key_in, 32 + 96 * (k + 1))
                nc.vector.tensor_tensor(flat(0), flat(0), cosT[:, toks], ALU.mult).then_inc(key_mul, 1)
                nc.vector.tensor_tensor(flat(1), flat(1), sinT[:, toks], ALU.mult).then_inc(key_mul, 1)
                dve.wait_ge(key_mul, 3 * k + 2)
                nc.vector.tensor_tensor(flat(0), flat(0), flat(1), ALU.add).then_inc(key_mul, 1)

            def lower_keys(k):
                up = ikeys[HD:P, k * KP:(k + 1) * KP]
                dve.wait_ge(key_hi, k + 1)
                nc.vector.tensor_tensor(up, flat(0)[HD:P], up.bitcast(fp32), ALU.subtract).then_inc(key_done, 1)

            def accumulate(j, h, x):
                c, w = plan.number[j, h, x], width(j, x)
                dve.wait_ge(relu_done, c)
                if h == 0:
                    nc.vector.tensor_scalar(score[:, x:x + w], relu[:, c % RELUS, 0:w], w_idx[:, j, h:h + 1], None,
                                            ALU.mult).then_inc(acc_done, 1)
                else:
                    dve.wait_ge(acc_done, plan.number[j, h - 1, x])
                    nc.vector.scalar_tensor_tensor(out=score[:, x:x + w], in0=relu[:, c % RELUS, 0:w],
                                                   scalar=w_idx[:, j, h:h + 1], in1=score[:, x:x + w],
                                                   op0=ALU.mult, op1=ALU.add).then_inc(acc_done, 1)

            def select(j, k):
                N = (j + 1) * P
                sc, m, junk = score[:, 0:N], left[:, 0:N], bias[:, 0:N]
                if k == 0:
                    dve.wait_ge(acc_done, last_piece(j))
                    if order[j]:
                        dve.wait_ge(bias_stored, 16 * order[j])
                    st.do(nc.vector.memset(score[0:CHUNK, N - CHUNK:N], BARRED))
                    st.do(nc.vector.tensor_scalar(junk, sc, 0.0, None, ALU.is_ge, ALU.add, accum_out=count[:, :]))
                    st.do(nc.vector.tensor_scalar(bound[:, :], count[:, :], float(topk), None, ALU.is_ge))
                    nc.vector.tensor_scalar(sign[:, :], bound[:, :], 2.0, -1.0, ALU.mult, ALU.add)
                    st.do(nc.vector.tensor_scalar(bound[:, :], bound[:, :], float(2 * topk - N - 1), float(N - topk + 1),
                                                  ALU.mult, ALU.add))
                    st.do(nc.vector.memset(trial[:, :], 2 ** (BITS - 1)))
                    st.do(nc.vector.tensor_scalar(m, sc, sign[:, 0:1], None, ALU.mult))
                elif k <= BITS:
                    bit = BITS - k
                    st.do(nc.vector.tensor_scalar(junk, m, trial[:, 0:1].bitcast(fp32), None, ALU.is_ge, ALU.add,
                                                  accum_out=count[:, :]))
                    st.do(nc.vector.tensor_scalar(drop[:, :], count[:, :], bound[:, 0:1], float(2 ** bit), ALU.is_lt, ALU.mult))
                    st.do(nc.vector.scalar_tensor_tensor(out=trial[:, :], in0=drop[:, :], scalar=2 ** bit // 2, in1=trial[:, :],
                                                         op0=ALU.bitwise_or, op1=ALU.bitwise_xor))
                elif k == BITS + 1:
                    st.do(nc.vector.tensor_scalar(value[:, :], trial[:, 0:1].bitcast(fp32), sign[:, 0:1], None, ALU.mult))
                    st.do(nc.vector.tensor_scalar(junk, sc, value[:, 0:1], None, ALU.is_gt, ALU.add, accum_out=count[:, :]))
                    nc.vector.tensor_scalar(room[:, :], count[:, :], -1.0, float(topk), ALU.mult, ALU.add)
                    st.do(nc.vector.tensor_scalar(m, sc, value[:, 0:1], None, ALU.is_equal))
                elif k == BITS + 2:
                    st.do(nc.vector.tensor_tensor_scan(bias[:, 0:N], m, m, 0.0, ALU.add, ALU.bypass))
                    st.do(nc.vector.scalar_tensor_tensor(out=m, in0=bias[:, 0:N], scalar=room[:, 0:1], in1=m,
                                                         op0=ALU.is_gt, op1=ALU.mult))
                else:
                    st.do(nc.vector.scalar_tensor_tensor(out=m, in0=sc, scalar=value[:, 0:1], in1=m, op0=ALU.is_lt, op1=ALU.add))
                    nc.vector.tensor_scalar(bias[:, 0:N], m, MASK_BIAS, None, ALU.mult).then_inc(selected, 1)
                    dve.wait_ge(selected, order[j] + 1)

            def selection(t, m):
                if t == 0 and m in KEY_STAGE:
                    rotate_keys(KEY_STAGE[m])
                if t == 0 and m - 1 in KEY_STAGE:
                    lower_keys(KEY_STAGE[m - 1])
                for kind, *part in plan.at("dve", t, m):
                    (accumulate if kind == "acc" else select)(*part)

            for t in range(NT):
                n[0] = 0
                pe, own, ac, po = waits(dve, t)
                col = lambda a: a[:, t, :].unsqueeze(2).to_broadcast([P, H, P])
                selection(t, 0)
                ac("rnk")
                step(nc.vector.tensor_tensor(qk[:, :, :, :], qkvz[:, t % 2, 0:2, :, :], rn[:, :, :, :], ALU.mult))
                ac("EG")
                step(nc.vector.tensor_tensor(B("X"), bank("gb"), col(gcum), ALU.subtract))
                step(nc.vector.tensor_tensor(tail[:, :], bank("gb")[:, :, P - 1], gcum[:, t, :], ALU.subtract))
                selection(t, 1)
                pe("att")
                po("Ds")
                for h in range(H):
                    last = nc.vector.scalar_tensor_tensor(out=big["N"][:, h, :], in0=bank("kk")[:, h, :],
                                                          scalar=beta[:, t, h:h + 1], in1=big["Ds"][:, h, :],
                                                          op0=ALU.mult, op1=ALU.mult)
                step(last)
                step(nc.vector.tensor_tensor(B("at"), bank("att"), B("Dq"), ALU.mult))
                selection(t, 2)
                pe("tr")
                step(nc.vector.tensor_tensor(B("m"), bank("NT"), bc(diag16), ALU.mult))
                step(nc.vector.tensor_tensor(B("LT"), bank("NT"), bc(off16), ALU.mult))
                selection(t, 3)
                ac("etail")
                pe("kT")
                step(nc.vector.tensor_tensor(B("kt"), bank("kT"), etail[:, :].unsqueeze(2).to_broadcast([P, H, P]), ALU.mult))
                step(nc.vector.tensor_tensor(B("kbe"), bank("kT"), col(nbeg), ALU.mult))
                pe("vT")
                step(nc.vector.tensor_tensor(B("vb"), bank("vT"), col(beta), ALU.mult))
                selection(t, 4)

                def add(name, out, acc, op=ALU.add):
                    pe(name)
                    step(nc.vector.tensor_tensor(B(out), B(acc), bank(name), op))

                po("Y")
                add("Y1", "Y", "Y")
                selection(t, 5)
                own("Y1")
                add("Y2", "Y", "Y")
                selection(t, 6)
                own("Y2")
                add("Y3", "Y", "Y")
                for m in (7, 8, 9):
                    selection(t, m)
                own("Y3")
                add("Z1", "Z", "Y", ALU.subtract)
                selection(t, 10)
                own("Z1")
                add("Z2", "Z", "Z")
                selection(t, 11)
                own("Z2")
                add("Z3", "Z", "Z")
                for m in (12, 13, 14):
                    selection(t, m)
                pe("state")
                for h in range(H):
                    last = nc.vector.scalar_tensor_tensor(out=st_S[:, h, :], in0=st_S[:, h, :], scalar=big["EG"][:, h, P - 1:P],
                                                          in1=bank("state")[:, h, :], op0=ALU.mult, op1=ALU.add)
                step(last)
                selection(t, 15)
                ac("orn")
                step(nc.vector.scalar_tensor_tensor(out=ph(B("otmp")), in0=ph(bank("out")), scalar=gg[:, 0:1], in1=ph(B("orn")),
                                                    op0=ALU.mult, op1=ALU.mult))
                selection(t, 16)
                assert n[0] == len(DV)


def indexed_attention(nc, S, topk, projT, consts, biasT, mixT):
    NT, PIECE = S // P, 1024
    G = A_HEADS // KV_HEADS
    UN = KV_HEADS * NT
    with ExitStack() as ctx:
        sb = lambda n, s, d=fp32: ctx.enter_context(nc.sbuf_tensor(n, s, d))
        sem = lambda n: ctx.enter_context(nc.semaphore(n))
        ident, ones = sb("a_ident", [P, P]), sb("a_ones", [P, P])
        cosT, sinT = sb("a_cos", [P, S]), sb("a_sin", [P, S])
        keys = sb("a_keys", [P, KV_HEADS, S], f32r)
        vals = sb("a_vals", [P, NT, KV_HEADS, 2 * HD], f32r)
        rot = sb("a_rot", [P, 2, 2, 8, P])
        q_hi = sb("a_qhi", [P, 2, 8, P], f32r)
        q_lo = sb("a_qlo", [P, 2, 8, P], f32r)
        bias = sb("a_bias", [P, 2, S])
        prob = sb("a_prob", [P, A_HEADS, S])
        mx = sb("a_mx", [P, 2, A_HEADS])
        nmx = sb("a_nmx", [P, A_HEADS])
        rsum = sb("a_rsum", [P, A_HEADS])
        rinv = sb("a_rinv", [P, A_HEADS])
        diag = sb("a_diag", [P, G, P])
        p_hi = sb("a_phi", [P, 2, G * P], f32r)
        p_lo = sb("a_plo", [P, 2, G * P], f32r)
        rb, low = sb("a_rb", [HD, G * P]), sb("a_low", [HD, G * P])
        out = sb("a_out", [HD, KV_HEADS, G, P])
        ps = ctx.enter_context(nc.psum_tensor("a_ps", [P, 8, 512], fp32))
        slot_ps = lambda n, w: ps[:, 2 * (n % 2):2 * (n % 2) + 2, :].rearrange("p a b -> p (a b)")[:, 0:w]
        T_BANK = lambda n: 4 + n % 2
        O_BANK = lambda u: 6 + u % 2

        const_in, const_set, key_mul, key_sin, key_rot, key_hi, key_done, v_in, v_T, v_hi, v_done = map(sem, (
            "a_const_in a_const_set a_key_mul a_key_sin a_key_rot a_key_hi a_key_done a_v_in a_v_T a_v_hi a_v_done").split())
        pair = lambda n: [sem(f"a_{n}{k}") for k in range(2)]
        rot_in, bias_in, stored = pair("rot_in"), pair("bias_in"), pair("stored")
        q_cos, q_sin, q_rot, q_hid, q_lod = map(sem, "a_q_cos a_q_sin a_q_rot a_q_hi_done a_q_lo_done".split())
        att_done, bias_set, masked, max_done, exp_done, rinv_done, diag_done = map(sem, (
            "a_att a_bias_set a_masked a_max a_exp a_rinvd a_diagd").split())
        pT_done, hi_done, lo_done, pv_done, o_done, rb_done, sum_done, norm_done = map(sem, (
            "a_pTd a_hi a_lo a_pv a_o a_rbd a_sum a_norm").split())
        dve_s = sem("a_dve")

        def pieces(t):
            n = (t + 1) * P
            return [(a, min(PIECE, n - a)) for a in range(0, n, PIECE)]

        selected = [t for t in range(NT) if (t + 1) * P > topk]
        units = [(t, g) for t in range(NT) for g in range(KV_HEADS)]
        items = [(t, h, p) for t, g in units for h in range(g * G, g * G + G) for p in range(len(pieces(t)))]
        place = {it: n for n, it in enumerate(items)}
        last_item = lambda u: place[units[u][0], units[u][1] * G + G - 1, len(pieces(units[u][0])) - 1]
        turn = lambda u: sum(units[v][0] + 2 for v in range(u))
        chunks_to = lambda u: sum(units[v][0] + 1 for v in range(u))

        KP = min(S, 1024)
        key_steps = [(k, a) for k in range(KV_HEADS) for a in range(0, S, KP)]
        NK = len(key_steps)
        flat = lambda s, r: rot[:, s, r].rearrange("p a b -> p (a b)")[:, 0:KP]
        q_slot = lambda t: (NK + t) % 2
        q_in_count = lambda t: 96 * ((NK + t) // 2 + 1)
        block = ctx.enter_context(nc.Block())

        rows = projT.rearrange("c p s -> (c p) s")
        out_rows = mixT.rearrange("c p s -> (c p) s")
        tokens = lambda t: slice(t * P, (t + 1) * P)

        @block.sync
        def _(sp):
            def load_bias(t):
                if t in selected:
                    i = selected.index(t)
                    if t >= 2:
                        sp.wait_ge(masked, last_item(KV_HEADS * (t - 2) + 1) + 1)
                    sp.dma_start(bias[:, t % 2, 0:(t + 1) * P], biasT[t, :, 0:(t + 1) * P]).then_inc(bias_in[t % 2], 16)

            for n, (k, a) in enumerate(key_steps):
                if n >= 2:
                    sp.wait_ge(key_done, n - 1)
                row = C_KA * P + k * HD
                rotated_rows(sp, flat(n % 2, 0), flat(n % 2, 1), rows[row:row + HD, a:a + KP], rot_in[n % 2])
                if n == 0:
                    for dst, src in ((cosT[:, :], consts["cosT"]), (sinT[:, :], consts["sinT"]), (ident[:, :], consts["ident"])):
                        sp.dma_start(dst, src).then_inc(const_in, 16)
                    sp.dma_start(prob[:, 0, :], projT[C_VA]).then_inc(v_in, 16)

            def store(u):
                t, g = units[u]
                sp.wait_ge(norm_done, u + 1)
                sp.dma_start(out_rows[g * G * HD:(g + 1) * G * HD, tokens(t)].rearrange("(h d) s -> d h s", d=HD),
                             out[:, g, :, :]).then_inc(stored[g], 16)

            for t in range(NT):
                if t >= 2:
                    sp.wait_ge(q_lod, t - 1)
                else:
                    sp.wait_ge(key_done, NK - 1 + t)
                rotated_rows(sp, rot[:, q_slot(t), 0], rot[:, q_slot(t), 1],
                             rows[C_QA * P:C_QA * P + A_HEADS * HD, tokens(t)].rearrange("(h r) s -> r h s", r=HD), rot_in[q_slot(t)])
                if t == 0:
                    load_bias(0)
                if t + 1 < NT:
                    load_bias(t + 1)
                if t >= 2:
                    store(2 * t - 4)
                    store(2 * t - 3)
            for u in range(2 * NT - 4, 2 * NT):
                store(u)
            for g in range(KV_HEADS):
                sp.wait_ge(stored[g], 16 * NT)

        @block.gpsimd
        def _(pool):
            nc.gpsimd.memset(ones[:, :], 1.0).then_inc(const_set, 1)
            pool.wait_ge(const_in, 48)
            for n, (k, a) in enumerate(key_steps):
                pool.wait_ge(rot_in[n % 2], 96 * (n // 2 + 1))
                nc.gpsimd.tensor_tensor(flat(n % 2, 1), flat(n % 2, 1), sinT[:, a:a + KP], ALU.mult).then_inc(key_sin, 1)

            def rotate(t):
                s = q_slot(t)
                table = sinT[:, tokens(t)].unsqueeze(1).to_broadcast([P, 8, P])
                pool.wait_ge(rot_in[s], q_in_count(t))
                nc.gpsimd.tensor_tensor(rot[:, s, 1], rot[:, s, 1], table, ALU.mult).then_inc(q_sin, 1)
                pool.wait_ge(q_sin, t + 1)
                pool.wait_ge(q_cos, t + 1)
                nc.gpsimd.tensor_tensor(rot[:, s, 0], rot[:, s, 0], rot[:, s, 1], ALU.add).then_inc(q_rot, 1)
                pool.wait_ge(q_hid, t + 1)
                nc.gpsimd.tensor_tensor(q_lo[:, t % 2], rot[:, s, 0], q_hi[:, t % 2].bitcast(fp32), ALU.subtract).then_inc(q_lod, 1)

            rotate(0)
            for u, (t, g) in enumerate(units):
                if g == 0 and t + 1 < NT:
                    rotate(t + 1)
                pool.wait_ge(rinv_done, u + 1)
                if u:
                    pool.wait_ge(o_done, u)
                nc.gpsimd.tensor_tensor(diag[:, :, :], ident[:, :].unsqueeze(1).to_broadcast([P, G, P]),
                                        rinv[:, g * G:(g + 1) * G].unsqueeze(2).to_broadcast([P, G, P]),
                                        ALU.mult).then_inc(diag_done, 1)

        @block.scalar
        def _(act):
            for n in range(NT // 4):
                act.wait_ge(v_T, n + 1)
                nc.scalar.activation(vals[:, 4 * n:4 * n + 4, :, 0:HD], ps[:, 4 + n % 2, :].rearrange(
                    "p (t g d) -> p t g d", t=4, g=KV_HEADS), ACT.Copy).then_inc(v_hi, 1)
            for n, (k, a) in enumerate(key_steps):
                act.wait_ge(key_rot, n + 1)
                nc.scalar.activation(keys[:, k, a:a + KP], flat(n % 2, 0), ACT.Copy).then_inc(key_hi, 1)

            def round_q(t):
                act.wait_ge(q_rot, t + 1)
                if t >= 2:
                    act.wait_ge(att_done, last_item(2 * (t - 2) + 1) + 1)
                nc.scalar.activation(q_hi[:, t % 2], rot[:, q_slot(t), 0], ACT.Copy).then_inc(q_hid, 1)

            def exponentials(u):
                t, g = units[u]
                act.wait_ge(max_done, u + 1)
                for h in range(g * G, (g + 1) * G):
                    nc.scalar.activation(prob[:, h, 0:(t + 1) * P], prob[:, h, 0:(t + 1) * P], ACT.Exp, bias=nmx[:, h:h + 1],
                                         scale=HD ** -0.5, accum_out=rsum[:, h:h + 1]).then_inc(exp_done, 1)

            def halves(u):
                t, g = units[u]
                for c in range(t + 1):
                    n, m = turn(u) + c, chunks_to(u) + c
                    act.wait_ge(pT_done, m + 1)
                    if m >= 2:
                        act.wait_ge(pv_done, m - 1)
                    nc.scalar.activation(p_hi[:, m % 2, :], ps[:, T_BANK(n), :], ACT.Copy).then_inc(hi_done, 1)
                act.wait_ge(o_done, u + 1)
                if u:
                    act.wait_ge(norm_done, u)
                nc.scalar.activation(rb[:, :], ps[0:HD, T_BANK(turn(u) + t + 1), :], ACT.Copy).then_inc(rb_done, 1)
                nc.scalar.activation(low[:, :], ps[HD:P, O_BANK(u), :], ACT.Copy).then_inc(rb_done, 1)

            round_q(0)
            for u, (t, g) in enumerate(units):
                if g == 0 and t + 1 < NT:
                    round_q(t + 1)
                if u:
                    halves(u - 1)
                exponentials(u)
            halves(UN - 1)

        @block.vector
        def _(dve):
            st = Steps(dve, dve_s)
            for n in range(NT // 4):
                dve.wait_ge(v_hi, n + 1)
                nc.vector.tensor_tensor(vals[:, 4 * n:4 * n + 4, :, HD:2 * HD], ps[:, 4 + n % 2, :].rearrange(
                    "p (t g d) -> p t g d", t=4, g=KV_HEADS), vals[:, 4 * n:4 * n + 4, :, 0:HD].bitcast(fp32),
                    ALU.subtract).then_inc(v_done, 1)
            dve.wait_ge(const_in, 48)
            for n, (k, a) in enumerate(key_steps):
                dve.wait_ge(rot_in[n % 2], 96 * (n // 2 + 1))
                nc.vector.tensor_tensor(flat(n % 2, 0), flat(n % 2, 0), cosT[:, a:a + KP], ALU.mult).then_inc(key_mul, 1)
                dve.wait_ge(key_mul, n + 1)
                dve.wait_ge(key_sin, n + 1)
                nc.vector.tensor_tensor(flat(n % 2, 0), flat(n % 2, 0), flat(n % 2, 1), ALU.add).then_inc(key_rot, 1)
                up = keys[HD:P, k, a:a + KP]
                dve.wait_ge(key_hi, n + 1)
                nc.vector.tensor_tensor(up, flat(n % 2, 0)[HD:P], up.bitcast(fp32), ALU.subtract).then_inc(key_done, 1)

            def rotate(t):
                s = q_slot(t)
                dve.wait_ge(rot_in[s], q_in_count(t))
                nc.vector.tensor_tensor(rot[:, s, 0], rot[:, s, 0], cosT[:, tokens(t)].unsqueeze(1).to_broadcast([P, 8, P]),
                                        ALU.mult).then_inc(q_cos, 1)

            def mask(u):
                t, g = units[u]
                N, hs = (t + 1) * P, slice(g * G, (g + 1) * G)
                if g == 0:
                    if t in selected:
                        dve.wait_ge(bias_in[t % 2], 16 * len([x for x in selected if x <= t and x % 2 == t % 2]))
                    else:
                        st.do(nc.vector.memset(bias[:, t % 2, 0:N], 0.0))
                        st.do(nc.vector.memset(bias[0:CHUNK, t % 2, N - CHUNK:N], MASK_BIAS))
                if u >= 2:
                    dve.wait_ge(pT_done, chunks_to(u - 1))
                for h in range(g * G, (g + 1) * G):
                    for p, (a, w) in enumerate(pieces(t)):
                        n = place[t, h, p]
                        dve.wait_ge(att_done, n + 1)
                        nc.vector.tensor_tensor_reduce(out=prob[:, h, a:a + w], in0=slot_ps(n, w), in1=bias[:, t % 2, a:a + w],
                                                       scale=1.0, scalar=-3.0e38, op0=ALU.add, op1=ALU.max,
                                                       accum_out=mx[:, p, h:h + 1]).then_inc(masked, 1)
                dve.wait_ge(masked, n + 1)
                if len(pieces(t)) == 2:
                    st.do(nc.vector.tensor_tensor(mx[:, 0, hs], mx[:, 0, hs], mx[:, 1, hs], ALU.max))
                if u >= 2:
                    dve.wait_ge(exp_done, G * (u - 1))
                nc.vector.tensor_scalar(nmx[:, hs], mx[:, 0, hs], -HD ** -0.5, None, ALU.mult).then_inc(max_done, 1)

            def halves(u):
                t, g = units[u]
                hs = slice(g * G, (g + 1) * G)
                dve.wait_ge(exp_done, G * (u + 1))
                if u >= 2:
                    dve.wait_ge(diag_done, u - 1)
                nc.vector.reciprocal(rinv[:, hs], rsum[:, hs]).then_inc(rinv_done, 1)
                for c in range(t + 1):
                    n, m = turn(u) + c, chunks_to(u) + c
                    dve.wait_ge(hi_done, m + 1)
                    nc.vector.tensor_tensor(p_lo[:, m % 2, :], ps[:, T_BANK(n), :], p_hi[:, m % 2, :].bitcast(fp32),
                                            ALU.subtract).then_inc(lo_done, 1)
                dve.wait_ge(rb_done, 2 * u + 2)
                o = out[:, g, :, :].rearrange("p a b -> p (a b)")
                if t:
                    dve.wait_ge(stored[g], 16 * t)
                nc.vector.tensor_tensor(o, ps[0:HD, O_BANK(u), :], low[:, :], ALU.add).then_inc(sum_done, 1)
                dve.wait_ge(sum_done, u + 1)
                nc.vector.tensor_tensor(o, o, rb[:, :], ALU.mult).then_inc(norm_done, 1)

            rotate(0)
            for u, (t, g) in enumerate(units):
                if g == 0 and t + 1 < NT:
                    rotate(t + 1)
                mask(u)
                if u:
                    halves(u - 1)
            halves(UN - 1)

        @block.tensor
        def _(pe):
            pe.wait_ge(const_in, 48)
            pe.wait_ge(v_in, 16)
            for n in range(NT // 4):
                if n >= 2:
                    pe.wait_ge(v_done, n - 1)
                for j in range(4):
                    last = nc.tensor.transpose(ps[:, 4 + n % 2, j * P:(j + 1) * P], prob[:, 0, tokens(4 * n + j)], ident[:, :])
                last.then_inc(v_T, 1)
            pe.wait_ge(const_set, 1)
            pe.wait_ge(v_done, NT // 4)
            pe.wait_ge(key_done, NK)

            def scores(u):
                t, g = units[u]
                pe.wait_ge(q_lod, t + 1)
                for h in range(g * G, (g + 1) * G):
                    for p, (a, w) in enumerate(pieces(t)):
                        n = place[t, h, p]
                        if n >= 2:
                            pe.wait_ge(masked, n - 1)
                        for x in range(0, w, 512):
                            y = min(512, w - x)
                            dst = slot_ps(n, w)[:, x:x + y]
                            nc.tensor.matmul(dst, q_hi[:, t % 2, h, :], keys[:, g, a + x:a + x + y], start=True, stop=False)
                            last = nc.tensor.matmul(dst, q_lo[:, t % 2, h, :], keys[:, g, a + x:a + x + y], start=False, stop=True)
                        last.then_inc(att_done, 1)

            def values(u):
                t, g = units[u]

                def bank_free(n):
                    if n < 2:
                        return
                    v = max(v for v in range(u + 1) if turn(v) <= n - 2)
                    c = n - 2 - turn(v)
                    if c == units[v][0] + 1:
                        pe.wait_ge(rb_done, 2 * v + 1)
                    else:
                        pe.wait_ge(lo_done, chunks_to(v) + c + 1)

                def transpose(c):
                    n = turn(u) + c
                    bank_free(n)
                    if c == 0:
                        pe.wait_ge(exp_done, G * (u + 1))
                    for j in range(G):
                        last = nc.tensor.transpose(ps[:, T_BANK(n), j * P:(j + 1) * P], prob[:, g * G + j, tokens(c)], ident[:, :])
                    last.then_inc(pT_done, 1)

                transpose(0)
                for c in range(t + 1):
                    if c < t:
                        transpose(c + 1)
                    m = chunks_to(u) + c
                    if c == 0 and u >= 2:
                        pe.wait_ge(norm_done, u - 1)
                    pe.wait_ge(hi_done, m + 1)
                    nc.tensor.matmul(ps[:, O_BANK(u), :], vals[:, c, g, :], p_hi[:, m % 2, :], start=(c == 0), stop=False)
                    pe.wait_ge(lo_done, m + 1)
                    nc.tensor.matmul(ps[:, O_BANK(u), :], vals[:, c, g, :], p_lo[:, m % 2, :],
                                     start=False, stop=(c == t)).then_inc(pv_done, 1)
                n = turn(u) + t + 1
                bank_free(n)
                pe.wait_ge(diag_done, u + 1)
                nc.tensor.matmul(ps[0:HD, T_BANK(n), :], ones[:, 0:HD], diag[:, :, :].rearrange("p a b -> p (a b)"),
                                 start=True, stop=True).then_inc(o_done, 1)

            for u in range(UN):
                scores(u)
                if u:
                    values(u - 1)
            values(UN - 1)


def output_and_mlp(nc, S, xT, mixT, w_units, g_ffn, g_final, outT):
    TB, NB, NG, U = 512, S // 512, D_FF // 512, 4
    SEGS, UNITS = 2 + 2 * NG, 4 * (2 + 2 * NG)
    F_BLK, Y_BLK = 2 * U + NG * U, NG * KC
    with ExitStack() as ctx:
        sb = lambda n, s, d=fp32: ctx.enter_context(nc.sbuf_tensor(n, s, d))
        sem = lambda n: ctx.enter_context(nc.semaphore(n))
        ones, eps_col = sb("f_ones", [P, P]), sb("f_eps", [P, 1])
        gf, gl = sb("f_gf", [P, KC]), sb("f_gl", [P, KC])
        raw = sb("f_raw", [P, U, KC, P])
        wh = sb("f_wh", [P, 2 * U, KC, P], f32r)
        wl = sb("f_wl", [P, 2 * U, KC, P], f32r)
        tmp = sb("f_tmp", [P, KC, TB])
        acc = sb("f_acc", [P, KC, TB])
        ah = sb("f_ah", [P, KC, TB], f32r)
        al = sb("f_al", [P, KC, TB], f32r)
        th = sb("f_th", [P, 2, U, TB], f32r)
        tl = sb("f_tl", [P, 2, U, TB], f32r)
        rl = sb("f_rl", [P, 2, TB])
        r2 = sb("f_r2", [P, 2, TB])
        rstd = sb("f_rstd", [P, TB])
        ps = ctx.enter_context(nc.psum_tensor("f_ps", [P, 8, TB], fp32))
        (const_in, const_set, mix_in, x_in, mh_done, ml_done, x_done, sq_done, ss_done, std_done, h_done, hh_done, hl_done,
         f_done, y_done, y_add, r_done, th_done, r2_done, tl_done, out_done, stored, w_hi, w_lo, dve_s) = map(
            sem, ["f_" + n for n in ("const_in const_set mix_in x_in mh_done ml_done x_done sq_done ss_done std_done h_done "
                                     "hh_done hl_done f_done y_done y_add r_done th_done r2_done tl_done out_done stored "
                                     "w_hi w_lo dve").split()])
        raw_in = [sem(f"f_raw_in{n}") for n in range(U)]
        Y0, R0, SS0 = 2 * KC, 1, 1
        block = ctx.enter_context(nc.Block())

        def segments(eng, b, body):
            body("O", 0, 0, 0, 0, ("O", 1, 1))
            body("O", 1, 0, 1, 1, ("W1", 0, 2))
            body("W1", 0, 0, 2, 0, ("W1", 1, 3))
            with eng.Fori(0, (NG - 2) // 2) as j:
                for v in range(2):
                    g = 2 * j + (v + 1)
                    body("W1", g, (v + 1) % 2, 2 * g + 1, 1, ("W2", g - 1, 2 * g + 2))
                    body("W2", g - 1, v % 2, 2 * g + 2, 0, ("W1", g + 1, 2 * g + 3))
            g = NG - 1
            body("W1", g, g % 2, 2 * g + 1, 1, ("W2", g - 1, 2 * g + 2))
            body("W2", g - 1, (g - 1) % 2, 2 * g + 2, 0, ("W2", g, 2 * g + 3))
            body("W2", g, g % 2, 2 * g + 3, 1, None)

        def tokens(b):
            return bass.ds(b * TB, TB)

        @block.sync
        def _(sp):
            sp.dma_start(gf[:, :], g_ffn).then_inc(const_in, 16)
            sp.dma_start(gl[:, :], g_final).then_inc(const_in, 16)
            sp.sem_inc(w_lo, U)
            sp.sem_inc(stored, 16)
            with sp.Fori(0, NB) as b:
                def unit(k, n):
                    sp.wait_ge(w_lo, UNITS * b + n + 1)
                    sp.dma_start(raw[:, k, :, :].rearrange("p a b -> p (a b)"),
                                 w_units[bass.ds(n, 1)].rearrange("a p n -> p (a n)")).then_inc(raw_in[k], 16)

                sp.wait_ge(ss_done, 2 * b + SS0)
                sp.dma_start(tmp[:, :, :], mixT[:, :, tokens(b)].rearrange("c p s -> p c s")).then_inc(mix_in, 16)
                sp.wait_ge(stored, 16 * b + 16)
                sp.dma_start(acc[:, :, :], xT[:, :, tokens(b)]).then_inc(x_in, 16)
                with sp.Fori(0, UNITS // U) as j:
                    for k in range(U):
                        unit(k, U * j + k)
                sp.wait_ge(out_done, KC * b + KC)
                sp.dma_start(outT[:, :, tokens(b)].rearrange("c p s -> p c s"), acc[:, :, :]).then_inc(stored, 16)
            sp.wait_ge(stored, 16 * NB + 16)

        @block.gpsimd
        def _(pool):
            nc.gpsimd.memset(ones[:, :], 1.0).then_inc(const_set, 1)
            nc.gpsimd.memset(eps_col[:, :], EPS).then_inc(const_set, 1)
            with pool.Fori(0, NB * UNITS // (2 * U)) as i:
                for s in range(2 * U):
                    pool.wait_ge(w_hi, 2 * U * i + s + 1)
                    nc.gpsimd.tensor_tensor(wl[:, s, :, :], raw[:, s % U, :, :], wh[:, s, :, :].bitcast(fp32),
                                            ALU.subtract).then_inc(w_lo, 1)

        @block.scalar
        def _(act):
            act.sem_inc(r_done, R0)
            act.wait_ge(const_set, 2)
            with act.Fori(0, NB) as b:
                def done(kind, g):
                    if kind == "W2":
                        act.wait_ge(y_done, Y_BLK * b + KC * g + KC + Y0)
                    else:
                        act.wait_ge(f_done, F_BLK * b + U * g + U + (2 * U if kind == "W1" else 0))

                def split(seg, half, s):
                    act.wait_ge(raw_in[s], 16 * (SEGS * b + seg) + 16)
                    nc.scalar.activation(wh[:, U * half + s, :, :], raw[:, s, :, :], ACT.Copy).then_inc(w_hi, 1)

                def normalise(second, h_out):
                    for k in range(KC):
                        if second:
                            act.wait_ge(y_add, Y_BLK * b + Y_BLK - KC + k + 1 + 4)
                        else:
                            act.wait_ge(x_done, KC * b + k + 1)
                        if k == 0 and second:
                            act.wait_ge(hl_done, KC * b + KC)
                        if k == 0 and not second:
                            act.wait_ge(ml_done, KC * b + KC)
                        nc.scalar.activation(tmp[:, k, :], acc[:, k, :], ACT.Square).then_inc(sq_done, 1)
                    act.wait_ge(ss_done, 2 * b + (2 if second else 1) + SS0)
                    nc.scalar.activation(rstd[:, :], ps[:, 6, :], ACT.Sqrt, scale=1.0 / D_MODEL,
                                         bias=eps_col[:, :]).then_inc(std_done, 1)
                    if not second:
                        for k in range(KC):
                            act.wait_ge(h_done, KC * b + k + 1)
                            nc.scalar.activation(ah[:, k, :], tmp[:, k, :], ACT.Copy).then_inc(hh_done, 1)

                act.wait_ge(y_done, Y_BLK * b + Y0)
                for s in range(U):
                    split(0, 0, s)
                act.wait_ge(mix_in, 16 * b + 16)
                for k in range(KC):
                    nc.scalar.activation(ah[:, k, :], tmp[:, k, :], ACT.Copy).then_inc(mh_done, 1)

                def segment(kind, g, par, seg, half, nxt):
                    for s in range(U):
                        if nxt:
                            if s == 0 and not (kind == "O" and g == 0):
                                before = {"O": ("O", 0), "W2": ("W1", g + 1)}.get(kind)
                                if kind == "W1":
                                    before = ("O", 1) if isinstance(seg, int) and seg == 2 else ("W2", g - 2)
                                if kind == "W1" and not (isinstance(seg, int) and seg == 2):
                                    act.wait_ge(y_done, Y_BLK * b + KC * g - KC + Y0)
                                    act.wait_ge(f_done, F_BLK * b + 3 * U)
                                else:
                                    done(*before)
                            split(nxt[2], 1 - half, s)
                        if kind == "W1":
                            n = U * g + s
                            act.wait_ge(f_done, F_BLK * b + 2 * U + n + 1)
                            act.wait_ge(tl_done, UW * b + n + 1)
                            nc.scalar.activation(rl[:, s % 2, :], ps[:, s % 2, :], ACT.Relu).then_inc(r_done, 1)
                            act.wait_ge(r_done, UW * b + n + 1 + R0)
                            act.wait_ge(y_done, Y_BLK * b + KC * g - KC + Y0)
                            nc.scalar.activation(th[:, par, s, :], rl[:, s % 2, :], ACT.Square).then_inc(th_done, 1)
                    if isinstance(seg, int) and seg == 1:
                        normalise(False, None)

                UW = NG * U
                segments(act, b, segment)
                normalise(True, None)

        @block.vector
        def _(dve):
            st = Steps(dve, dve_s)
            UW = NG * U
            dve.sem_inc(tl_done, 2)
            dve.sem_inc(y_add, 4)
            dve.wait_ge(const_in, 32)
            with dve.Fori(0, NB) as b:
                st.loop(0, b, 2)
                for k in range(KC):
                    dve.wait_ge(mh_done, KC * b + k + 1)
                    nc.vector.tensor_tensor(al[:, k, :], tmp[:, k, :], ah[:, k, :].bitcast(fp32), ALU.subtract).then_inc(ml_done, 1)

                def segment(kind, g, par, seg, half, nxt):
                    if kind == "O":
                        for s in range(U):
                            k = U * g + s
                            if k == 0:
                                dve.wait_ge(x_in, 16 * b + 16)
                            dve.wait_ge(f_done, F_BLK * b + k + 1)
                            nc.vector.tensor_tensor(acc[:, k, :], acc[:, k, :], ps[:, s % 2, :], ALU.add).then_inc(x_done, 1)
                        if g == 1:
                            dve.wait_ge(std_done, 2 * b + 1)
                            st.do(nc.vector.reciprocal(rstd[:, :], rstd[:, :]))
                            for k in range(KC):
                                nc.vector.scalar_tensor_tensor(out=tmp[:, k, :], in0=acc[:, k, :], scalar=gf[:, k:k + 1],
                                                               in1=rstd[:, :], op0=ALU.mult, op1=ALU.mult).then_inc(h_done, 1)
                            for k in range(KC):
                                dve.wait_ge(hh_done, KC * b + k + 1)
                                nc.vector.tensor_tensor(al[:, k, :], tmp[:, k, :], ah[:, k, :].bitcast(fp32),
                                                        ALU.subtract).then_inc(hl_done, 1)
                    elif kind == "W1":
                        for s in range(U):
                            n = U * g + s
                            dve.wait_ge(r_done, UW * b + n + 1 + R0)
                            nc.vector.tensor_tensor(r2[:, s % 2, :], rl[:, s % 2, :], rl[:, s % 2, :], ALU.mult).then_inc(r2_done, 1)
                            dve.wait_ge(th_done, UW * b + n + 1)
                            dve.wait_ge(r2_done, UW * b + n + 1)
                            nc.vector.tensor_tensor(tl[:, par, s, :], r2[:, s % 2, :], th[:, par, s, :].bitcast(fp32),
                                                    ALU.subtract).then_inc(tl_done, 1)
                    else:
                        for k in range(KC):
                            dve.wait_ge(y_done, Y_BLK * b + KC * g + k + 1 + Y0)
                            nc.vector.tensor_tensor(acc[:, k, :], acc[:, k, :], ps[:, 2 + k % 4, :], ALU.add).then_inc(y_add, 1)

                segments(dve, b, segment)
                dve.wait_ge(std_done, 2 * b + 2)
                st.do(nc.vector.reciprocal(rstd[:, :], rstd[:, :]))
                for k in range(KC):
                    nc.vector.scalar_tensor_tensor(out=acc[:, k, :], in0=acc[:, k, :], scalar=gl[:, k:k + 1],
                                                   in1=rstd[:, :], op0=ALU.mult, op1=ALU.mult).then_inc(out_done, 1)
            st.leave(NB)

        @block.tensor
        def _(pe):
            UW = NG * U
            pe.sem_inc(y_done, Y0)
            pe.sem_inc(ss_done, SS0)
            pe.wait_ge(const_set, 2)
            with pe.Fori(0, NB) as b:
                def sum_squares(first):
                    for k in range(KC):
                        pe.wait_ge(sq_done, 2 * KC * b + k + 1 + (0 if first else KC))
                        last = nc.tensor.matmul(ps[:, 6, :], ones[:, :], tmp[:, k, :], start=(k == 0), stop=(k == KC - 1))
                    last.then_inc(ss_done, 1)

                def three(dst, hi, lo, rh, rl_, first, last):
                    nc.tensor.matmul(dst, hi, rh, start=first, stop=False)
                    nc.tensor.matmul(dst, hi, rl_, start=False, stop=False)
                    return nc.tensor.matmul(dst, lo, rh, start=False, stop=last)

                def segment(kind, g, par, seg, half, nxt):
                    if kind != "W2":
                        for s in range(U):
                            pe.wait_ge(w_lo, UNITS * b + U * seg + s + 1 + U)
                            if kind == "O":
                                if g == 0 and s == 0:
                                    pe.wait_ge(r_done, UW * b + R0)
                                    pe.wait_ge(ml_done, KC * b + KC)
                                if g or s >= 2:
                                    pe.wait_ge(x_done, KC * b + U * g + s - 1)
                            elif isinstance(seg, int) and seg == 2 and s < 2:
                                pe.wait_ge(x_done, KC * b + KC)
                                pe.wait_ge(hl_done, KC * b + KC)
                            else:
                                pe.wait_ge(r_done, UW * b + U * g + s - 1 + R0)
                            for k in range(KC):
                                last = three(ps[:, s % 2, :], wh[:, U * half + s, k, :], wl[:, U * half + s, k, :],
                                             ah[:, k, :], al[:, k, :], k == 0, k == KC - 1)
                            last.then_inc(f_done, 1)
                        if isinstance(seg, int) and seg == 1:
                            sum_squares(True)
                    else:
                        pe.wait_ge(w_lo, UNITS * b + U * seg + U + U)
                        pe.wait_ge(tl_done, UW * b + U * g + U + 2)
                        for k in range(KC):
                            pe.wait_ge(y_add, Y_BLK * b + KC * g + k + 1)
                            for s in range(U):
                                last = three(ps[:, 2 + k % 4, :], wh[:, U * half + s, k, :], wl[:, U * half + s, k, :],
                                             th[:, par, s, :], tl[:, par, s, :], s == 0, s == U - 1)
                            last.then_inc(y_done, 1)

                segments(pe, b, segment)
                sum_squares(False)


def program(nc, S, a, projT, biasT, mixT, outT):
    norm_and_projection(nc, S, a["xT"], a["g_mix"], a["conv_w"], a["w_proj"], projT)
    topk = min(TOPK_MAX, S // 4)
    deltanet_and_selection(nc, S, topk, projT, a["a_log"], a["dt_bias"], a["g_gdn"], a, mixT, biasT)
    indexed_attention(nc, S, topk, projT, a, biasT, mixT)
    output_and_mlp(nc, S, a["xT"], mixT, a["w_units"], a["g_ffn"], a["g_final"], outT)


def shape_constants(S):
    i = np.arange(P)
    f = lambda m: np.ascontiguousarray(m.astype(np.float32))
    same = (i[:, None] // 16) == (i[None, :] // 16)
    half = HD // 2
    inv = (1.0 / (np.float32(10000.0) ** (np.arange(half, dtype=np.float32) / np.float32(half)))).astype(np.float32)
    ang = np.arange(S, dtype=np.float32)[None, :] * inv[i % half][:, None]
    sign = np.where(i % HD < half, -1.0, 1.0).astype(np.float32)[:, None]
    return {
        "ident": f(np.eye(P)), "triu": f(i[:, None] <= i[None, :]), "incl": f(i[:, None] >= i[None, :]),
        "strict": f(i[:, None] > i[None, :]), "diag16": f(same), "off16": f(~same),
        "cosT": f(np.cos(ang)), "sinT": f(np.sin(ang) * sign),
    }


def proj_columns():
    sizes = [A_HEADS * HD, KV_HEADS * HD, KV_HEADS * HD, IDX_HEADS * HD, HD, IDX_HEADS] + [B_HEADS * BD] * 4 + [B_HEADS] * 2
    off = np.concatenate([[0], np.cumsum(sizes)])
    qa, ka, va, qi, ki, wi, qb, kb, vb, zb, bb, ab = [list(range(off[n], off[n + 1])) for n in range(len(sizes))]
    small = wi + bb + ab
    return small + [-1] * (P - HD - len(small)) + ki + qi + qa + ka + va + qb + kb + vb + zb


def weight_units(w_out, w_ff1, w_ff2):
    by_output = lambda w: w.reshape(KC, P, -1, P).transpose(2, 1, 0, 3).reshape(-1, P, KC * P)
    o, w1 = by_output(w_out), by_output(w_ff1)
    w2 = w_ff2.reshape(-1, P, D_MODEL)
    n = D_FF // 512
    part = lambda w, g: w[4 * g:4 * g + 4]
    seq = [o, part(w1, 0)]
    for g in range(1, n):
        seq += [part(w1, g), part(w2, g - 1)]
    return np.ascontiguousarray(np.concatenate(seq + [part(w2, n - 1)]))


def host_layout(d):
    x = d["x"][0]
    S = x.shape[0]
    cols = np.array(proj_columns())
    w = np.zeros((D_MODEL, (N_CHUNK + 1) * P), np.float32)
    w[:, :len(cols)] = np.where(cols >= 0, d["w_in"][0][:, cols], np.float32(0))
    chunks = lambda a: np.ascontiguousarray(a.reshape(KC, P, -1, P).transpose(2, 1, 0, 3))
    col = lambda g: np.ascontiguousarray(g.reshape(-1, P).T)
    return {
        "xT": np.ascontiguousarray(x.T.reshape(KC, P, S).transpose(1, 0, 2)),
        "g_mix": col(d["norm_mix_g"][0]),
        "conv_w": np.ascontiguousarray(d["conv_w"][0].reshape(CONV, N_CONV, P).transpose(2, 1, 0)),
        "w_proj": chunks(w),
        "w_units": weight_units(d["w_out"][0], d["w_ff1"][0], d["w_ff2"][0]),
        "g_ffn": col(d["norm_ffn_g"][0]), "g_final": col(d["norm_final_g"]),
        "a_log": d["a_log"][0:1], "dt_bias": d["dt_bias"][0:1], "g_gdn": col(d["gdn_norm_g"][0]),
    }


_OUT = "out_dram"


def kernel(**inputs):
    import concourse.bacc as bacc
    from concourse.bass_utils import run_bass_kernel_spmd

    d = {k: np.asarray(v) for k, v in inputs.items()}
    S = d["x"].shape[1]
    arrays = {**host_layout(d), **shape_constants(S)}
    arrays = {k: np.ascontiguousarray(v) for k, v in arrays.items()}
    nc = bacc.Bacc("TRN2", target_bir_lowering=False, num_devices=1)
    a = {n: nc.dram_tensor(n, v.shape, fp32, kind="ExternalInput").ap() for n, v in arrays.items()}
    projT = nc.dram_tensor("projT", (N_CHUNK, P, S), fp32, kind="Internal").ap()
    biasT = nc.dram_tensor("biasT", (S // P, P, S), fp32, kind="Internal").ap()
    mixT = nc.dram_tensor("mixT", (KC, P, S), fp32, kind="Internal").ap()
    outT = nc.dram_tensor(_OUT, (KC, P, S), fp32, kind="ExternalOutput").ap()
    program(nc, S, a, projT, biasT, mixT, outT)
    r = run_bass_kernel_spmd(nc, [arrays], core_ids=[0])
    out = r.results[0][_OUT].reshape(D_MODEL, S)
    return np.ascontiguousarray(out.T)[None]
```

```python
import numpy as np
import concourse.bass as bass
from concourse import mybir
from contextlib import ExitStack

fp32 = mybir.dt.float32
f32r = mybir.dt.float32r
i32 = mybir.dt.int32
ALU = mybir.AluOpType
ACT = mybir.ActivationFunctionType

P = 128
D_MODEL, D_FF = 1024, 4096
KC = D_MODEL // P
A_HEADS, KV_HEADS, HD = 8, 2, 64
IDX_HEADS = 8
B_HEADS, BD = 4, 128
CONV = 4
TOPK_MAX, CHUNK = 256, 64
EPS = 1e-6
C_SMALL, C_QI, C_QA, C_KA, C_VA, C_CONV, C_Z, N_CHUNK = 0, 1, 5, 9, 10, 11, 23, 27
N_CONV = C_Z - C_CONV
HALO = 4
BARRED = -2.0e38
MASK_BIAS = -1.0e38


class Steps:

    def __init__(self, eng, sem):
        self.eng, self.sem, self.base, self.n = eng, sem, 0, 0

    def do(self, ins):
        ins.then_inc(self.sem, 1)
        self.n += 1
        self.eng.wait_ge(self.sem, self.base + self.n)

    def loop(self, done, i, per):
        self.base, self.n, self.at = i * per + done, 0, (done, per)

    def leave(self, turns):
        done, per = self.at
        assert self.n == per, self.n
        self.base, self.n = 0, done + per * turns


def norm_and_projection(nc, S, xT, g_mix, conv_w, w_proj, projT):
    XB = 256
    NX, NB = S // XB, S // 512
    with ExitStack() as ctx:
        sb = lambda n, s, d=fp32: ctx.enter_context(nc.sbuf_tensor(n, s, d))
        sem = lambda n: ctx.enter_context(nc.semaphore(n))
        xh = sb("xh", [P, KC, S], f32r)
        xl = sb("xl", [P, KC, S], f32r)
        work = sb("work", [P, 8192])
        xb = work[:, 0:4096].rearrange("p (u k s) -> p u k s", u=2, k=KC)
        xsq = work[:, 4096:6144].rearrange("p (k s) -> p k s", k=KC)
        xn = work[:, 6144:8192].rearrange("p (k s) -> p k s", k=KC)
        conv_acc = work[:, 0:2 * S].rearrange("p (u s) -> p u s", u=2)
        conv_out = work[:, 2 * S:4 * S].rearrange("p (u s) -> p u s", u=2)
        rstd = sb("rstd", [P, XB])
        ones = sb("ones", [P, P])
        gm = sb("gm", [P, KC])
        eps_col = sb("eps_col", [P, 1])
        cw = sb("cw", [P, N_CONV, CONV])
        wraw = sb("wraw", [P, 2, KC, P])
        wh = sb("wh", [P, 2, KC, P], f32r)
        wl = sb("wl", [P, 2, KC, P], f32r)
        stage = sb("stage", [P, 2, HALO + S])
        ps = ctx.enter_context(nc.psum_tensor("ps", [P, 8, 512], fp32))
        const_in, const_set = sem("const_in"), sem("const_set")
        pair = lambda n: [sem(f"{n}{u}") for u in range(2)]
        x_in, w_in, plain_out, conv_stored, z_out = map(pair, ["x_in", "w_in", "plain_out", "conv_stored", "z_out"])
        sq_done, ss_done, std_done, xn_done, xh_done, xl_done = map(
            sem, ["sq_done", "ss_done", "std_done", "xn_done", "xh_done", "xl_done"])
        w_hi, w_lo = map(sem, ["w_hi", "w_lo"])
        acc_done, evac_done = map(sem, ["acc_done", "evac_done"])
        conv_done, silu_done = map(sem, ["conv_done", "silu_done"])
        dve_s = sem("dve_s")
        N_PLAIN, N_Z = C_CONV, N_CHUNK - C_Z
        block = ctx.enter_context(nc.Block())

        @block.sync
        def _(sp):
            for stored in plain_out + conv_stored + z_out:
                sp.sem_inc(stored, 16)
            sp.dma_start(gm[:, :], g_mix).then_inc(const_in, 16)
            sp.dma_start(cw[:, :, :], conv_w).then_inc(const_in, 16)
            with sp.Fori(0, NX // 2) as i:
                for u in range(2):
                    sp.wait_ge(xl_done, 2 * i + u + 1)
                    sp.dma_start(xb[:, u, :, :], xT[:, :, bass.ds(i * 2 * XB + u * XB, XB)]).then_inc(x_in[u], 16)
            with sp.Fori(0, (N_CHUNK + 1) // 2) as i:
                for u in range(2):
                    sp.wait_ge(w_lo, 2 * i + u + 1)
                    sp.dma_start(wraw[:, u, :, :], w_proj[bass.ds(2 * i + u, 1)].rearrange(
                        "a p k n -> p (a k) n")).then_inc(w_in[u], 16)

        @block.gpsimd
        def _(pool):
            pool.sem_inc(w_lo, 2)
            nc.gpsimd.memset(ones[:, :], 1.0).then_inc(const_set, 1)
            nc.gpsimd.memset(stage[:, :, 0:HALO], 0.0).then_inc(const_set, 1)
            nc.gpsimd.memset(eps_col[:, :], EPS).then_inc(const_set, 1)
            with pool.Fori(0, (N_CHUNK + 1) // 2) as i:
                for u in range(2):
                    c = 2 * i + u
                    pool.wait_ge(w_hi, c + 1)
                    pool.wait_ge(acc_done, NB * c + NB)
                    nc.gpsimd.tensor_tensor(wl[:, u, :, :], wraw[:, u, :, :], wh[:, u, :, :].bitcast(fp32),
                                            ALU.subtract).then_inc(w_lo, 1)

        @block.vector
        def _(dve):
            st = Steps(dve, dve_s)
            dve.sem_inc(xl_done, 2)
            dve.wait_ge(const_in, 32)
            with dve.Fori(0, NX // 2) as i:
                st.loop(0, i, 2)
                for u in range(2):
                    b = 2 * i + u
                    tok = bass.ds(i * 2 * XB + u * XB, XB)
                    dve.wait_ge(std_done, b + 1)
                    st.do(nc.vector.reciprocal(rstd[:, :], rstd[:, :]))
                    for k in range(KC):
                        last = nc.vector.scalar_tensor_tensor(
                            out=xn[:, k, :], in0=xb[:, u, k, :], scalar=gm[:, k:k + 1], in1=rstd[:, :],
                            op0=ALU.mult, op1=ALU.mult)
                    last.then_inc(xn_done, 1)
                    dve.wait_ge(xh_done, b + 1)
                    nc.vector.tensor_tensor(xl[:, :, tok], xn[:, :, :], xh[:, :, tok].bitcast(fp32),
                                            ALU.subtract).then_inc(xl_done, 1)
                    dve.wait_ge(xl_done, b + 3)
            st.leave(NX // 2)
            done = st.n
            with dve.Fori(0, N_CONV // 2) as i:
                st.loop(done, i, 2 * (CONV - 1))
                for v in range(2):
                    k, u = 2 * i + v, (C_CONV + v) % 2
                    dve.wait_ge(evac_done, NB * k + NB * (C_CONV + 3))
                    dve.wait_ge(silu_done, k + 1)
                    st.do(nc.vector.tensor_scalar(conv_acc[:, u, :], stage[:, u, 1:1 + S],
                                                  cw[:, bass.ds(k, 1), 0:1].rearrange("p a b -> p (a b)"),
                                                  None, ALU.mult))
                    for j in range(1, CONV):
                        ins = nc.vector.scalar_tensor_tensor(
                            out=conv_acc[:, u, :], in0=stage[:, u, 1 + j:1 + j + S],
                            scalar=cw[:, bass.ds(k, 1), j:j + 1].rearrange("p a b -> p (a b)"),
                            in1=conv_acc[:, u, :], op0=ALU.mult, op1=ALU.add)
                        if j < CONV - 1:
                            st.do(ins)
                        else:
                            ins.then_inc(conv_done, 1)
            st.leave(N_CONV // 2)

        @block.scalar
        def _(act):
            act.sem_inc(evac_done, 2 * NB)
            act.sem_inc(conv_done, 2)
            act.sem_inc(silu_done, 2)
            with act.Fori(0, NX // 2) as i:
                for u in range(2):
                    b = 2 * i + u
                    act.wait_ge(x_in[u], 16 * i + 16)
                    nc.scalar.activation(xsq[:, :, :], xb[:, u, :, :], ACT.Square).then_inc(sq_done, 1)
                    act.wait_ge(ss_done, b + 1)
                    nc.scalar.activation(rstd[:, :], ps[:, 7, 0:XB], ACT.Sqrt, scale=1.0 / D_MODEL,
                                         bias=eps_col[:, :]).then_inc(std_done, 1)
                    act.wait_ge(xn_done, b + 1)
                    nc.scalar.activation(xh[:, :, bass.ds(i * 2 * XB + u * XB, XB)], xn[:, :, :],
                                         ACT.Copy).then_inc(xh_done, 1)

            def split_hi(c, turn, u):
                act.wait_ge(w_in[u], 16 * turn + 16)
                act.wait_ge(acc_done, NB * c + NB)
                nc.scalar.activation(wh[:, u, :, :], wraw[:, u, :, :], ACT.Copy).then_inc(w_hi, 1)

            def chunk(kind, c, turn, k, kturn, u):
                split_hi(c + 1, turn + u, 1 - u)
                if kind == "plain":
                    act.wait_ge(plain_out[u], 16 * kturn + 16)
                elif kind == "conv":
                    act.wait_ge(plain_out[u], 16 * ((N_PLAIN + 1 - u) // 2) + 16)
                    act.wait_ge(conv_done, k + 1)
                else:
                    act.wait_ge(z_out[u], 16 * kturn + 16)
                for tb in range(NB):
                    act.wait_ge(acc_done, NB * c + tb + 1 + 2 * NB)
                    nc.scalar.activation(stage[:, u, HALO + 512 * tb:HALO + 512 * (tb + 1)], ps[:, NB * u + tb, :],
                                         ACT.Silu if kind == "z" else ACT.Copy).then_inc(evac_done, 1)
                if kind == "conv":
                    act.wait_ge(conv_done, k + 3)
                    act.wait_ge(conv_stored[u], 16 * kturn + 16)
                    nc.scalar.activation(conv_out[:, u, :], conv_acc[:, u, :], ACT.Silu).then_inc(silu_done, 1)
                    act.wait_ge(silu_done, k + 3)
                    src, stored = conv_out[:, u, :], conv_stored
                else:
                    act.wait_ge(evac_done, NB * c + 3 * NB)
                    src, stored = stage[:, u, HALO:HALO + S], plain_out if kind == "plain" else z_out
                act.dma_start(projT[bass.ds(c, 1)].rearrange("a p s -> p (a s)"), src).then_inc(stored[u], 16)

            split_hi(0, 0, 0)
            chunk("plain", 0, 0, 0, 0, 0)
            for kind, first, n in (("plain", 1, N_PLAIN - 1), ("conv", C_CONV, N_CONV), ("z", C_Z, N_Z)):
                with act.Fori(0, n // 2) as i:
                    for v, u in ((0, 1), (1, 0)):
                        k = 2 * i + v + (1 if kind == "plain" else 0)
                        chunk(kind, 2 * i + (first + v), i + (first + v) // 2, k, i + (v if kind == "plain" else 0), u)
            for u in range(2):
                act.wait_ge(plain_out[u], 16 * ((N_PLAIN + 1 - u) // 2) + 16)
                act.wait_ge(conv_stored[u], 16 * (N_CONV // 2) + 16)
                act.wait_ge(z_out[u], 16 * (N_Z // 2) + 16)

        @block.tensor
        def _(pe):
            pe.sem_inc(acc_done, 2 * NB)
            pe.wait_ge(const_set, 3)
            with pe.Fori(0, NX) as i:
                pe.wait_ge(sq_done, i + 1)
                for k in range(KC):
                    last = nc.tensor.matmul(ps[:, 7, 0:XB], ones[:, :], xsq[:, k, :], start=(k == 0), stop=(k == KC - 1))
                last.then_inc(ss_done, 1)
            pe.wait_ge(xl_done, NX + 2)

            def project(c, u):
                pe.wait_ge(w_lo, c + 3)
                for tb in range(NB):
                    pe.wait_ge(evac_done, NB * c + tb + 1)
                    tok = slice(512 * tb, 512 * (tb + 1))
                    for kc in range(KC):
                        acc = ps[:, NB * u + tb, :]
                        nc.tensor.matmul(acc, wh[:, u, kc, :], xh[:, kc, tok], start=(kc == 0), stop=False)
                        nc.tensor.matmul(acc, wh[:, u, kc, :], xl[:, kc, tok], start=False, stop=False)
                        last = nc.tensor.matmul(acc, wl[:, u, kc, :], xh[:, kc, tok], start=False, stop=(kc == KC - 1))
                    last.then_inc(acc_done, 1)

            with pe.Fori(0, N_CHUNK // 2) as i:
                for u in range(2):
                    project(2 * i + u, u)
            project(N_CHUNK - 1, 0)


R_W, R_B, R_A = 0, IDX_HEADS, IDX_HEADS + B_HEADS
N_SMALL = IDX_HEADS + 2 * B_HEADS


ROUND = "b0 f0 b1 f1 b2 f2 b3 f3 b4 b5 f4 b6 f5 b7 f6 b8 b9 f7 b10 b11 b12".split()
STAGES = len(ROUND)
SPARE = [1.0 if s[0] == "b" else 0.4 for s in ROUND]
BUSY_POOL = ("b0", "f3", "f5")
BITS = 31
RELUS = 4


class SelectionPlan:

    def __init__(self, S, topk):
        NT = S // P
        end = STAGES * NT
        self.tiles = [t for t in range(NT) if (t + 1) * P > topk]
        assert all(t * P + CHUNK >= topk for t in self.tiles)
        self.parts = {}
        self.number, acc_slot, relu_slot, score_slot = {}, [], [], []
        cost = lambda j, k: (500 + 1.05 * (j + 1) * P) * (1 if 1 <= k <= BITS else 2)
        pieces = lambda j: [(h, x) for h in range(IDX_HEADS) for x in range(0, (j + 1) * P, 512)]
        total = sum(sum(cost(j, k) for k in range(BITS + 4)) + 600 * len(pieces(j)) for j in self.tiles)
        slot = 16
        rate = total / sum(SPARE[s % STAGES] for s in range(slot, end - 2))
        ahead = [0.0]

        def dve(slot, part, cost):
            while ahead[0] + cost / 2 > 0 and slot < end - 1:
                slot += 1
                ahead[0] -= rate * SPARE[slot % STAGES]
            ahead[0] += cost
            self.put("dve", slot, part)
            return slot

        q_slot = self.rotation(self.tiles[0], 10)
        for i, j in enumerate(self.tiles):
            slot = max(slot, q_slot + 1)
            ready = q_slot
            if i + 1 < len(self.tiles):
                q_slot = self.rotation(self.tiles[i + 1], slot)
            for h, x in pieces(j):
                slot = dve(slot, ("acc", j, h, x), 600)
                n = len(acc_slot)
                acc_slot.append(slot)
                relu_slot.append(max(ready, slot - 3, acc_slot[n - RELUS] if n >= RELUS else 0))
                score_slot.append(max(ready, relu_slot[n] - 2, relu_slot[n - 2] if n >= 2 else 0))
                self.number[j, h, x] = n + 1
                self.put("act", relu_slot[n], ("relu", j, h, x))
                self.put("pe", score_slot[n], ("scores", j, h, x))
            for k in range(BITS + 4):
                slot = dve(slot, ("select", j, k), cost(j, k))
            self.put("sp", slot, ("store", j))

    def rotation(self, j, slot):
        self.put("sp", slot, ("load", j))
        slot += 1
        for k in range(4):
            while ROUND[slot % STAGES] in BUSY_POOL:
                slot += 1
            if k == 3:
                self.put("act", slot, ("round", j))
            self.put("pool", slot, ("rotate", j, k))
            slot += 1
        return slot - 1

    def put(self, eng, slot, part):
        self.parts.setdefault((eng, slot), []).append(part)

    def at(self, eng, t, m):
        return self.parts.get((eng, STAGES * t + m), [])


def rotated_rows(eng, a, b, src, sem_in):
    half = HD // 2
    for base in (0, HD):
        eng.dma_start(a[base:base + HD], src).then_inc(sem_in, 16)
        eng.dma_start(b[base:base + half], src[half:HD]).then_inc(sem_in, 16)
        eng.dma_start(b[base + half:base + HD], src[0:half]).then_inc(sem_in, 16)


def deltanet_and_selection(nc, S, topk, projT, a_log, dt_bias, g_gdn, consts, mixT, biasT):
    NT = S // P
    H, W = B_HEADS, B_HEADS * P
    QK = float(BD) ** -0.5
    plan = SelectionPlan(S, topk)
    with ExitStack() as ctx:
        sb = lambda n, s, d=fp32: ctx.enter_context(nc.sbuf_tensor(n, s, d))
        sem = lambda n: ctx.enter_context(nc.semaphore(n))
        ident = sb("g_ident", [P, P])
        triu = sb("g_triu", [P, P])
        ones = sb("g_ones", [P, P])
        incl = sb("g_incl", [P, P])
        strict = sb("g_strict", [P, P])
        diag16 = sb("g_diag16", [P, P])
        off16 = sb("g_off16", [P, P])
        small = sb("g_small", [N_SMALL, S])
        cosT, sinT = sb("i_cos", [P, S]), sb("i_sin", [P, S])
        ikeys = sb("i_keys", [P, S], f32r)
        rot = sb("i_rot", [P, 2, IDX_HEADS, P])
        q_hi, q_lo = sb("i_qhi", [P, 2, IDX_HEADS, P], f32r), sb("i_qlo", [P, 2, IDX_HEADS, P], f32r)
        w_idx = sb("i_w", [P, NT, IDX_HEADS])
        relu = sb("i_relu", [P, RELUS, 512])
        score, left, bias = sb("i_score", [P, S]), sb("i_left", [P, S]), sb("i_bias", [P, S])
        count, bound, sign, value, room = [sb("i_" + n, [P, 1]) for n in "count bound sign value room".split()]
        trial, drop = sb("i_trial", [P, 1], i32), sb("i_drop", [P, 1], i32)
        eps_col = sb("g_eps", [P, 1])
        ln_qk = sb("g_ln_qk", [P, 1])
        one_col = sb("g_one", [P, 1])
        alog = sb("g_alog", [P, H])
        dtb = sb("g_dtb", [P, H])
        gg = sb("g_gg", [P, 1])
        sm = sb("g_sm", [P, NT, N_SMALL])
        beta = sb("g_beta", [P, NT, H])
        gate = sb("g_gate", [P, NT, H])
        sp_a = sb("g_spa", [P, NT, H])
        sp_b = sb("g_spb", [P, NT, H])
        gcum = sb("g_gcum", [P, NT, H])
        egc = sb("g_egc", [P, NT, H])
        nbeg = sb("g_nbeg", [P, NT, H])
        qkvz = sb("g_qkvz", [P, 2, 4, H, P])
        sq = sb("g_sq", [P, 2, H, P])
        rn = sq
        qk = sb("g_qk", [P, 2, H, P])
        big = {n: sb("g_" + n, [P, H, P]) for n in
               "G X Dq Ds N at m n L Y n2 m2 n4 m4 n8 Dinv E F E2 F2 E4 Z wT vnew osq".split()}
        B = lambda n: big[n][:, :, :]
        two = {n: sb("g_" + n, [P, 2, H, P]) for n in "EG LT attT kt kbe vb qd".split()}
        T = lambda n, t: two[n][:, t % 2, :, :]
        out_b = sb("g_out", [P, 2, H, P])
        st_S = sb("g_state", [P, H, P])
        tail = sb("g_tail", [P, H])
        etail = sb("g_etail", [P, H])
        ps = ctx.enter_context(nc.psum_tensor("g_ps", [P, 6, H, P], fp32))
        ips = ctx.enter_context(nc.psum_tensor("i_ps", [P, 2, 512], fp32))
        BANK = {n: i % 3 for i, n in enumerate("ssq ssk gb kk att NT atT kT vT n2 m2".split())}
        BANK |= {n: 3 + i % 3 for i, n in enumerate(
            "n4 m4 Y1 n8 Y2 Y3 Dinv E F Z1 E2 F2 Z2 E4 Z3 wT vnew out state oss".split())}
        bank = lambda n: ps[:, BANK[n], :, :]
        const_in, const_set = sem("g_const_in"), sem("g_const_set")
        load = [sem(f"g_load{u}") for u in range(2)]
        stored = [sem(f"g_stored{u}") for u in range(2)]
        done = {e: [sem(f"g_{e}_{part}") for part in ("front", "back")] for e in ("pe", "dve", "act", "pool")}
        z_in = [sem(f"g_z_in{u}") for u in range(2)]
        sel_s, key_in, key_mul, key_hi, key_done, w_done = map(sem, "i_sel i_key_in i_key_mul i_key_hi i_key_done i_w_done".split())
        q_in, q_mul, q_rot, q_hid, q_lod = map(sem, "i_q_in i_q_mul i_q_rot i_q_hid i_q_lod".split())
        scored, relu_done, acc_done, selected, bias_stored = map(sem, "i_scored i_relu i_acc i_selected i_stored".split())
        dve_s, act_s, pool_s, pe_s = sem("g_dve"), sem("g_act"), sem("g_pool"), sem("g_pe")
        block = ctx.enter_context(nc.Block())
        ph = lambda a: a.rearrange("p a b -> p (a b)")
        bc = lambda m: m[:, :].unsqueeze(1).to_broadcast([P, H, P])

        count_of = lambda names: {n: i + 1 for i, n in enumerate(names.split())}
        FRONT = {"pe": count_of("ss gb kk att tr kT vT n2 m2"), "dve": count_of("qk X tail N at m LT kt kbe vb"),
                 "act": count_of("sq ln rnq rnk EG D etail attT n2 m2"), "pool": count_of("G X Dq Ds qd n L")}
        BACK = {"pe": count_of("n4 m4 Y1 n8 Y2 Y3 Dinv E F Z1 E2 F2 Z2 E4 Z3 wT vnew out state oss"),
                "dve": count_of("Y1 Y2 Y3 Z1 Z2 Z3 S otmp"), "act": count_of("n4 m4 n8 Dinv E F E2 F2 E4 wT vnew osq oln orn"),
                "pool": count_of("Y out")}

        def waits(eng, t, part):
            names = (FRONT, BACK)[part]
            wait = lambda e: lambda n: eng.wait_ge(done[e][part], len(names[e]) * t + names[e][n])
            return wait("pe"), wait("dve"), wait("act"), wait("pool")

        def run_turns(selection, front, back):
            for s in [s for s in ROUND if s[0] == "f"]:
                front(0, s)
            for t in range(NT):
                for m, s in enumerate(ROUND):
                    selection(t, m)
                    if s[0] == "b":
                        back(t, s)
                    elif t + 1 < NT:
                        front(t + 1, s)

        order = {j: i for i, j in enumerate(plan.tiles)}
        last_piece = lambda j: plan.number[j, IDX_HEADS - 1, (j + 1) * P - ((j + 1) * P - 1) % 512 - 1]
        KEY_STAGE = {2 + 4 * k: k for k in range(-(-S // 1024))}
        KP = min(S, 1024)
        flat = lambda k: rot[:, k].rearrange("p a b -> p (a b)")[:, 0:KP]
        rows = projT.rearrange("c p s -> (c p) s")
        tokens = lambda t: slice(t * P, (t + 1) * P)
        width = lambda j, x: min(512, (j + 1) * P - x)

        @block.sync
        def _(sp):
            for dst, src in ((ident[:, :], consts["ident"]), (triu[:, :], consts["triu"]), (incl[:, :], consts["incl"]),
                             (strict[:, :], consts["strict"]), (diag16[:, :], consts["diag16"]), (off16[:, :], consts["off16"]),
                             (small[:, :], projT[0, 0:N_SMALL, :]), (alog[:, :], a_log.to_broadcast([P, H])),
                             (dtb[:, :], dt_bias.to_broadcast([P, H])), (gg[:, :], g_gdn)):
                sp.dma_start(dst, src).then_inc(const_in, 16)

            def load_tile(t, first, last, sems):
                sp.dma_start(qkvz[:, t % 2, first:last, :, :].rearrange("p a h s -> p (a h) s"),
                             projT[C_CONV + H * first:C_CONV + H * last, :, tokens(t)].rearrange("c p s -> p c s")
                             ).then_inc(sems[t % 2], 16)

            for t in range(2):
                load_tile(t, 0, 3, load)
                load_tile(t, 3, 4, z_in)
            sp.dma_start(cosT[:, :], consts["cosT"]).then_inc(key_in, 16)
            sp.dma_start(sinT[:, :], consts["sinT"]).then_inc(key_in, 16)
            for n in range(S // KP):
                if n:
                    sp.wait_ge(key_done, n)
                row = C_SMALL * P + HD
                rotated_rows(sp, flat(0), flat(1), rows[row:row + HD, n * KP:(n + 1) * KP], key_in)

            def selection(t, m):
                for kind, j in plan.at("sp", t, m):
                    if kind == "load":
                        if order[j]:
                            sp.wait_ge(q_lod, order[j])
                        else:
                            sp.wait_ge(key_done, S // KP)
                        rotated_rows(sp, rot[:, 0], rot[:, 1], rows[C_QI * P:C_QI * P + IDX_HEADS * HD, tokens(j)]
                                     .rearrange("(h r) s -> r h s", r=HD), q_in)
                    else:
                        sp.wait_ge(selected, order[j] + 1)
                        sp.dma_start(biasT[j, :, 0:(j + 1) * P], bias[:, 0:(j + 1) * P]).then_inc(bias_stored, 16)

            for t in range(NT):
                if t + 2 < NT:
                    waits(sp, t, 0)[0]("vT")
                    waits(sp, t, 0)[1]("qk")
                    load_tile(t + 2, 0, 3, load)
                for m in range(STAGES):
                    selection(t, m)
                waits(sp, t, 1)[3]("out")
                sp.dma_start(mixT[4:8, :, tokens(t)].rearrange("c p s -> p c s"), out_b[:, t % 2, :, :]).then_inc(stored[t % 2], 16)
                if t + 2 < NT:
                    load_tile(t + 2, 3, 4, z_in)
            for u in range(2):
                sp.wait_ge(stored[u], 16 * (NT // 2))
            sp.wait_ge(bias_stored, 16 * len(plan.tiles))

        @block.gpsimd
        def _(pool):
            nc.gpsimd.memset(ones[:, :], 1.0).then_inc(const_set, 1)
            nc.gpsimd.memset(eps_col[:, :], EPS).then_inc(const_set, 1)
            nc.gpsimd.memset(one_col[:, :], 1.0).then_inc(const_set, 1)
            nc.gpsimd.memset(ln_qk[:, :], float(np.log(QK))).then_inc(const_set, 1)
            nc.gpsimd.memset(st_S[:, :, :], 0.0).then_inc(const_set, 1)
            pool.wait_ge(const_in, 160)
            pool.wait_ge(dve_s, 7)

            def selection(t, m):
                for _, j, k in plan.at("pool", t, m):
                    i = order[j]
                    table = lambda tab: tab[:, tokens(j)].unsqueeze(1).to_broadcast([P, IDX_HEADS, P])
                    if k == 0:
                        pool.wait_ge(q_in, 96 * (i + 1))
                        nc.gpsimd.tensor_tensor(rot[:, 0], rot[:, 0], table(cosT), ALU.mult).then_inc(q_mul, 1)
                    elif k == 1:
                        nc.gpsimd.tensor_tensor(rot[:, 1], rot[:, 1], table(sinT), ALU.mult).then_inc(q_mul, 1)
                    elif k == 2:
                        pool.wait_ge(q_mul, 2 * (i + 1))
                        nc.gpsimd.tensor_tensor(rot[:, 0], rot[:, 0], rot[:, 1], ALU.add).then_inc(q_rot, 1)
                    else:
                        pool.wait_ge(q_hid, i + 1)
                        nc.gpsimd.tensor_tensor(q_lo[:, i % 2], rot[:, 0], q_hi[:, i % 2].bitcast(fp32),
                                                ALU.subtract).then_inc(q_lod, 1)

            def front(t, s):
                pe, dv, ac, po = waits(pool, t, 0)
                step = lambda ins: ins.then_inc(done["pool"][0], 1)
                if s == "f0":
                    step(nc.gpsimd.tensor_tensor(B("G"), bc(triu), gate[:, t, :].unsqueeze(2).to_broadcast([P, H, P]), ALU.mult))
                if s == "f3":
                    dv("X")
                    step(nc.gpsimd.tensor_tensor(B("X"), B("X"), bc(incl), ALU.mult))
                    ac("D")
                    step(nc.gpsimd.tensor_tensor(B("Dq"), B("X"), bc(incl), ALU.mult))
                    step(nc.gpsimd.tensor_tensor(B("Ds"), B("X"), bc(strict), ALU.mult))
                if s == "f4":
                    step(nc.gpsimd.tensor_tensor(T("qd", t), qk[:, 0, :, :], T("EG", t), ALU.mult))
                if s == "f5":
                    dv("N")
                    step(nc.gpsimd.tensor_tensor(B("n"), B("N"), bc(diag16), ALU.mult))
                    step(nc.gpsimd.tensor_tensor(B("L"), B("N"), bc(off16), ALU.mult))

            def back(t, s):
                pe, dv, ac, po = waits(pool, t, 1)
                step = lambda ins: ins.then_inc(done["pool"][1], 1)
                if s == "b0":
                    waits(pool, t, 0)[1]("m")
                    step(nc.gpsimd.tensor_tensor(B("Y"), bc(ident), B("m"), ALU.subtract))
                if s == "b12":
                    dv("otmp")
                    pool.wait_ge(z_in[t % 2], 16 * (t // 2 + 1))
                    if t >= 2:
                        pool.wait_ge(stored[t % 2], 16 * (t // 2))
                    step(nc.gpsimd.tensor_tensor(out_b[:, t % 2, :, :], B("osq"), qkvz[:, t % 2, 3, :, :], ALU.mult))

            run_turns(selection, front, back)

        @block.tensor
        def _(pe):
            pe.wait_ge(const_in, 160)
            pe.wait_ge(const_set, 5)
            for t in range(NT):
                last = nc.tensor.transpose(ph(ps[:, 0, :, :])[:, t * N_SMALL:(t + 1) * N_SMALL],
                                           small[:, t * P:(t + 1) * P], ident[0:N_SMALL, 0:N_SMALL])
            last.then_inc(pe_s, 1)
            pe.wait_ge(dve_s, 6)
            nc.tensor.matmul(ph(ps[:, 1, :, :])[:, 0:NT * H], triu[:, :], gate[:, :, :].rearrange("p a b -> p (a b)"),
                             start=True, stop=True).then_inc(pe_s, 1)
            pe.wait_ge(dve_s, 7)
            pe.wait_ge(act_s, 6)

            def selection(t, m):
                for _, j, h, x in plan.at("pe", t, m):
                    n, w, i = plan.number[j, h, x], width(j, x), order[j]
                    if n == 1:
                        pe.wait_ge(key_done, S // KP)
                    if h == x == 0:
                        pe.wait_ge(q_lod, i + 1)
                    if n > 2:
                        pe.wait_ge(relu_done, n - 2)
                    dst = ips[:, n % 2, 0:w]
                    nc.tensor.matmul(dst, q_hi[:, i % 2, h, :], ikeys[:, x:x + w], start=True, stop=False)
                    nc.tensor.matmul(dst, q_lo[:, i % 2, h, :], ikeys[:, x:x + w], start=False, stop=True).then_inc(scored, 1)

            def heads(part, name, lhsT, rhs, more=None):
                for h in range(H):
                    last = nc.tensor.matmul(bank(name)[:, h, :], lhsT[:, h, :], rhs[:, h, :], start=True, stop=more is None)
                    if more:
                        last = nc.tensor.matmul(bank(name)[:, h, :], more[0][:, h, :], more[1][:, h, :], start=False, stop=True)
                last.then_inc(done["pe"][part], 1)

            def transposes(name, src):
                for h in range(H):
                    last = nc.tensor.transpose(bank(name)[:, h, :], src[:, h, :], ident[:, :])
                return last

            def over_features(name, src):
                return nc.tensor.matmul(ph(bank(name)), ones[:, :], ph(src), start=True, stop=True)

            def front(t, s):
                _, dv, ac, po = waits(pe, t, 0)
                done_f = done["pe"][0]
                if s == "f0":
                    if t:
                        waits(pe, t - 1, 0)[2]("m2")
                        waits(pe, t - 1, 0)[1]("vb")
                    ac("sq")
                    over_features("ssq", sq[:, 0, :, :])
                    over_features("ssk", sq[:, 1, :, :]).then_inc(done_f, 1)
                    po("G")
                    over_features("gb", B("G")).then_inc(done_f, 1)
                if s == "f3":
                    dv("qk")
                    heads(0, "kk", qk[:, 1, :, :], qk[:, 1, :, :])
                    heads(0, "att", qk[:, 0, :, :], qk[:, 1, :, :])
                if s == "f5":
                    dv("at")
                    transposes("NT", B("N"))
                    transposes("atT", B("at")).then_inc(done_f, 1)
                    transposes("kT", qk[:, 1, :, :]).then_inc(done_f, 1)
                if s == "f6":
                    dv("LT")
                    transposes("vT", qkvz[:, t % 2, 2, :, :]).then_inc(done_f, 1)
                if s == "f7":
                    po("n")
                    ac("attT")
                    heads(0, "n2", B("m"), B("n"))
                    dv("kbe")
                    heads(0, "m2", B("n"), B("m"))

            def back(t, s):
                _, dv, ac, po = waits(pe, t, 1)
                if s == "b0":
                    if t:
                        waits(pe, t - 1, 1)[1]("otmp")
                        waits(pe, t - 1, 1)[2]("oln")
                    waits(pe, t, 0)[2]("m2")
                    heads(1, "n4", B("m2"), B("n2"))
                    heads(1, "m4", B("n2"), B("m2"))
                    po("Y")
                    heads(1, "Y1", B("n2"), B("Y"))
                if s == "b1":
                    ac("m4")
                    heads(1, "n8", B("m4"), B("n4"))
                    dv("Y1")
                    heads(1, "Y2", B("n4"), B("Y"))
                if s == "b2":
                    dv("Y2")
                    ac("n8")
                    heads(1, "Y3", B("n8"), B("Y"))
                if s == "b3":
                    dv("Y3")
                    transposes("Dinv", B("Y")).then_inc(done["pe"][1], 1)
                if s == "b4":
                    ac("Dinv")
                    heads(1, "E", T("LT", t), B("Dinv"))
                    heads(1, "F", B("Dinv"), T("LT", t))
                if s == "b5":
                    ac("E")
                    heads(1, "Z1", B("E"), B("Y"))
                    ac("F")
                    heads(1, "E2", B("F"), B("E"))
                    heads(1, "F2", B("E"), B("F"))
                if s == "b6":
                    ac("E2")
                    dv("Z1")
                    heads(1, "Z2", B("E2"), B("Z"))
                    ac("F2")
                    heads(1, "E4", B("F2"), B("E2"))
                if s == "b7":
                    ac("E4")
                    dv("Z2")
                    heads(1, "Z3", B("E4"), B("Z"))
                if s == "b8":
                    dv("Z3")
                    waits(pe, t, 0)[1]("vb")
                    heads(1, "wT", T("kbe", t), B("Z"))
                if s == "b9":
                    ac("wT")
                    if t:
                        waits(pe, t - 1, 1)[1]("S")
                    heads(1, "vnew", B("Z"), T("vb", t), (B("wT"), st_S[:, :, :]))
                if s == "b10":
                    ac("vnew")
                    waits(pe, t, 0)[3]("qd")
                    heads(1, "out", st_S[:, :, :], T("qd", t), (B("vnew"), T("attT", t)))
                    heads(1, "state", T("kt", t), B("vnew"))
                if s == "b11":
                    ac("osq")
                    over_features("oss", B("osq")).then_inc(done["pe"][1], 1)

            run_turns(selection, front, back)

        @block.scalar
        def _(act):
            n = [0]

            def step(ins):
                ins.then_inc(act_s, 1)
                n[0] += 1

            act.wait_ge(const_set, 5)
            act.wait_ge(const_in, 160)
            act.wait_ge(dve_s, 1)
            step(nc.scalar.activation(beta[:, :, :], sm[:, :, R_B:R_B + H], ACT.Sigmoid))
            act.wait_ge(dve_s, 3)
            step(nc.scalar.activation(sp_b[:, :, :], sp_b[:, :, :], ACT.Exp))
            act.wait_ge(act_s, 2)
            step(nc.scalar.activation(sp_b[:, :, :], sp_b[:, :, :], ACT.Ln, bias=one_col[:, :]))
            step(nc.scalar.activation(alog[:, :], alog[:, :], ACT.Exp))
            act.wait_ge(pe_s, 2)
            step(nc.scalar.activation(gcum[:, :, :].rearrange("p a b -> p (a b)"), ph(ps[:, 1, :, :])[:, 0:NT * H], ACT.Copy))
            act.wait_ge(act_s, 5)
            step(nc.scalar.activation(egc[:, :, :], gcum[:, :, :], ACT.Exp))
            assert n[0] == 6
            nc.scalar.activation(w_idx[:, :, :], sm[:, :, R_W:R_W + IDX_HEADS], ACT.Copy,
                                 scale=float((IDX_HEADS * HD) ** -0.5)).then_inc(w_done, 1)

            def selection(t, m):
                if t == 0 and m in KEY_STAGE:
                    k = KEY_STAGE[m]
                    act.wait_ge(key_mul, 3 * (k + 1))
                    nc.scalar.activation(ikeys[:, k * KP:(k + 1) * KP], flat(0), ACT.Copy).then_inc(key_hi, 1)
                for kind, j, *piece in plan.at("act", t, m):
                    if kind == "round":
                        i = order[j]
                        act.wait_ge(q_rot, i + 1)
                        if i >= 2:
                            act.wait_ge(scored, last_piece(plan.tiles[i - 2]))
                        nc.scalar.activation(q_hi[:, i % 2], rot[:, 0], ACT.Copy).then_inc(q_hid, 1)
                    else:
                        c = plan.number[j, *piece]
                        w = width(j, piece[1])
                        act.wait_ge(scored, c)
                        if c > RELUS:
                            act.wait_ge(acc_done, c - RELUS)
                        nc.scalar.activation(relu[:, c % RELUS, 0:w], ips[:, c % 2, 0:w], ACT.Relu).then_inc(relu_done, 1)

            def front(t, s):
                pe, dv, ac, po = waits(act, t, 0)
                step = lambda ins: ins.then_inc(done["act"][0], 1)
                if s == "f0":
                    act.wait_ge(load[t % 2], 16 * (t // 2 + 1))
                    step(nc.scalar.activation(sq[:, :, :, :], qkvz[:, t % 2, 0:2, :, :], ACT.Square))
                if s == "f1":
                    pe("ss")
                    step(nc.scalar.activation(rn[:, :, :, :], ps[:, 0:2, :, :], ACT.Ln, bias=eps_col[:, :]))
                    ac("ln")
                    step(nc.scalar.activation(rn[:, 0, :, :], rn[:, 0, :, :], ACT.Exp, scale=-0.5, bias=ln_qk[:, :]))
                    step(nc.scalar.activation(rn[:, 1, :, :], rn[:, 1, :, :], ACT.Exp, scale=-0.5))
                    pe("gb")
                    step(nc.scalar.activation(T("EG", t), bank("gb"), ACT.Exp))
                if s == "f3":
                    po("X")
                    step(nc.scalar.activation(B("X"), B("X"), ACT.Exp, scale=-1.0))
                    dv("tail")
                    step(nc.scalar.activation(etail[:, :], tail[:, :], ACT.Exp))
                if s == "f5":
                    pe("tr")
                    step(nc.scalar.activation(T("attT", t), bank("atT"), ACT.Copy))
                if s == "f7":
                    for name in ("n2", "m2"):
                        pe(name)
                        step(nc.scalar.activation(B(name), bank(name), ACT.Copy))

            COPIES = {"b0": "n4 m4", "b1": "n8", "b3": "Dinv", "b4": "E F", "b5": "E2 F2", "b6": "E4", "b8": "wT", "b9": "vnew"}

            def back(t, s):
                pe, dv, ac, po = waits(act, t, 1)
                step = lambda ins: ins.then_inc(done["act"][1], 1)
                for name in COPIES.get(s, "").split():
                    pe(name)
                    step(nc.scalar.activation(B(name), bank(name), ACT.Copy))
                if s == "b10":
                    pe("out")
                    step(nc.scalar.activation(B("osq"), bank("out"), ACT.Square))
                if s == "b11":
                    pe("oss")
                    step(nc.scalar.activation(B("osq"), bank("oss"), ACT.Ln, scale=1.0 / BD, bias=eps_col[:, :]))
                    ac("oln")
                    step(nc.scalar.activation(B("osq"), B("osq"), ACT.Exp, scale=-0.5))

            run_turns(selection, front, back)

        @block.vector
        def _(dve):
            n = [0]
            st = Steps(dve, sel_s)

            def step(ins):
                ins.then_inc(dve_s, 1)
                n[0] += 1

            dve.wait_ge(const_in, 160)
            dve.wait_ge(pe_s, 1)
            step(nc.vector.tensor_copy(sm[:, :, :].rearrange("p a b -> p (a b)"), ph(ps[:, 0, :, :])[:, 0:NT * N_SMALL]))
            dve.wait_ge(dve_s, 1)
            step(nc.vector.tensor_tensor(sp_a[:, :, :], sm[:, :, R_A:R_A + H],
                                         dtb[:, :].unsqueeze(1).to_broadcast([P, NT, H]), ALU.add))
            dve.wait_ge(dve_s, 2)
            step(nc.vector.scalar_tensor_tensor(out=sp_b[:, :, :], in0=sp_a[:, :, :], scalar=-1.0, in1=sp_a[:, :, :],
                                                op0=ALU.mult, op1=ALU.min))
            dve.wait_ge(act_s, 4)
            step(nc.vector.scalar_tensor_tensor(out=sp_a[:, :, :], in0=sp_a[:, :, :], scalar=0.0, in1=sp_b[:, :, :],
                                                op0=ALU.max, op1=ALU.add))
            dve.wait_ge(dve_s, 4)
            step(nc.vector.scalar_tensor_tensor(out=gate[:, :, :], in0=sp_a[:, :, :], scalar=-1.0,
                                                in1=alog[:, :].unsqueeze(1).to_broadcast([P, NT, H]),
                                                op0=ALU.mult, op1=ALU.mult))
            dve.wait_ge(dve_s, 5)
            step(nc.vector.tensor_copy(sp_a[:, :, :], gate[:, :, :]))
            dve.wait_ge(act_s, 6)
            step(nc.vector.scalar_tensor_tensor(out=nbeg[:, :, :], in0=beta[:, :, :], scalar=-1.0, in1=egc[:, :, :],
                                                op0=ALU.mult, op1=ALU.mult))
            assert n[0] == 7
            dve.wait_ge(w_done, 1)

            def rotate_keys(k):
                toks = slice(k * KP, (k + 1) * KP)
                dve.wait_ge(key_in, 32 + 96 * (k + 1))
                nc.vector.tensor_tensor(flat(0), flat(0), cosT[:, toks], ALU.mult).then_inc(key_mul, 1)
                nc.vector.tensor_tensor(flat(1), flat(1), sinT[:, toks], ALU.mult).then_inc(key_mul, 1)
                dve.wait_ge(key_mul, 3 * k + 2)
                nc.vector.tensor_tensor(flat(0), flat(0), flat(1), ALU.add).then_inc(key_mul, 1)

            def lower_keys(k):
                up = ikeys[HD:P, k * KP:(k + 1) * KP]
                dve.wait_ge(key_hi, k + 1)
                nc.vector.tensor_tensor(up, flat(0)[HD:P], up.bitcast(fp32), ALU.subtract).then_inc(key_done, 1)

            def accumulate(j, h, x):
                c, w = plan.number[j, h, x], width(j, x)
                dve.wait_ge(relu_done, c)
                if h == 0:
                    nc.vector.tensor_scalar(score[:, x:x + w], relu[:, c % RELUS, 0:w], w_idx[:, j, h:h + 1], None,
                                            ALU.mult).then_inc(acc_done, 1)
                else:
                    dve.wait_ge(acc_done, plan.number[j, h - 1, x])
                    nc.vector.scalar_tensor_tensor(out=score[:, x:x + w], in0=relu[:, c % RELUS, 0:w],
                                                   scalar=w_idx[:, j, h:h + 1], in1=score[:, x:x + w],
                                                   op0=ALU.mult, op1=ALU.add).then_inc(acc_done, 1)

            def select(j, k):
                N = (j + 1) * P
                sc, m, junk = score[:, 0:N], left[:, 0:N], bias[:, 0:N]
                if k == 0:
                    dve.wait_ge(acc_done, last_piece(j))
                    if order[j]:
                        dve.wait_ge(bias_stored, 16 * order[j])
                    st.do(nc.vector.memset(score[0:CHUNK, N - CHUNK:N], BARRED))
                    st.do(nc.vector.tensor_scalar(junk, sc, 0.0, None, ALU.is_ge, ALU.add, accum_out=count[:, :]))
                    st.do(nc.vector.tensor_scalar(bound[:, :], count[:, :], float(topk), None, ALU.is_ge))
                    nc.vector.tensor_scalar(sign[:, :], bound[:, :], 2.0, -1.0, ALU.mult, ALU.add)
                    st.do(nc.vector.tensor_scalar(bound[:, :], bound[:, :], float(2 * topk - N - 1), float(N - topk + 1),
                                                  ALU.mult, ALU.add))
                    st.do(nc.vector.memset(trial[:, :], 2 ** (BITS - 1)))
                    st.do(nc.vector.tensor_scalar(m, sc, sign[:, 0:1], None, ALU.mult))
                elif k <= BITS:
                    bit = BITS - k
                    st.do(nc.vector.tensor_scalar(junk, m, trial[:, 0:1].bitcast(fp32), None, ALU.is_ge, ALU.add,
                                                  accum_out=count[:, :]))
                    st.do(nc.vector.tensor_scalar(drop[:, :], count[:, :], bound[:, 0:1], float(2 ** bit), ALU.is_lt, ALU.mult))
                    st.do(nc.vector.scalar_tensor_tensor(out=trial[:, :], in0=drop[:, :], scalar=2 ** bit // 2, in1=trial[:, :],
                                                         op0=ALU.bitwise_or, op1=ALU.bitwise_xor))
                elif k == BITS + 1:
                    st.do(nc.vector.tensor_scalar(value[:, :], trial[:, 0:1].bitcast(fp32), sign[:, 0:1], None, ALU.mult))
                    st.do(nc.vector.tensor_scalar(junk, sc, value[:, 0:1], None, ALU.is_gt, ALU.add, accum_out=count[:, :]))
                    nc.vector.tensor_scalar(room[:, :], count[:, :], -1.0, float(topk), ALU.mult, ALU.add)
                    st.do(nc.vector.tensor_scalar(m, sc, value[:, 0:1], None, ALU.is_equal))
                elif k == BITS + 2:
                    st.do(nc.vector.tensor_tensor_scan(bias[:, 0:N], m, m, 0.0, ALU.add, ALU.bypass))
                    st.do(nc.vector.scalar_tensor_tensor(out=m, in0=bias[:, 0:N], scalar=room[:, 0:1], in1=m,
                                                         op0=ALU.is_gt, op1=ALU.mult))
                else:
                    st.do(nc.vector.scalar_tensor_tensor(out=m, in0=sc, scalar=value[:, 0:1], in1=m, op0=ALU.is_lt, op1=ALU.add))
                    nc.vector.tensor_scalar(bias[:, 0:N], m, MASK_BIAS, None, ALU.mult).then_inc(selected, 1)
                    dve.wait_ge(selected, order[j] + 1)

            def selection(t, m):
                if t == 0 and m in KEY_STAGE:
                    rotate_keys(KEY_STAGE[m])
                if t == 0 and m - 1 in KEY_STAGE:
                    lower_keys(KEY_STAGE[m - 1])
                for kind, *part in plan.at("dve", t, m):
                    (accumulate if kind == "acc" else select)(*part)

            col = lambda a, t: a[:, t, :].unsqueeze(2).to_broadcast([P, H, P])

            def front(t, s):
                pe, own, ac, po = waits(dve, t, 0)
                step = lambda ins: ins.then_inc(done["dve"][0], 1)
                if s == "f2":
                    ac("rnk")
                    step(nc.vector.tensor_tensor(qk[:, :, :, :], qkvz[:, t % 2, 0:2, :, :], rn[:, :, :, :], ALU.mult))
                    ac("EG")
                    step(nc.vector.tensor_tensor(B("X"), bank("gb"), col(gcum, t), ALU.subtract))
                    step(nc.vector.tensor_tensor(tail[:, :], bank("gb")[:, :, P - 1], gcum[:, t, :], ALU.subtract))
                if s == "f4":
                    pe("att")
                    po("Ds")
                    for h in range(H):
                        last = nc.vector.scalar_tensor_tensor(out=big["N"][:, h, :], in0=bank("kk")[:, h, :],
                                                              scalar=beta[:, t, h:h + 1], in1=big["Ds"][:, h, :],
                                                              op0=ALU.mult, op1=ALU.mult)
                    step(last)
                    step(nc.vector.tensor_tensor(B("at"), bank("att"), B("Dq"), ALU.mult))
                if s == "f6":
                    pe("tr")
                    step(nc.vector.tensor_tensor(B("m"), bank("NT"), bc(diag16), ALU.mult))
                    step(nc.vector.tensor_tensor(T("LT", t), bank("NT"), bc(off16), ALU.mult))
                    ac("etail")
                    pe("kT")
                    step(nc.vector.tensor_tensor(T("kt", t), bank("kT"), etail[:, :].unsqueeze(2).to_broadcast([P, H, P]), ALU.mult))
                    step(nc.vector.tensor_tensor(T("kbe", t), bank("kT"), col(nbeg, t), ALU.mult))
                if s == "f7":
                    pe("vT")
                    step(nc.vector.tensor_tensor(T("vb", t), bank("vT"), col(beta, t), ALU.mult))

            def back(t, s):
                pe, own, ac, po = waits(dve, t, 1)
                step = lambda ins: ins.then_inc(done["dve"][1], 1)

                def add(name, out, acc, op=ALU.add):
                    pe(name)
                    step(nc.vector.tensor_tensor(B(out), B(acc), bank(name), op))

                if s == "b0":
                    po("Y")
                    add("Y1", "Y", "Y")
                if s == "b1":
                    own("Y1")
                    add("Y2", "Y", "Y")
                if s == "b2":
                    own("Y2")
                    add("Y3", "Y", "Y")
                if s == "b5":
                    own("Y3")
                    add("Z1", "Z", "Y", ALU.subtract)
                if s == "b6":
                    own("Z1")
                    add("Z2", "Z", "Z")
                if s == "b7":
                    own("Z2")
                    add("Z3", "Z", "Z")
                if s == "b10":
                    pe("state")
                    for h in range(H):
                        last = nc.vector.scalar_tensor_tensor(out=st_S[:, h, :], in0=st_S[:, h, :], scalar=T("EG", t)[:, h, P - 1:P],
                                                              in1=bank("state")[:, h, :], op0=ALU.mult, op1=ALU.add)
                    step(last)
                if s == "b11":
                    ac("orn")
                    step(nc.vector.scalar_tensor_tensor(out=ph(B("osq")), in0=ph(bank("out")), scalar=gg[:, 0:1], in1=ph(B("osq")),
                                                        op0=ALU.mult, op1=ALU.mult))

            run_turns(selection, front, back)


def indexed_attention(nc, S, topk, projT, consts, biasT, mixT):
    NT, PIECE = S // P, 1024
    G = A_HEADS // KV_HEADS
    UN = KV_HEADS * NT
    with ExitStack() as ctx:
        sb = lambda n, s, d=fp32: ctx.enter_context(nc.sbuf_tensor(n, s, d))
        sem = lambda n: ctx.enter_context(nc.semaphore(n))
        ident, ones = sb("a_ident", [P, P]), sb("a_ones", [P, P])
        cosT, sinT = sb("a_cos", [P, S]), sb("a_sin", [P, S])
        keys = sb("a_keys", [P, KV_HEADS, S], f32r)
        vals = sb("a_vals", [P, NT, KV_HEADS, 2 * HD], f32r)
        rot = sb("a_rot", [P, 2, 2, 8, P])
        q_hi = sb("a_qhi", [P, 2, 8, P], f32r)
        q_lo = sb("a_qlo", [P, 2, 8, P], f32r)
        bias = sb("a_bias", [P, 2, S])
        prob = sb("a_prob", [P, A_HEADS, S])
        mx = sb("a_mx", [P, 2, A_HEADS])
        nmx = sb("a_nmx", [P, A_HEADS])
        rsum = sb("a_rsum", [P, A_HEADS])
        rinv = sb("a_rinv", [P, A_HEADS])
        diag = sb("a_diag", [P, G, P])
        p_hi = sb("a_phi", [P, 3, G * P], f32r)
        p_lo = sb("a_plo", [P, 3, G * P], f32r)
        rb, low = sb("a_rb", [HD, G * P]), sb("a_low", [HD, G * P])
        out = sb("a_out", [HD, KV_HEADS, G, P])
        ps = ctx.enter_context(nc.psum_tensor("a_ps", [P, 8, 512], fp32))
        slot_ps = lambda n, w: ps[:, 2 * (n % 2):2 * (n % 2) + 2, :].rearrange("p a b -> p (a b)")[:, 0:w]
        T_BANK = lambda n: 4 + n % 3
        O_BANK = 7

        const_in, const_set, key_mul, key_sin, key_rot, key_hi, key_done, v_in, v_T, v_hi, v_done = map(sem, (
            "a_const_in a_const_set a_key_mul a_key_sin a_key_rot a_key_hi a_key_done a_v_in a_v_T a_v_hi a_v_done").split())
        pair = lambda n: [sem(f"a_{n}{k}") for k in range(2)]
        rot_in, bias_in, stored = pair("rot_in"), pair("bias_in"), pair("stored")
        q_cos, q_sin, q_rot, q_hid, q_lod = map(sem, "a_q_cos a_q_sin a_q_rot a_q_hi_done a_q_lo_done".split())
        att_done, bias_set, masked, max_done, exp_done, rinv_done, diag_done = map(sem, (
            "a_att a_bias_set a_masked a_max a_exp a_rinvd a_diagd").split())
        pT_done, hi_done, lo_done, pv_done, o_done, rb_done, sum_done, norm_done = map(sem, (
            "a_pTd a_hi a_lo a_pv a_o a_rbd a_sum a_norm").split())
        dve_s = sem("a_dve")

        def pieces(t):
            n = (t + 1) * P
            return [(a, min(PIECE, n - a)) for a in range(0, n, PIECE)]

        selected = [t for t in range(NT) if (t + 1) * P > topk]
        units = [(t, g) for t in range(NT) for g in range(KV_HEADS)]
        items = [(t, h, p) for t, g in units for h in range(g * G, g * G + G) for p in range(len(pieces(t)))]
        place = {it: n for n, it in enumerate(items)}
        last_item = lambda u: place[units[u][0], units[u][1] * G + G - 1, len(pieces(units[u][0])) - 1]

        def turn_steps(u):
            items = [(h, p) for h in range(units[u + 1][1] * G, units[u + 1][1] * G + G)
                     for p in range(len(pieces(units[u + 1][0])))] if u + 1 < UN else []
            chunks = units[u][0] + 1 if u >= 0 else 0
            for item in items:
                yield "scores", item
            for c in range(chunks):
                yield "chunk", c
            yield "end", None

        turn = lambda u: sum(units[v][0] + 2 for v in range(u))
        chunks_to = lambda u: sum(units[v][0] + 1 for v in range(u))

        KP = min(S, 1024)
        key_steps = [(k, a) for k in range(KV_HEADS) for a in range(0, S, KP)]
        NK = len(key_steps)
        flat = lambda s, r: rot[:, s, r].rearrange("p a b -> p (a b)")[:, 0:KP]
        q_slot = lambda t: (NK + t) % 2
        q_in_count = lambda t: 96 * ((NK + t) // 2 + 1)
        block = ctx.enter_context(nc.Block())

        rows = projT.rearrange("c p s -> (c p) s")
        out_rows = mixT.rearrange("c p s -> (c p) s")
        tokens = lambda t: slice(t * P, (t + 1) * P)

        @block.sync
        def _(sp):
            def load_bias(t):
                if t in selected:
                    i = selected.index(t)
                    if t >= 2:
                        sp.wait_ge(masked, last_item(KV_HEADS * (t - 2) + 1) + 1)
                    sp.dma_start(bias[:, t % 2, 0:(t + 1) * P], biasT[t, :, 0:(t + 1) * P]).then_inc(bias_in[t % 2], 16)

            for n, (k, a) in enumerate(key_steps):
                if n >= 2:
                    sp.wait_ge(key_done, n - 1)
                row = C_KA * P + k * HD
                rotated_rows(sp, flat(n % 2, 0), flat(n % 2, 1), rows[row:row + HD, a:a + KP], rot_in[n % 2])
                if n == 0:
                    for dst, src in ((cosT[:, :], consts["cosT"]), (sinT[:, :], consts["sinT"]), (ident[:, :], consts["ident"])):
                        sp.dma_start(dst, src).then_inc(const_in, 16)
                    sp.dma_start(prob[:, 0, :], projT[C_VA]).then_inc(v_in, 16)

            def store(u):
                t, g = units[u]
                sp.wait_ge(norm_done, u + 1)
                sp.dma_start(out_rows[g * G * HD:(g + 1) * G * HD, tokens(t)].rearrange("(h d) s -> d h s", d=HD),
                             out[:, g, :, :]).then_inc(stored[g], 16)

            for t in range(NT):
                if t >= 2:
                    sp.wait_ge(q_lod, t - 1)
                else:
                    sp.wait_ge(key_done, NK - 1 + t)
                rotated_rows(sp, rot[:, q_slot(t), 0], rot[:, q_slot(t), 1],
                             rows[C_QA * P:C_QA * P + A_HEADS * HD, tokens(t)].rearrange("(h r) s -> r h s", r=HD), rot_in[q_slot(t)])
                if t == 0:
                    load_bias(0)
                if t + 1 < NT:
                    load_bias(t + 1)
                if t >= 2:
                    store(2 * t - 4)
                    store(2 * t - 3)
            for u in range(2 * NT - 4, 2 * NT):
                store(u)
            for g in range(KV_HEADS):
                sp.wait_ge(stored[g], 16 * NT)

        @block.gpsimd
        def _(pool):
            nc.gpsimd.memset(ones[:, :], 1.0).then_inc(const_set, 1)
            pool.wait_ge(const_in, 48)
            for n, (k, a) in enumerate(key_steps):
                pool.wait_ge(rot_in[n % 2], 96 * (n // 2 + 1))
                nc.gpsimd.tensor_tensor(flat(n % 2, 1), flat(n % 2, 1), sinT[:, a:a + KP], ALU.mult).then_inc(key_sin, 1)

            def rotate(t):
                s = q_slot(t)
                table = sinT[:, tokens(t)].unsqueeze(1).to_broadcast([P, 8, P])
                pool.wait_ge(rot_in[s], q_in_count(t))
                nc.gpsimd.tensor_tensor(rot[:, s, 1], rot[:, s, 1], table, ALU.mult).then_inc(q_sin, 1)
                pool.wait_ge(q_sin, t + 1)
                pool.wait_ge(q_cos, t + 1)
                nc.gpsimd.tensor_tensor(rot[:, s, 0], rot[:, s, 0], rot[:, s, 1], ALU.add).then_inc(q_rot, 1)
                pool.wait_ge(q_hid, t + 1)
                nc.gpsimd.tensor_tensor(q_lo[:, t % 2], rot[:, s, 0], q_hi[:, t % 2].bitcast(fp32), ALU.subtract).then_inc(q_lod, 1)

            rotate(0)
            for u, (t, g) in enumerate(units):
                if g == 0 and t + 1 < NT:
                    rotate(t + 1)
                pool.wait_ge(rinv_done, u + 1)
                if u:
                    pool.wait_ge(o_done, u)
                nc.gpsimd.tensor_tensor(diag[:, :, :], ident[:, :].unsqueeze(1).to_broadcast([P, G, P]),
                                        rinv[:, g * G:(g + 1) * G].unsqueeze(2).to_broadcast([P, G, P]),
                                        ALU.mult).then_inc(diag_done, 1)

        @block.scalar
        def _(act):
            for n in range(NT // 4):
                act.wait_ge(v_T, n + 1)
                nc.scalar.activation(vals[:, 4 * n:4 * n + 4, :, 0:HD], ps[:, 4 + n % 2, :].rearrange(
                    "p (t g d) -> p t g d", t=4, g=KV_HEADS), ACT.Copy).then_inc(v_hi, 1)
            for n, (k, a) in enumerate(key_steps):
                act.wait_ge(key_rot, n + 1)
                nc.scalar.activation(keys[:, k, a:a + KP], flat(n % 2, 0), ACT.Copy).then_inc(key_hi, 1)

            def round_q(t):
                act.wait_ge(q_rot, t + 1)
                if t >= 2:
                    act.wait_ge(att_done, last_item(2 * (t - 2) + 1) + 1)
                nc.scalar.activation(q_hi[:, t % 2], rot[:, q_slot(t), 0], ACT.Copy).then_inc(q_hid, 1)

            def exponential(u, h):
                N = (units[u][0] + 1) * P
                act.wait_ge(max_done, G * u + h % G + 1)
                nc.scalar.activation(prob[:, h, 0:N], prob[:, h, 0:N], ACT.Exp, bias=nmx[:, h:h + 1],
                                     scale=HD ** -0.5, accum_out=rsum[:, h:h + 1]).then_inc(exp_done, 1)

            def high_half(u, c):
                n, m = turn(u) + c, chunks_to(u) + c
                act.wait_ge(pT_done, m + 1)
                if m >= 3:
                    act.wait_ge(pv_done, m - 2)
                nc.scalar.activation(p_hi[:, m % 3, :], ps[:, T_BANK(n), :], ACT.Copy).then_inc(hi_done, 1)

            def finish(u):
                act.wait_ge(o_done, u + 1)
                if u:
                    act.wait_ge(norm_done, u)
                nc.scalar.activation(rb[:, :], ps[0:HD, T_BANK(turn(u) + units[u][0] + 1), :], ACT.Copy).then_inc(rb_done, 1)
                nc.scalar.activation(low[:, :], ps[HD:P, O_BANK, :], ACT.Copy).then_inc(rb_done, 1)

            round_q(0)
            for u in range(-1, UN):
                if u + 1 < UN and units[u + 1][1] == 0 and units[u + 1][0] + 1 < NT:
                    round_q(units[u + 1][0] + 1)
                for kind, what in turn_steps(u):
                    if kind == "chunk":
                        high_half(u, what)
                    elif kind == "end":
                        if u >= 0:
                            finish(u)
                        if u + 1 < UN:
                            for h in range(units[u + 1][1] * G, units[u + 1][1] * G + G):
                                exponential(u + 1, h)

        @block.vector
        def _(dve):
            st = Steps(dve, dve_s)
            for n in range(NT // 4):
                dve.wait_ge(v_hi, n + 1)
                nc.vector.tensor_tensor(vals[:, 4 * n:4 * n + 4, :, HD:2 * HD], ps[:, 4 + n % 2, :].rearrange(
                    "p (t g d) -> p t g d", t=4, g=KV_HEADS), vals[:, 4 * n:4 * n + 4, :, 0:HD].bitcast(fp32),
                    ALU.subtract).then_inc(v_done, 1)
            dve.wait_ge(const_in, 48)
            for n, (k, a) in enumerate(key_steps):
                dve.wait_ge(rot_in[n % 2], 96 * (n // 2 + 1))
                nc.vector.tensor_tensor(flat(n % 2, 0), flat(n % 2, 0), cosT[:, a:a + KP], ALU.mult).then_inc(key_mul, 1)
                dve.wait_ge(key_mul, n + 1)
                dve.wait_ge(key_sin, n + 1)
                nc.vector.tensor_tensor(flat(n % 2, 0), flat(n % 2, 0), flat(n % 2, 1), ALU.add).then_inc(key_rot, 1)
                up = keys[HD:P, k, a:a + KP]
                dve.wait_ge(key_hi, n + 1)
                nc.vector.tensor_tensor(up, flat(n % 2, 0)[HD:P], up.bitcast(fp32), ALU.subtract).then_inc(key_done, 1)

            def rotate(t):
                s = q_slot(t)
                dve.wait_ge(rot_in[s], q_in_count(t))
                nc.vector.tensor_tensor(rot[:, s, 0], rot[:, s, 0], cosT[:, tokens(t)].unsqueeze(1).to_broadcast([P, 8, P]),
                                        ALU.mult).then_inc(q_cos, 1)

            def begin(u):
                t, g = units[u]
                N = (t + 1) * P
                if g == 0:
                    if t in selected:
                        dve.wait_ge(bias_in[t % 2], 16 * len([x for x in selected if x <= t and x % 2 == t % 2]))
                    else:
                        st.do(nc.vector.memset(bias[:, t % 2, 0:N], 0.0))
                        st.do(nc.vector.memset(bias[0:CHUNK, t % 2, N - CHUNK:N], MASK_BIAS))
                if u >= 2:
                    dve.wait_ge(pT_done, chunks_to(u - 1))
                    dve.wait_ge(exp_done, G * (u - 1))

            def mask(u, h, p):
                t, g = units[u]
                a, w = pieces(t)[p]
                n = place[t, h, p]
                dve.wait_ge(att_done, n + 1)
                nc.vector.tensor_tensor_reduce(out=prob[:, h, a:a + w], in0=slot_ps(n, w), in1=bias[:, t % 2, a:a + w],
                                               scale=1.0, scalar=-3.0e38, op0=ALU.add, op1=ALU.max,
                                               accum_out=mx[:, p, h:h + 1]).then_inc(masked, 1)
                if p == len(pieces(t)) - 1:
                    dve.wait_ge(masked, n + 1)
                    nc.vector.tensor_scalar(nmx[:, h:h + 1], mx[:, 0, h:h + 1], mx[:, p, h:h + 1], -HD ** -0.5,
                                            ALU.max, ALU.mult).then_inc(max_done, 1)

            def low_half(u, c):
                n, m = turn(u) + c, chunks_to(u) + c
                if c == 0:
                    hs = slice(units[u][1] * G, (units[u][1] + 1) * G)
                    dve.wait_ge(exp_done, G * (u + 1))
                    if u >= 2:
                        dve.wait_ge(diag_done, u - 1)
                    nc.vector.reciprocal(rinv[:, hs], rsum[:, hs]).then_inc(rinv_done, 1)
                dve.wait_ge(hi_done, m + 1)
                nc.vector.tensor_tensor(p_lo[:, m % 3, :], ps[:, T_BANK(n), :], p_hi[:, m % 3, :].bitcast(fp32),
                                        ALU.subtract).then_inc(lo_done, 1)

            def finish(u):
                t, g = units[u]
                dve.wait_ge(rb_done, 2 * u + 2)
                o = out[:, g, :, :].rearrange("p a b -> p (a b)")
                if t:
                    dve.wait_ge(stored[g], 16 * t)
                nc.vector.tensor_tensor(o, ps[0:HD, O_BANK, :], low[:, :], ALU.add).then_inc(sum_done, 1)
                dve.wait_ge(sum_done, u + 1)
                nc.vector.tensor_tensor(o, o, rb[:, :], ALU.mult).then_inc(norm_done, 1)

            rotate(0)
            for u in range(-1, UN):
                if u + 1 < UN:
                    if units[u + 1][1] == 0 and units[u + 1][0] + 1 < NT:
                        rotate(units[u + 1][0] + 1)
                    begin(u + 1)
                for kind, what in turn_steps(u):
                    if kind == "chunk":
                        low_half(u, what)
                    elif kind == "scores":
                        mask(u + 1, *what)
                    elif u >= 0:
                        finish(u)

        @block.tensor
        def _(pe):
            pe.wait_ge(const_in, 48)
            pe.wait_ge(v_in, 16)
            for n in range(NT // 4):
                if n >= 2:
                    pe.wait_ge(v_done, n - 1)
                for j in range(4):
                    last = nc.tensor.transpose(ps[:, 4 + n % 2, j * P:(j + 1) * P], prob[:, 0, tokens(4 * n + j)], ident[:, :])
                last.then_inc(v_T, 1)
            pe.wait_ge(const_set, 1)
            pe.wait_ge(v_done, NT // 4)
            pe.wait_ge(key_done, NK)

            def scores(u, h, p):
                t, g = units[u]
                a, w = pieces(t)[p]
                n = place[t, h, p]
                if h == p == 0:
                    pe.wait_ge(q_lod, t + 1)
                if n >= 2:
                    pe.wait_ge(masked, n - 1)
                for x in range(0, w, 512):
                    y = min(512, w - x)
                    dst = slot_ps(n, w)[:, x:x + y]
                    nc.tensor.matmul(dst, q_hi[:, t % 2, h, :], keys[:, g, a + x:a + x + y], start=True, stop=False)
                    last = nc.tensor.matmul(dst, q_lo[:, t % 2, h, :], keys[:, g, a + x:a + x + y], start=False, stop=True)
                last.then_inc(att_done, 1)

            def bank_free(u, n):
                if n < 3:
                    return
                v = max(v for v in range(u + 1) if turn(v) <= n - 3)
                c = n - 3 - turn(v)
                if c == units[v][0] + 1:
                    pe.wait_ge(rb_done, 2 * v + 1)
                else:
                    pe.wait_ge(lo_done, chunks_to(v) + c + 1)

            def transpose(u, c):
                g, n = units[u][1], turn(u) + c
                bank_free(u, n)
                if c == 0:
                    pe.wait_ge(exp_done, G * (u + 1))
                for j in range(G):
                    last = nc.tensor.transpose(ps[:, T_BANK(n), j * P:(j + 1) * P], prob[:, g * G + j, tokens(c)], ident[:, :])
                last.then_inc(pT_done, 1)

            def values(u, c):
                (t, g), m = units[u], chunks_to(u) + c
                if c == 0 and u:
                    pe.wait_ge(norm_done, u)
                pe.wait_ge(hi_done, m + 1)
                nc.tensor.matmul(ps[:, O_BANK, :], vals[:, c, g, :], p_hi[:, m % 3, :], start=(c == 0), stop=False)
                pe.wait_ge(lo_done, m + 1)
                nc.tensor.matmul(ps[:, O_BANK, :], vals[:, c, g, :], p_lo[:, m % 3, :],
                                 start=False, stop=(c == t)).then_inc(pv_done, 1)

            for u in range(-1, UN):
                for kind, what in turn_steps(u):
                    if kind == "scores":
                        scores(u + 1, *what)
                    elif kind == "chunk":
                        if what == 0:
                            for c in range(min(2, units[u][0] + 1)):
                                transpose(u, c)
                        if what + 2 <= units[u][0]:
                            transpose(u, what + 2)
                        values(u, what)
                    elif u >= 0:
                        n = turn(u) + units[u][0] + 1
                        bank_free(u, n)
                        pe.wait_ge(diag_done, u + 1)
                        nc.tensor.matmul(ps[0:HD, T_BANK(n), :], ones[:, 0:HD], diag[:, :, :].rearrange("p a b -> p (a b)"),
                                         start=True, stop=True).then_inc(o_done, 1)


def output_and_mlp(nc, S, xT, mixT, w_units, g_ffn, g_final, outT):
    TB, NB, NG, U = 512, S // 512, D_FF // 512, 4
    SEGS, UNITS = 2 + 2 * NG, 4 * (2 + 2 * NG)
    F_BLK, Y_BLK = 2 * U + NG * U, NG * KC
    with ExitStack() as ctx:
        sb = lambda n, s, d=fp32: ctx.enter_context(nc.sbuf_tensor(n, s, d))
        sem = lambda n: ctx.enter_context(nc.semaphore(n))
        ones, eps_col = sb("f_ones", [P, P]), sb("f_eps", [P, 1])
        gf, gl = sb("f_gf", [P, KC]), sb("f_gl", [P, KC])
        raw = sb("f_raw", [P, U, KC, P])
        wh = sb("f_wh", [P, 2 * U, KC, P], f32r)
        wl = sb("f_wl", [P, 2 * U, KC, P], f32r)
        tmp = sb("f_tmp", [P, KC, TB])
        acc = sb("f_acc", [P, KC, TB])
        ah = sb("f_ah", [P, KC, TB], f32r)
        al = sb("f_al", [P, KC, TB], f32r)
        th = sb("f_th", [P, 2, U, TB], f32r)
        tl = sb("f_tl", [P, 2, U, TB], f32r)
        rl = sb("f_rl", [P, 2, TB])
        r2 = sb("f_r2", [P, 2, TB])
        rstd = sb("f_rstd", [P, TB])
        ps = ctx.enter_context(nc.psum_tensor("f_ps", [P, 8, TB], fp32))
        (const_in, const_set, mix_in, x_in, mh_done, ml_done, x_done, sq_done, ss_done, std_done, h_done, hh_done, hl_done,
         f_done, y_done, y_add, r_done, th_done, r2_done, tl_done, out_done, stored, w_hi, w_lo, dve_s) = map(
            sem, ["f_" + n for n in ("const_in const_set mix_in x_in mh_done ml_done x_done sq_done ss_done std_done h_done "
                                     "hh_done hl_done f_done y_done y_add r_done th_done r2_done tl_done out_done stored "
                                     "w_hi w_lo dve").split()])
        raw_in = [sem(f"f_raw_in{n}") for n in range(U)]
        Y0, R0, SS0 = 2 * KC, 1, 1
        block = ctx.enter_context(nc.Block())

        def segments(eng, b, body, last=True):
            body("O", 0, 0, 0, 0, ("O", 1, 1))
            body("O", 1, 0, 1, 1, ("W1", 0, 2))
            body("W1", 0, 0, 2, 0, ("W1", 1, 3))
            with eng.Fori(0, (NG - 2) // 2) as j:
                for v in range(2):
                    g = 2 * j + (v + 1)
                    body("W1", g, (v + 1) % 2, 2 * g + 1, 1, ("W2", g - 1, 2 * g + 2))
                    body("W2", g - 1, v % 2, 2 * g + 2, 0, ("W1", g + 1, 2 * g + 3))
            g = NG - 1
            body("W1", g, g % 2, 2 * g + 1, 1, ("W2", g - 1, 2 * g + 2))
            body("W2", g - 1, (g - 1) % 2, 2 * g + 2, 0, ("W2", g, 2 * g + 3))
            body("W2", g, g % 2, 2 * g + 3, 1, None if last else ("next block", 0, SEGS))

        def tokens(b):
            return bass.ds(b * TB, TB)

        @block.sync
        def _(sp):
            sp.dma_start(gf[:, :], g_ffn).then_inc(const_in, 16)
            sp.dma_start(gl[:, :], g_final).then_inc(const_in, 16)
            sp.sem_inc(w_lo, U)
            sp.sem_inc(stored, 16)

            def load_unit(k, b, n, row):
                sp.wait_ge(w_lo, UNITS * b + n + 1)
                sp.dma_start(raw[:, k, :, :].rearrange("p a b -> p (a b)"), row).then_inc(raw_in[k], 16)

            def load_mix(b, tok):
                sp.wait_ge(ss_done, 2 * b + SS0)
                sp.dma_start(tmp[:, :, :], mixT[:, :, tok].rearrange("c p s -> p c s")).then_inc(mix_in, 16)

            def load_block(b, last):
                for k in range(U):
                    load_unit(k, b, U + k, w_units[U + k])
                sp.wait_ge(stored, 16 * b + 16)
                sp.dma_start(acc[:, :, :], xT[:, :, tokens(b)]).then_inc(x_in, 16)
                with sp.Fori(2, UNITS // U) as j:
                    for k in range(U):
                        load_unit(k, b, U * j + k, w_units[bass.ds(U * j + k, 1)].rearrange("a p n -> p (a n)"))
                if not last:
                    for k in range(U):
                        load_unit(k, b, UNITS + k, w_units[k])
                    load_mix(b + 1, bass.ds(b * TB + TB, TB))
                sp.wait_ge(out_done, KC * b + KC)
                sp.dma_start(outT[:, :, tokens(b)].rearrange("c p s -> p c s"), acc[:, :, :]).then_inc(stored, 16)

            for k in range(U):
                load_unit(k, 0, k, w_units[k])
            load_mix(0, slice(0, TB))
            with sp.Fori(0, NB - 1) as b:
                load_block(b, False)
            load_block(NB - 1, True)
            sp.wait_ge(stored, 16 * NB + 16)

        @block.gpsimd
        def _(pool):
            nc.gpsimd.memset(ones[:, :], 1.0).then_inc(const_set, 1)
            nc.gpsimd.memset(eps_col[:, :], EPS).then_inc(const_set, 1)
            with pool.Fori(0, NB * UNITS // (2 * U)) as i:
                for s in range(2 * U):
                    pool.wait_ge(w_hi, 2 * U * i + s + 1)
                    nc.gpsimd.tensor_tensor(wl[:, s, :, :], raw[:, s % U, :, :], wh[:, s, :, :].bitcast(fp32),
                                            ALU.subtract).then_inc(w_lo, 1)

        @block.scalar
        def _(act):
            act.sem_inc(r_done, R0)
            act.wait_ge(const_set, 2)
            def block_of(b, last):
                def done(kind, g):
                    if kind == "W2":
                        act.wait_ge(y_done, Y_BLK * b + KC * g + KC + Y0)
                    else:
                        act.wait_ge(f_done, F_BLK * b + U * g + U + (2 * U if kind == "W1" else 0))

                def split(seg, half, s):
                    act.wait_ge(raw_in[s], 16 * (SEGS * b + seg) + 16)
                    nc.scalar.activation(wh[:, U * half + s, :, :], raw[:, s, :, :], ACT.Copy).then_inc(w_hi, 1)

                def normalise(second, h_out):
                    for k in range(KC):
                        if second:
                            act.wait_ge(y_add, Y_BLK * b + Y_BLK - KC + k + 1 + 4)
                        else:
                            act.wait_ge(x_done, KC * b + k + 1)
                        if k == 0 and second:
                            act.wait_ge(hl_done, KC * b + KC)
                        if k == 0 and not second:
                            act.wait_ge(ml_done, KC * b + KC)
                        nc.scalar.activation(tmp[:, k, :], acc[:, k, :], ACT.Square).then_inc(sq_done, 1)
                    act.wait_ge(ss_done, 2 * b + (2 if second else 1) + SS0)
                    nc.scalar.activation(rstd[:, :], ps[:, 6, :], ACT.Sqrt, scale=1.0 / D_MODEL,
                                         bias=eps_col[:, :]).then_inc(std_done, 1)
                    if not second:
                        for k in range(KC):
                            act.wait_ge(h_done, KC * b + k + 1)
                            nc.scalar.activation(ah[:, k, :], tmp[:, k, :], ACT.Copy).then_inc(hh_done, 1)

                act.wait_ge(y_done, Y_BLK * b + Y0)
                act.wait_ge(mix_in, 16 * b + 16)
                for k in range(KC):
                    nc.scalar.activation(ah[:, k, :], tmp[:, k, :], ACT.Copy).then_inc(mh_done, 1)

                def segment(kind, g, par, seg, half, nxt):
                    for s in range(U):
                        if nxt:
                            if s == 0 and not (kind == "O" and g == 0):
                                before = {"O": ("O", 0), "W2": ("W1", g + 1)}.get(kind)
                                if nxt[0] == "next block":
                                    before = ("W2", g - 1)
                                if kind == "W1":
                                    before = ("O", 1) if isinstance(seg, int) and seg == 2 else ("W2", g - 2)
                                if kind == "W1" and not (isinstance(seg, int) and seg == 2):
                                    act.wait_ge(y_done, Y_BLK * b + KC * g - KC + Y0)
                                    act.wait_ge(f_done, F_BLK * b + 3 * U)
                                else:
                                    done(*before)
                            split(nxt[2], 1 - half, s)
                        if kind == "W1":
                            n = U * g + s
                            act.wait_ge(f_done, F_BLK * b + 2 * U + n + 1)
                            act.wait_ge(tl_done, UW * b + n + 1)
                            nc.scalar.activation(rl[:, s % 2, :], ps[:, s % 2, :], ACT.Relu).then_inc(r_done, 1)
                            act.wait_ge(r_done, UW * b + n + 1 + R0)
                            act.wait_ge(y_done, Y_BLK * b + KC * g - KC + Y0)
                            nc.scalar.activation(th[:, par, s, :], rl[:, s % 2, :], ACT.Square).then_inc(th_done, 1)
                    if isinstance(seg, int) and seg == 1:
                        normalise(False, None)

                UW = NG * U
                segments(act, b, segment, last)
                normalise(True, None)

            for s in range(U):
                act.wait_ge(raw_in[s], 16)
                nc.scalar.activation(wh[:, s, :, :], raw[:, s, :, :], ACT.Copy).then_inc(w_hi, 1)
            with act.Fori(0, NB - 1) as b:
                block_of(b, False)
            block_of(NB - 1, True)

        @block.vector
        def _(dve):
            st = Steps(dve, dve_s)
            UW = NG * U
            dve.sem_inc(tl_done, 2)
            dve.sem_inc(y_add, 4)
            dve.wait_ge(const_in, 32)
            with dve.Fori(0, NB) as b:
                st.loop(0, b, 2)
                for k in range(KC):
                    dve.wait_ge(mh_done, KC * b + k + 1)
                    nc.vector.tensor_tensor(al[:, k, :], tmp[:, k, :], ah[:, k, :].bitcast(fp32), ALU.subtract).then_inc(ml_done, 1)

                def segment(kind, g, par, seg, half, nxt):
                    if kind == "O":
                        for s in range(U):
                            k = U * g + s
                            if k == 0:
                                dve.wait_ge(x_in, 16 * b + 16)
                            dve.wait_ge(f_done, F_BLK * b + k + 1)
                            nc.vector.tensor_tensor(acc[:, k, :], acc[:, k, :], ps[:, s % 2, :], ALU.add).then_inc(x_done, 1)
                        if g == 1:
                            dve.wait_ge(std_done, 2 * b + 1)
                            st.do(nc.vector.reciprocal(rstd[:, :], rstd[:, :]))
                            for k in range(KC):
                                nc.vector.scalar_tensor_tensor(out=tmp[:, k, :], in0=acc[:, k, :], scalar=gf[:, k:k + 1],
                                                               in1=rstd[:, :], op0=ALU.mult, op1=ALU.mult).then_inc(h_done, 1)
                            for k in range(KC):
                                dve.wait_ge(hh_done, KC * b + k + 1)
                                nc.vector.tensor_tensor(al[:, k, :], tmp[:, k, :], ah[:, k, :].bitcast(fp32),
                                                        ALU.subtract).then_inc(hl_done, 1)
                    elif kind == "W1":
                        for s in range(U):
                            n = U * g + s
                            dve.wait_ge(r_done, UW * b + n + 1 + R0)
                            nc.vector.tensor_tensor(r2[:, s % 2, :], rl[:, s % 2, :], rl[:, s % 2, :], ALU.mult).then_inc(r2_done, 1)
                            dve.wait_ge(th_done, UW * b + n + 1)
                            dve.wait_ge(r2_done, UW * b + n + 1)
                            nc.vector.tensor_tensor(tl[:, par, s, :], r2[:, s % 2, :], th[:, par, s, :].bitcast(fp32),
                                                    ALU.subtract).then_inc(tl_done, 1)
                    else:
                        for k in range(KC):
                            dve.wait_ge(y_done, Y_BLK * b + KC * g + k + 1 + Y0)
                            nc.vector.tensor_tensor(acc[:, k, :], acc[:, k, :], ps[:, 2 + k % 4, :], ALU.add).then_inc(y_add, 1)

                segments(dve, b, segment)
                dve.wait_ge(std_done, 2 * b + 2)
                st.do(nc.vector.reciprocal(rstd[:, :], rstd[:, :]))
                for k in range(KC):
                    nc.vector.scalar_tensor_tensor(out=acc[:, k, :], in0=acc[:, k, :], scalar=gl[:, k:k + 1],
                                                   in1=rstd[:, :], op0=ALU.mult, op1=ALU.mult).then_inc(out_done, 1)
            st.leave(NB)

        @block.tensor
        def _(pe):
            UW = NG * U
            pe.sem_inc(y_done, Y0)
            pe.sem_inc(ss_done, SS0)
            pe.wait_ge(const_set, 2)
            with pe.Fori(0, NB) as b:
                def sum_squares(first):
                    for k in range(KC):
                        pe.wait_ge(sq_done, 2 * KC * b + k + 1 + (0 if first else KC))
                        last = nc.tensor.matmul(ps[:, 6, :], ones[:, :], tmp[:, k, :], start=(k == 0), stop=(k == KC - 1))
                    last.then_inc(ss_done, 1)

                def three(dst, hi, lo, rh, rl_, first, last):
                    nc.tensor.matmul(dst, hi, rh, start=first, stop=False)
                    nc.tensor.matmul(dst, hi, rl_, start=False, stop=False)
                    return nc.tensor.matmul(dst, lo, rh, start=False, stop=last)

                def segment(kind, g, par, seg, half, nxt):
                    if kind != "W2":
                        for s in range(U):
                            pe.wait_ge(w_lo, UNITS * b + U * seg + s + 1 + U)
                            if kind == "O":
                                if g == 0 and s == 0:
                                    pe.wait_ge(r_done, UW * b + R0)
                                    pe.wait_ge(ml_done, KC * b + KC)
                                if g or s >= 2:
                                    pe.wait_ge(x_done, KC * b + U * g + s - 1)
                            elif isinstance(seg, int) and seg == 2 and s < 2:
                                pe.wait_ge(x_done, KC * b + KC)
                                pe.wait_ge(hl_done, KC * b + KC)
                            else:
                                pe.wait_ge(r_done, UW * b + U * g + s - 1 + R0)
                            for k in range(KC):
                                last = three(ps[:, s % 2, :], wh[:, U * half + s, k, :], wl[:, U * half + s, k, :],
                                             ah[:, k, :], al[:, k, :], k == 0, k == KC - 1)
                            last.then_inc(f_done, 1)
                        if isinstance(seg, int) and seg == 1:
                            sum_squares(True)
                    else:
                        pe.wait_ge(w_lo, UNITS * b + U * seg + U + U)
                        pe.wait_ge(tl_done, UW * b + U * g + U + 2)
                        for k in range(KC):
                            pe.wait_ge(y_add, Y_BLK * b + KC * g + k + 1)
                            for s in range(U):
                                last = three(ps[:, 2 + k % 4, :], wh[:, U * half + s, k, :], wl[:, U * half + s, k, :],
                                             th[:, par, s, :], tl[:, par, s, :], s == 0, s == U - 1)
                            last.then_inc(y_done, 1)

                segments(pe, b, segment)
                sum_squares(False)


def program(nc, S, a, projT, biasT, mixT, outT):
    norm_and_projection(nc, S, a["xT"], a["g_mix"], a["conv_w"], a["w_proj"], projT)
    topk = min(TOPK_MAX, S // 4)
    deltanet_and_selection(nc, S, topk, projT, a["a_log"], a["dt_bias"], a["g_gdn"], a, mixT, biasT)
    indexed_attention(nc, S, topk, projT, a, biasT, mixT)
    output_and_mlp(nc, S, a["xT"], mixT, a["w_units"], a["g_ffn"], a["g_final"], outT)


def shape_constants(S):
    i = np.arange(P)
    f = lambda m: np.ascontiguousarray(m.astype(np.float32))
    same = (i[:, None] // 16) == (i[None, :] // 16)
    half = HD // 2
    inv = (1.0 / (np.float32(10000.0) ** (np.arange(half, dtype=np.float32) / np.float32(half)))).astype(np.float32)
    ang = np.arange(S, dtype=np.float32)[None, :] * inv[i % half][:, None]
    sign = np.where(i % HD < half, -1.0, 1.0).astype(np.float32)[:, None]
    return {
        "ident": f(np.eye(P)), "triu": f(i[:, None] <= i[None, :]), "incl": f(i[:, None] >= i[None, :]),
        "strict": f(i[:, None] > i[None, :]), "diag16": f(same), "off16": f(~same),
        "cosT": f(np.cos(ang)), "sinT": f(np.sin(ang) * sign),
    }


def proj_columns():
    sizes = [A_HEADS * HD, KV_HEADS * HD, KV_HEADS * HD, IDX_HEADS * HD, HD, IDX_HEADS] + [B_HEADS * BD] * 4 + [B_HEADS] * 2
    off = np.concatenate([[0], np.cumsum(sizes)])
    qa, ka, va, qi, ki, wi, qb, kb, vb, zb, bb, ab = [list(range(off[n], off[n + 1])) for n in range(len(sizes))]
    small = wi + bb + ab
    return small + [-1] * (P - HD - len(small)) + ki + qi + qa + ka + va + qb + kb + vb + zb


def weight_units(w_out, w_ff1, w_ff2):
    by_output = lambda w: w.reshape(KC, P, -1, P).transpose(2, 1, 0, 3).reshape(-1, P, KC * P)
    o, w1 = by_output(w_out), by_output(w_ff1)
    w2 = w_ff2.reshape(-1, P, D_MODEL)
    n = D_FF // 512
    part = lambda w, g: w[4 * g:4 * g + 4]
    seq = [o, part(w1, 0)]
    for g in range(1, n):
        seq += [part(w1, g), part(w2, g - 1)]
    return np.ascontiguousarray(np.concatenate(seq + [part(w2, n - 1)]))


def host_layout(d):
    x = d["x"][0]
    S = x.shape[0]
    cols = np.array(proj_columns())
    w = np.zeros((D_MODEL, (N_CHUNK + 1) * P), np.float32)
    w[:, :len(cols)] = np.where(cols >= 0, d["w_in"][0][:, cols], np.float32(0))
    chunks = lambda a: np.ascontiguousarray(a.reshape(KC, P, -1, P).transpose(2, 1, 0, 3))
    col = lambda g: np.ascontiguousarray(g.reshape(-1, P).T)
    return {
        "xT": np.ascontiguousarray(x.T.reshape(KC, P, S).transpose(1, 0, 2)),
        "g_mix": col(d["norm_mix_g"][0]),
        "conv_w": np.ascontiguousarray(d["conv_w"][0].reshape(CONV, N_CONV, P).transpose(2, 1, 0)),
        "w_proj": chunks(w),
        "w_units": weight_units(d["w_out"][0], d["w_ff1"][0], d["w_ff2"][0]),
        "g_ffn": col(d["norm_ffn_g"][0]), "g_final": col(d["norm_final_g"]),
        "a_log": d["a_log"][0:1], "dt_bias": d["dt_bias"][0:1], "g_gdn": col(d["gdn_norm_g"][0]),
    }


_OUT = "out_dram"


def kernel(**inputs):
    import concourse.bacc as bacc
    from concourse.bass_utils import run_bass_kernel_spmd

    d = {k: np.asarray(v) for k, v in inputs.items()}
    S = d["x"].shape[1]
    arrays = {**host_layout(d), **shape_constants(S)}
    arrays = {k: np.ascontiguousarray(v) for k, v in arrays.items()}
    nc = bacc.Bacc("TRN2", target_bir_lowering=False, num_devices=1)
    a = {n: nc.dram_tensor(n, v.shape, fp32, kind="ExternalInput").ap() for n, v in arrays.items()}
    projT = nc.dram_tensor("projT", (N_CHUNK, P, S), fp32, kind="Internal").ap()
    biasT = nc.dram_tensor("biasT", (S // P, P, S), fp32, kind="Internal").ap()
    mixT = nc.dram_tensor("mixT", (KC, P, S), fp32, kind="Internal").ap()
    outT = nc.dram_tensor(_OUT, (KC, P, S), fp32, kind="ExternalOutput").ap()
    program(nc, S, a, projT, biasT, mixT, outT)
    r = run_bass_kernel_spmd(nc, [arrays], core_ids=[0])
    out = r.results[0][_OUT].reshape(D_MODEL, S)
    return np.ascontiguousarray(out.T)[None]
```
